# Optimizing a Trainium2 kernel written in Bass

```python
import jax, jax.numpy as jnp
from jax import lax
import numpy as np
import math

D_MODEL = 1024
BATCH = 1
SEQ = 256
DEPTH = 2

A_HEADS = 4
A_KEY_DIM = 128
A_VAL_DIM = 128
A_KEY_WIDTH = A_HEADS * A_KEY_DIM
A_WIDTH = A_HEADS * A_VAL_DIM
HGRN_CHUNK = 64
B_WIDTH = D_MODEL - A_WIDTH
B_BLOCKS = 8
B_BLOCK_DIM = B_WIDTH // B_BLOCKS
B_CONV = 4
RG_C = 8.0
C_HEADS = 16
C_HEAD_DIM = D_MODEL // C_HEADS
Q_BLOCK = 128
D_FF = 2816
FFN_CONV = 3
EPS = 1e-6

N_EVEN = (DEPTH + 1) // 2
N_ODD = DEPTH // 2
EVEN_SIZES = (A_KEY_WIDTH, A_KEY_WIDTH, A_WIDTH, A_WIDTH, B_WIDTH, B_WIDTH)
EVEN_IN = sum(EVEN_SIZES)
ODD_SIZES = (D_MODEL, D_MODEL, D_MODEL, C_HEADS)
ODD_IN = sum(ODD_SIZES)


def rms_norm(x, gain):
    xf = x.astype(jnp.float32)
    y = xf * lax.rsqrt(jnp.mean(xf * xf, axis=-1, keepdims=True) + EPS)
    return (y * gain.astype(jnp.float32)).astype(x.dtype)

def split_cols(t, sizes):
    return jnp.split(t, list(np.cumsum(sizes)[:-1]), axis=-1)

def causal_dwconv(x, w, b):
    K, C = w.shape
    y = lax.conv_general_dilated(x, w[:, None, :].astype(x.dtype), window_strides=(1,),
                                 padding=[(K - 1, 0)], dimension_numbers=('NWC', 'WIO', 'NWC'),
                                 feature_group_count=C)
    return y + b.astype(x.dtype)

def hgrn2_mix(q, f_logit, v, g, lb, norm_gain):
    Bsz, T, _ = q.shape
    N = T // HGRN_CHUNK

    def heads(t, d):
        return t.reshape(Bsz, N, HGRN_CHUNK, A_HEADS, d).transpose(0, 3, 1, 2, 4)

    forget = lb + (1.0 - lb) * jax.nn.sigmoid(f_logit.astype(jnp.float32))
    qh = heads(jax.nn.silu(q.astype(jnp.float32)), A_KEY_DIM)
    kh = heads(1.0 - forget, A_KEY_DIM)
    bcum = jnp.cumsum(heads(jnp.log(forget), A_KEY_DIM), axis=3)
    vh = heads(v.astype(jnp.float32), A_VAL_DIM)
    b_last = bcum[:, :, :, -1:]
    q_dec = qh * jnp.exp(bcum)
    scores = jnp.einsum('bhnck,bhnsk->bhncs', q_dec, kh * jnp.exp(-bcum))
    causal = jnp.tril(jnp.ones((HGRN_CHUNK, HGRN_CHUNK), dtype=bool))
    scores = jnp.where(causal, scores, 0.0)
    o_intra = jnp.einsum('bhncs,bhnsv->bhncv', scores, vh)
    chunk_upd = jnp.einsum('bhnck,bhncv->bhnkv', kh * jnp.exp(b_last - bcum), vh)
    chunk_dec = jnp.exp(b_last[:, :, :, 0])

    def step(S, inp):
        dec, upd = inp
        return dec[..., None] * S + upd, S

    S0 = jnp.zeros((Bsz, A_HEADS, A_KEY_DIM, A_VAL_DIM), jnp.float32)
    _, S_prev = lax.scan(step, S0, (jnp.moveaxis(chunk_dec, 2, 0), jnp.moveaxis(chunk_upd, 2, 0)))
    S_prev = jnp.moveaxis(S_prev, 0, 2)
    o = o_intra + jnp.einsum('bhnck,bhnkv->bhncv', q_dec, S_prev)
    o = o.transpose(0, 2, 3, 1, 4).reshape(Bsz, T, A_HEADS, A_VAL_DIM)
    o = o * lax.rsqrt(jnp.mean(o * o, axis=-1, keepdims=True) + EPS)
    o = o * norm_gain.astype(jnp.float32).reshape(A_HEADS, A_VAL_DIM)
    return o.reshape(Bsz, T, A_WIDTH) * jax.nn.sigmoid(g.astype(jnp.float32))

def block_diag(x, w, b):
    xb = x.reshape(x.shape[0], x.shape[1], B_BLOCKS, B_BLOCK_DIM)
    return jnp.einsum('btni,nij->btnj', xb, w.astype(jnp.float32)).reshape(x.shape) + b.astype(jnp.float32)

def rglru_mix(x_br, y_br, conv_w, conv_b, wa, ba, wx, bx, lam):
    xf = causal_dwconv(x_br, conv_w, conv_b).astype(jnp.float32)
    r = jax.nn.sigmoid(block_diag(xf, wa, ba))
    i = jax.nn.sigmoid(block_diag(xf, wx, bx))
    log_a = -RG_C * r * jax.nn.softplus(-lam.astype(jnp.float32))
    a = jnp.exp(log_a)
    u = jnp.sqrt(-jnp.expm1(2.0 * log_a)) * (i * xf)

    def combine(left, right):
        a1, b1 = left
        a2, b2 = right
        return a1 * a2, a2 * b1 + b2

    _, h = lax.associative_scan(combine, (a, u), axis=1)
    return h * jax.nn.gelu(y_br.astype(jnp.float32))

def fox_attention(q, k, v, f_logit):
    Bsz, T, _ = q.shape

    def heads(t):
        return t.astype(jnp.float32).reshape(Bsz, T, C_HEADS, C_HEAD_DIM).transpose(0, 2, 1, 3)

    qh = heads(q) * (C_HEAD_DIM ** -0.5)
    kh, vh = heads(k), heads(v)
    c = jnp.cumsum(jax.nn.log_sigmoid(f_logit.astype(jnp.float32)), axis=1).transpose(0, 2, 1)
    outs = []
    for blk in range(T // Q_BLOCK):
        s0 = blk * Q_BLOCK
        end = s0 + Q_BLOCK
        logits = jnp.einsum('bhqd,bhkd->bhqk', qh[:, :, s0:end], kh[:, :, :end])
        logits = logits + c[:, :, s0:end, None] - c[:, :, None, :end]
        mask = (s0 + jnp.arange(Q_BLOCK))[:, None] >= jnp.arange(end)[None, :]
        p = jax.nn.softmax(jnp.where(mask, logits, -jnp.inf), axis=-1)
        outs.append(jnp.einsum('bhqk,bhkd->bhqd', p, vh[:, :, :end]))
    o = jnp.concatenate(outs, axis=2)
    return o.transpose(0, 2, 1, 3).reshape(Bsz, T, D_MODEL)

def conv_ffn(x, w_up, conv_w, conv_b, w_down):
    hid = causal_dwconv(x @ w_up, conv_w, conv_b)
    gate, val = jnp.split(hid, 2, axis=-1)
    return (jax.nn.gelu(gate) * val) @ w_down

def first_inputs(seed: int = 0) -> dict:
    key = jax.random.key(seed)
    ks = jax.random.split(key, 20)
    f32 = jnp.float32
    nrm = jax.random.normal
    a0 = jax.random.uniform(ks[11], (N_EVEN, B_WIDTH), f32, 0.9 ** (1.0 / RG_C), 0.999 ** (1.0 / RG_C))
    return {
        'x': nrm(ks[0], (BATCH, SEQ, D_MODEL), f32),
        'norm_gains': 1.0 + 0.1 * nrm(ks[1], (DEPTH, 4, D_MODEL), f32),
        'even_w_in': nrm(ks[2], (N_EVEN, D_MODEL, EVEN_IN), f32) * D_MODEL ** -0.5,
        'hgrn_lb_logits': 0.1 * nrm(ks[3], (DEPTH + 1, A_KEY_WIDTH), f32),
        'hgrn_norm': 1.0 + 0.1 * nrm(ks[4], (N_EVEN, A_WIDTH), f32),
        'rg_conv_w': nrm(ks[5], (N_EVEN, B_CONV, B_WIDTH), f32) * B_CONV ** -0.5,
        'rg_conv_b': 0.01 * nrm(ks[6], (N_EVEN, B_WIDTH), f32),
        'rg_wa': nrm(ks[7], (N_EVEN, B_BLOCKS, B_BLOCK_DIM, B_BLOCK_DIM), f32) * B_BLOCK_DIM ** -0.5,
        'rg_ba': 0.01 * nrm(ks[8], (N_EVEN, B_WIDTH), f32),
        'rg_wx': nrm(ks[9], (N_EVEN, B_BLOCKS, B_BLOCK_DIM, B_BLOCK_DIM), f32) * B_BLOCK_DIM ** -0.5,
        'rg_bx': 0.01 * nrm(ks[10], (N_EVEN, B_WIDTH), f32),
        'rg_lambda': jnp.log(a0) - jnp.log1p(-a0),
        'even_w_out': nrm(ks[12], (N_EVEN, A_WIDTH + B_WIDTH, D_MODEL), f32) * (A_WIDTH + B_WIDTH) ** -0.5,
        'odd_w_in': nrm(ks[13], (N_ODD, D_MODEL, ODD_IN), f32) * D_MODEL ** -0.5,
        'fox_f_bias': jax.random.uniform(ks[14], (N_ODD, C_HEADS), f32, 1.0, 5.0),
        'odd_w_out': nrm(ks[15], (N_ODD, D_MODEL, D_MODEL), f32) * D_MODEL ** -0.5,
        'ffn_w_up': nrm(ks[16], (DEPTH, D_MODEL, 2 * D_FF), f32) * D_MODEL ** -0.5,
        'ffn_conv_w': nrm(ks[17], (DEPTH, FFN_CONV, 2 * D_FF), f32) * FFN_CONV ** -0.5,
        'ffn_conv_b': 0.01 * nrm(ks[18], (DEPTH, 2 * D_FF), f32),
        'ffn_w_down': nrm(ks[19], (DEPTH, D_FF, D_MODEL), f32) * D_FF ** -0.5,
    }

def first_block(x, norm_gains, even_w_in, hgrn_lb_logits, hgrn_norm, rg_conv_w, rg_conv_b, rg_wa, rg_ba,
              rg_wx, rg_bx, rg_lambda, even_w_out, odd_w_in, fox_f_bias, odd_w_out,
              ffn_w_up, ffn_conv_w, ffn_conv_b, ffn_w_down):
    lb_all = jnp.cumsum(jax.nn.softmax(hgrn_lb_logits.astype(jnp.float32), axis=0), axis=0)
    for l in range(DEPTH):
        g = norm_gains[l]
        h = rms_norm(x, g[0])
        if l % 2 == 0:
            e = l // 2
            qa, fa, ia, ga, xb, yb = split_cols(h @ even_w_in[e], EVEN_SIZES)
            oa = hgrn2_mix(qa, fa, ia, ga, lb_all[l], hgrn_norm[e])
            ob = rglru_mix(xb, yb, rg_conv_w[e], rg_conv_b[e], rg_wa[e], rg_ba[e], rg_wx[e], rg_bx[e], rg_lambda[e])
            mix = jnp.concatenate([oa, ob], axis=-1).astype(h.dtype) @ even_w_out[e]
        else:
            o = l // 2
            qc, kc, vc, fc = split_cols(h @ odd_w_in[o], ODD_SIZES)
            mix = fox_attention(qc, kc, vc, fc + fox_f_bias[o]).astype(h.dtype) @ odd_w_out[o]
        x = x + rms_norm(mix, g[1])
        h = rms_norm(x, g[2])
        x = x + rms_norm(conv_ffn(h, ffn_w_up[l], ffn_conv_w[l], ffn_conv_b[l], ffn_w_down[l]), g[3])
    return x


N_MIXERS = 2
N_EVEN_2 = (DEPTH + 1) // 2
N_ODD_2 = DEPTH // 2

MLA_HEADS = 16
QK_NOPE = 64
QK_ROPE = 32
V_DIM = 64
Q_LORA = 384
KV_LORA = 256
MLA_IN = Q_LORA + KV_LORA + QK_ROPE
ROPE_THETA = 10000.0
NEG_INF = -1e30

S5_GROUP = 16
S5_GROUPS = D_MODEL // S5_GROUP
S5_STATE = 64
DT_MIN = 0.001
DT_MAX = 0.1

N_EXPERTS = 8
TOP_K = 2
D_FF_EXPERT = 3584


def rmsnorm(x, g):
    xf = x.astype(jnp.float32)
    y = xf * lax.rsqrt(jnp.mean(xf * xf, axis=-1, keepdims=True) + EPS)
    return (y * g.astype(jnp.float32)).astype(x.dtype)

def rope(x, cos, sin):
    x1, x2 = jnp.split(x, 2, axis=-1)
    return jnp.concatenate([x1 * cos - x2 * sin, x2 * cos + x1 * sin], axis=-1).astype(x.dtype)

def mla_mixer(h, positions, w_in, q_norm, w_uq, kv_norm, w_ukv, w_o):
    B, S, _ = h.shape
    f32 = jnp.float32
    proj = h @ w_in
    c_q = rmsnorm(proj[..., :Q_LORA], q_norm)
    c_kv = rmsnorm(proj[..., Q_LORA:Q_LORA + KV_LORA], kv_norm)
    k_pe = proj[..., Q_LORA + KV_LORA:]
    q = (c_q @ w_uq).reshape(B, S, MLA_HEADS, QK_NOPE + QK_ROPE)
    q_nope, q_pe = q[..., :QK_NOPE], q[..., QK_NOPE:]
    inv_freq = ROPE_THETA ** (-jnp.arange(0, QK_ROPE, 2, dtype=f32) / QK_ROPE)
    ang = positions.astype(f32)[..., None] * inv_freq
    cos, sin = jnp.cos(ang), jnp.sin(ang)
    q_pe = rope(q_pe, cos[:, :, None, :], sin[:, :, None, :])
    k_pe = rope(k_pe, cos, sin)
    kv = (c_kv @ w_ukv).reshape(B, S, MLA_HEADS, QK_NOPE + V_DIM)
    k_nope, v = kv[..., :QK_NOPE], kv[..., QK_NOPE:]
    scale = 1.0 / math.sqrt(QK_NOPE + QK_ROPE)
    n_blocks = S // Q_BLOCK

    def to_blocks(t):
        return t.reshape(B, n_blocks, Q_BLOCK, *t.shape[2:]).swapaxes(0, 1)

    k_idx = jnp.arange(S, dtype=jnp.int32)

    def attend_block(args):
        qn, qp, start = args
        s = (jnp.einsum('bqhd,bkhd->bhqk', qn, k_nope, preferred_element_type=f32)
             + jnp.einsum('bqhr,bkr->bhqk', qp, k_pe, preferred_element_type=f32))
        q_idx = start + jnp.arange(Q_BLOCK, dtype=jnp.int32)
        causal = k_idx[None, :] <= q_idx[:, None]
        s = jnp.where(causal, s * scale, NEG_INF)
        p = jax.nn.softmax(s, axis=-1).astype(v.dtype)
        return jnp.einsum('bhqk,bkhd->bqhd', p, v)

    starts = jnp.arange(n_blocks, dtype=jnp.int32) * Q_BLOCK
    o = lax.map(attend_block, (to_blocks(q_nope), to_blocks(q_pe), starts))
    o = o.swapaxes(0, 1).reshape(B, S, MLA_HEADS * V_DIM)
    return o @ w_o

def _complex_affine_combine(left, right):
    a1r, a1i, b1r, b1i = left
    a2r, a2i, b2r, b2i = right
    ar = a2r * a1r - a2i * a1i
    ai = a2r * a1i + a2i * a1r
    br = a2r * b1r - a2i * b1i + b2r
    bi = a2r * b1i + a2i * b1r + b2i
    return (ar, ai, br, bi)

def s5_mixer(h, w_in, lam_re, lam_im, log_dt, b_re, b_im, c_re, c_im, d_skip, w_glu):
    B, S, D = h.shape
    f32 = jnp.float32
    u = (h @ w_in).astype(f32).reshape(B, S, S5_GROUPS, S5_GROUP)
    lr, li = lam_re.astype(f32), lam_im.astype(f32)
    dt = jnp.exp(log_dt.astype(f32))[:, None]
    mag = jnp.exp(lr * dt)
    ar = mag * jnp.cos(li * dt)
    ai = mag * jnp.sin(li * dt)
    den = lr * lr + li * li
    gr = ((ar - 1.0) * lr + ai * li) / den
    gi = (ai * lr - (ar - 1.0) * li) / den
    br, bi = b_re.astype(f32), b_im.astype(f32)
    bbr = gr[..., None] * br - gi[..., None] * bi
    bbi = gr[..., None] * bi + gi[..., None] * br
    bu_r = jnp.einsum('bsgh,gph->sbgp', u, bbr)
    bu_i = jnp.einsum('bsgh,gph->sbgp', u, bbi)
    a_r = jnp.broadcast_to(ar[None, None], (S, 1, S5_GROUPS, S5_STATE))
    a_i = jnp.broadcast_to(ai[None, None], (S, 1, S5_GROUPS, S5_STATE))
    _, _, xr, xi = lax.associative_scan(_complex_affine_combine, (a_r, a_i, bu_r, bu_i), axis=0)
    y = (jnp.einsum('sbgp,ghp->bsgh', xr, c_re.astype(f32))
         - jnp.einsum('sbgp,ghp->bsgh', xi, c_im.astype(f32))
         + d_skip.astype(f32) * u)
    y = jax.nn.gelu(y.reshape(B, S, D)).astype(h.dtype)
    z = y @ w_glu
    return z[..., :D] * jax.nn.sigmoid(z[..., D:])

def swiglu(h, w_gate, w_up, w_down):
    return (jax.nn.silu(h @ w_gate) * (h @ w_up)) @ w_down

def moe_swiglu(h, w_router, w_gate, w_up, w_down):
    B, S, D = h.shape
    t = h.reshape(B * S, D)
    logits = (t @ w_router).astype(jnp.float32)
    top_vals, top_idx = lax.top_k(logits, TOP_K)
    gates = jax.nn.softmax(top_vals, axis=-1)
    combine = jnp.sum(jax.nn.one_hot(top_idx, N_EXPERTS, dtype=jnp.float32) * gates[..., None], axis=1)
    out = jnp.zeros_like(t)
    for e in range(N_EXPERTS):
        he = swiglu(t, w_gate[e], w_up[e], w_down[e])
        out = out + combine[:, e:e + 1].astype(t.dtype) * he
    return out.reshape(B, S, D)

def second_inputs(seed: int = 0) -> dict:
    key = jax.random.key(seed)
    ks = iter(jax.random.split(key, 40))
    f32 = jnp.float32

    def nrm(shape, scale):
        return jax.random.normal(next(ks), shape, f32) * scale

    D = D_MODEL
    x = jax.random.normal(next(ks), (BATCH, SEQ, D), f32)
    offset = jax.random.randint(next(ks), (BATCH, 1), 0, 1024, dtype=jnp.int32)
    positions = offset + jnp.arange(SEQ, dtype=jnp.int32)[None, :]
    mix_norm = 1.0 + nrm((DEPTH, D), 0.05)
    ffn_norm = 1.0 + nrm((DEPTH, D), 0.05)
    final_norm = 1.0 + nrm((D,), 0.05)
    mla_w_in = nrm((N_EVEN_2, D, MLA_IN), D ** -0.5)
    mla_q_norm = 1.0 + nrm((N_EVEN_2, Q_LORA), 0.05)
    mla_w_uq = nrm((N_EVEN_2, Q_LORA, MLA_HEADS * (QK_NOPE + QK_ROPE)), Q_LORA ** -0.5)
    mla_kv_norm = 1.0 + nrm((N_EVEN_2, KV_LORA), 0.05)
    mla_w_ukv = nrm((N_EVEN_2, KV_LORA, MLA_HEADS * (QK_NOPE + V_DIM)), KV_LORA ** -0.5)
    mla_w_o = nrm((N_EVEN_2, MLA_HEADS * V_DIM, D), (MLA_HEADS * V_DIM) ** -0.5)
    ffn_w_gate = nrm((N_EVEN_2, D, D_FF), D ** -0.5)
    ffn_w_up = nrm((N_EVEN_2, D, D_FF), D ** -0.5)
    ffn_w_down = nrm((N_EVEN_2, D_FF, D), D_FF ** -0.5)
    s5_w_in = nrm((N_ODD_2, D, D), D ** -0.5)
    s5_lambda_re = -0.5 + nrm((N_ODD_2, S5_GROUPS, S5_STATE), 0.01)
    s5_lambda_im = math.pi * jnp.arange(S5_STATE, dtype=f32)[None, None, :] + nrm((N_ODD_2, S5_GROUPS, S5_STATE), 0.01)
    s5_log_dt = jax.random.uniform(next(ks), (N_ODD_2, S5_GROUPS), f32, math.log(DT_MIN), math.log(DT_MAX))
    s5_b_re = nrm((N_ODD_2, S5_GROUPS, S5_STATE, S5_GROUP), (2 * S5_GROUP) ** -0.5)
    s5_b_im = nrm((N_ODD_2, S5_GROUPS, S5_STATE, S5_GROUP), (2 * S5_GROUP) ** -0.5)
    s5_c_re = nrm((N_ODD_2, S5_GROUPS, S5_GROUP, S5_STATE), (2 * S5_STATE) ** -0.5)
    s5_c_im = nrm((N_ODD_2, S5_GROUPS, S5_GROUP, S5_STATE), (2 * S5_STATE) ** -0.5)
    s5_d = nrm((N_ODD_2, S5_GROUPS, S5_GROUP), 1.0)
    s5_w_glu = nrm((N_ODD_2, D, 2 * D), D ** -0.5)
    moe_w_router = nrm((N_ODD_2, D, N_EXPERTS), D ** -0.5)
    moe_w_gate = nrm((N_ODD_2, N_EXPERTS, D, D_FF_EXPERT), D ** -0.5)
    moe_w_up = nrm((N_ODD_2, N_EXPERTS, D, D_FF_EXPERT), D ** -0.5)
    moe_w_down = nrm((N_ODD_2, N_EXPERTS, D_FF_EXPERT, D), D_FF_EXPERT ** -0.5)
    return {
        "x": x, "positions": positions,
        "mix_norm": mix_norm, "ffn_norm": ffn_norm, "final_norm": final_norm,
        "mla_w_in": mla_w_in, "mla_q_norm": mla_q_norm, "mla_w_uq": mla_w_uq,
        "mla_kv_norm": mla_kv_norm, "mla_w_ukv": mla_w_ukv, "mla_w_o": mla_w_o,
        "ffn_w_gate": ffn_w_gate, "ffn_w_up": ffn_w_up, "ffn_w_down": ffn_w_down,
        "s5_w_in": s5_w_in, "s5_lambda_re": s5_lambda_re, "s5_lambda_im": s5_lambda_im,
        "s5_log_dt": s5_log_dt, "s5_b_re": s5_b_re, "s5_b_im": s5_b_im,
        "s5_c_re": s5_c_re, "s5_c_im": s5_c_im, "s5_d": s5_d, "s5_w_glu": s5_w_glu,
        "moe_w_router": moe_w_router, "moe_w_gate": moe_w_gate,
        "moe_w_up": moe_w_up, "moe_w_down": moe_w_down,
    }

def second_block(x, positions, mix_norm, ffn_norm, final_norm,
              mla_w_in, mla_q_norm, mla_w_uq, mla_kv_norm, mla_w_ukv, mla_w_o,
              ffn_w_gate, ffn_w_up, ffn_w_down,
              s5_w_in, s5_lambda_re, s5_lambda_im, s5_log_dt, s5_b_re, s5_b_im,
              s5_c_re, s5_c_im, s5_d, s5_w_glu,
              moe_w_router, moe_w_gate, moe_w_up, moe_w_down):
    h = x
    for i in range(DEPTH):
        j = i // N_MIXERS
        hn = rmsnorm(h, mix_norm[i])
        if i % N_MIXERS == 0:
            h = h + mla_mixer(hn, positions, mla_w_in[j], mla_q_norm[j], mla_w_uq[j],
                              mla_kv_norm[j], mla_w_ukv[j], mla_w_o[j])
        else:
            h = h + s5_mixer(hn, s5_w_in[j], s5_lambda_re[j], s5_lambda_im[j], s5_log_dt[j],
                             s5_b_re[j], s5_b_im[j], s5_c_re[j], s5_c_im[j], s5_d[j], s5_w_glu[j])
        hn = rmsnorm(h, ffn_norm[i])
        if i % 2 == 0:
            h = h + swiglu(hn, ffn_w_gate[j], ffn_w_up[j], ffn_w_down[j])
        else:
            h = h + moe_swiglu(hn, moe_w_router[j], moe_w_gate[j], moe_w_up[j], moe_w_down[j])
    return rmsnorm(h, final_norm)


def setup_inputs(seed=0):
    out = dict(first_inputs(seed))
    for name, value in second_inputs(seed + 1).items():
        if name != "x":
            out[name + "_2"] = value
    return out


def reference(
    x, norm_gains, even_w_in, hgrn_lb_logits, hgrn_norm, rg_conv_w, rg_conv_b, rg_wa, rg_ba,
    rg_wx, rg_bx, rg_lambda, even_w_out, odd_w_in, fox_f_bias, odd_w_out, ffn_w_up, ffn_conv_w,
    ffn_conv_b, ffn_w_down, positions_2, mix_norm_2, ffn_norm_2, final_norm_2, mla_w_in_2,
    mla_q_norm_2, mla_w_uq_2, mla_kv_norm_2, mla_w_ukv_2, mla_w_o_2, ffn_w_gate_2, ffn_w_up_2,
    ffn_w_down_2, s5_w_in_2, s5_lambda_re_2, s5_lambda_im_2, s5_log_dt_2, s5_b_re_2, s5_b_im_2,
    s5_c_re_2, s5_c_im_2, s5_d_2, s5_w_glu_2, moe_w_router_2, moe_w_gate_2, moe_w_up_2,
    moe_w_down_2,
):
    x = first_block(
        x, norm_gains, even_w_in, hgrn_lb_logits, hgrn_norm, rg_conv_w, rg_conv_b, rg_wa, rg_ba,
        rg_wx, rg_bx, rg_lambda, even_w_out, odd_w_in, fox_f_bias, odd_w_out, ffn_w_up,
        ffn_conv_w, ffn_conv_b, ffn_w_down,
    )
    return second_block(
        x, positions_2, mix_norm_2, ffn_norm_2, final_norm_2, mla_w_in_2, mla_q_norm_2,
        mla_w_uq_2, mla_kv_norm_2, mla_w_ukv_2, mla_w_o_2, ffn_w_gate_2, ffn_w_up_2,
        ffn_w_down_2, s5_w_in_2, s5_lambda_re_2, s5_lambda_im_2, s5_log_dt_2, s5_b_re_2,
        s5_b_im_2, s5_c_re_2, s5_c_im_2, s5_d_2, s5_w_glu_2, moe_w_router_2, moe_w_gate_2,
        moe_w_up_2, moe_w_down_2,
    )


_drawn_inputs = setup_inputs


def setup_inputs(seed=0):
    import zlib

    import numpy as np

    out = dict(_drawn_inputs(seed))
    spreads = {}
    factors = {'hgrn_lb_logits': 4.924,
     'rg_ba': 8.0,
     'rg_bx': 8.0,
     'ffn_conv_b': 3.364,
     'mix_norm_2': 2.893,
     'mla_q_norm_2': 8.0,
     'mla_kv_norm_2': 5.224,
     's5_lambda_re_2': 64.0,
     's5_lambda_im_2': 26.824,
     's5_log_dt_2': 39.2,
     's5_b_re_2': 59.384,
     's5_b_im_2': 50.248,
     's5_c_re_2': 29.936,
     's5_c_im_2': 51.24,
     'ffn_norm_2': 3.825}
    for name, (base, spread) in spreads.items():
        noise = np.random.default_rng([zlib.crc32(name.encode()), seed]).standard_normal(out[name].shape)
        drawn = base * np.exp(spread * noise) if base else spread * noise
        out[name] = __import__('jax').numpy.asarray(drawn.astype(out[name].dtype))
    for name, factor in factors.items():
        out[name] = (out[name] * factor).astype(out[name].dtype)
    return out
```

```python
from contextlib import ExitStack

import numpy as np

import concourse.bass as bass
from concourse import mybir

P = 128
T = 256
D = 1024
KD = D // P
HEADS = 16
HD = D // HEADS
ROPE = 32
EPS = 1e-6
NEG = -1e30

A_HEADS = 4
CHUNK = 64
NCHUNK = T // CHUNK
RG_C = 8.0
RG_TILES = 4
RG_TAPS = 4
FF = 2816
FF_TILES = FF // P
FF_TAPS = 3
EXPERTS = 8
FE = 3584
FE_TILES = FE // P
Q_LORA, KV_LORA = 384, 256
S5_TILES = 32

SLOTS = 4
SLOT = 6144
UNIT_TILES = 6
WORK = 4
HALF = SLOT // 2
HALVES = 7
CAP = 96
FT_UNIT = 2

F32 = mybir.dt.float32
ALU = mybir.AluOpType
ACT = mybir.ActivationFunctionType
AX = mybir.AxisListType

TURN_A = 6.28125
TURN_B = float(np.float32(np.floor((2 * np.pi - TURN_A) * 2.0**21) / 2.0**21))
TURN_C = float(np.float32(2 * np.pi - TURN_A - TURN_B))
INV_TURN = float(np.float32(1 / (2 * np.pi)))
ROUND = 12582912.0
PI_SAFE = 3.1415925
TWO_PI_SAFE = 6.283185

LINEAR = {
    "even_in": (24, 8), "even_out": (8, 8), "odd_qk": (16, 8), "odd_out": (8, 8),
    "mla_in": (6, 8), "mla_uq": (12, 3), "mla_uk": (8, 2), "mla_o": (8, 8),
    "s5_in": (8, 8), "s5_glu": (16, 8),
}
LINEAR_ORDER = list(LINEAR)


def phase_units(name):
    if name in LINEAR:
        tiles, k = LINEAR[name]
        per = UNIT_TILES if k == KD else tiles
        return [min(per, tiles - t) * k * P for t in range(0, tiles, per)]
    if name == "odd_v":
        return [KD * 512] * 2
    if name == "mla_uv":
        return [2 * D]
    return [SLOT] * (FF_TILES // FT_UNIT)


STREAM = ["even_in", "even_out", "ffn0", "odd_qk", "odd_v", "odd_out", "ffn1", "mla_in", "mla_uq",
          "mla_uk", "mla_uv", "mla_o", "ffn2", "s5_in", "s5_glu"]
UNIT0, LOADED, _n = {}, [], [0] * SLOTS
for _name in STREAM:
    UNIT0[_name] = len(LOADED)
    for _ in phase_units(_name):
        _s = len(LOADED) % SLOTS
        _n[_s] += 16
        LOADED.append(_n[_s])
TILE0, _t = {}, 0
for _name in LINEAR_ORDER:
    TILE0[_name] = _t
    _t += LINEAR[_name][0]
FFN = {"ffn0": FF_TILES, "ffn1": FF_TILES, "ffn2": FF_TILES, "moe": EXPERTS * FE_TILES}
FT0, _t = {}, 0
for _name, _c in FFN.items():
    FT0[_name] = _t
    _t += _c

NORMS = [("n0", 8), ("n1", 8), ("n2", 8), ("n3", 8), ("n4", 8), ("n5", 8), ("n6", 8), ("n7", 8),
         ("m0", 8), ("mq", 3), ("mkv", 2), ("m1", 8), ("m2", 8), ("m3", 8), ("mf", 8)]
NORM_NO = {n: i for i, (n, _) in enumerate(NORMS)}
SQ0, _t = {}, 0
for _name, _c in NORMS:
    SQ0[_name] = _t
    _t += _c
X_VERSION = {"n0": 1, "n2": 2, "n4": 3, "n6": 4, "m0": 5, "m1": 6, "m2": 7, "m3": 8, "mf": 9}

VEC = {}
_t = 0
for _name, _c in [("norm_gains", 64), ("lb_logits", 12), ("hgrn_norm", 4), ("rg_conv_w", 16),
                  ("rg_conv_b", 4), ("rg_ba", 4), ("rg_bx", 4), ("rg_lambda", 4),
                  ("ffn_conv_w", 2 * 3 * 2 * FF_TILES), ("ffn_conv_b", 2 * 2 * FF_TILES),
                  ("mix_norm", 16), ("ffn_norm", 16), ("final_norm", 8), ("q_norm", 3),
                  ("kv_norm", 2), ("s5_d", 8), ("lam_re", 32), ("lam_im", 32), ("log_dt", 32),
                  ("inv_freq", 1), ("fox_bias", 1)]:
    VEC[_name] = _t
    _t += _c
N_VEC = _t

CST = {}
_t = 0
for _name, _c in [("ident", P), ("mask", P), ("rot", P), ("chunk", T), ("time", T), ("iota8", 8), ("before", P), ("part", 1)]:
    CST[_name] = _t
    _t += _c
N_CST = _t


class Order:

    def __init__(self, eng, sem):
        self.eng, self.sem, self.n = eng, sem, 0

    def mark(self, instruction):
        instruction.then_inc(self.sem, 1)
        self.n += 1
        return self.n

    def wait(self, n=None):
        self.eng.wait_ge(self.sem, self.n if n is None else n)


def build_program(nc, a):
    ctx = ExitStack()
    with ctx:
        def sb(name, shape, dt=F32):
            return ctx.enter_context(nc.sbuf_tensor(name, shape, dt))

        def sem(name):
            return ctx.enter_context(nc.semaphore(name))

        slots = [sb(f"slot{i}", [P, SLOT]) for i in range(SLOTS)]
        xT = sb("xT", [P, KD, T])
        hT = sb("hT", [P, KD, T])
        sq = sb("sq", [P, KD, T])
        yT = sb("yT", [P, KD, T])
        mixT = sb("mixT", [P, KD, T])
        proj = sb("proj", [P, 20, T])
        vtok = sb("vtok", [P, 2, D])
        scr = sb("scr", [P, 38 * T])
        xbp = sb("xbp", [P, RG_TILES, T + 3])
        rgw = sb("rgw", [P, 2, RG_TILES, P])
        vec = sb("vec", [P, N_VEC])
        cst = sb("cst", [P, N_CST])
        wf = sb("wf", [P, KD, HEADS])
        wr = sb("wr", [P, KD, EXPERTS])
        ones = sb("ones", [P, P])
        rms = sb("rms", [P, T])
        rstd = sb("rstd", [P, T])
        stat = sb("stat", [P, 4, 2 * HEADS])
        tiny = sb("tiny", [P, 24, 8])
        idx = sb("idx", [P, 2, 8], mybir.dt.uint32)
        crowded = sb("crowded", [P, 1], mybir.dt.int32)
        pos_i = sb("pos_i", [1, T], mybir.dt.int32)

        ident = cst[:, CST["ident"]:CST["ident"] + P]
        mask = cst[:, CST["mask"]:CST["mask"] + P]
        rot = cst[:, CST["rot"]:CST["rot"] + P]
        chunk_mask = cst[:, CST["chunk"]:CST["chunk"] + T]
        time_row = cst[:, CST["time"]:CST["time"] + T]
        before = cst[:, CST["before"]:CST["before"] + P]
        partition = cst[:, CST["part"]:CST["part"] + 1]
        iota8 = cst[:, CST["iota8"]:CST["iota8"] + 8]

        def v(name, i, n=1):
            return vec[:, VEC[name] + i:VEC[name] + i + n]

        def part(start, tiles=1):
            return scr[:, start * T:(start + tiles) * T]

        ps = ctx.enter_context(nc.psum_tensor("ps", [P, 8, 512], F32))

        def acc(i):
            return ps[:, i // 2, (i % 2) * T:(i % 2) * T + T]

        def work(i):
            return ps[:, 4 + i % WORK, 0:T]

        def pair(f, k):
            return ps[:, 4 + f % 2 * 2 + k, 0:T]

        small_loaded = sem("small_loaded")
        x_loaded = sem("x_loaded")
        s5_loaded = sem("s5_loaded")
        slot_loaded = [sem(f"slot_loaded{i}") for i in range(SLOTS)]
        slot_free = sem("slot_free")
        cleared = sem("cleared")
        x_turned = sem("x_turned")
        x_ready = sem("x_ready")
        h_ready = sem("h_ready")
        sq_ready = sem("sq_ready")
        sum_ready = sem("sum_ready")
        rms_ready = sem("rms_ready")
        rstd_ready = sem("rstd_ready")
        tile_ready = sem("tile_ready")
        tile_taken = sem("tile_taken")
        up_ready = sem("up_ready")
        gate_init = sem("gate_init")
        gate_conv = sem("gate_conv")
        gate_act = sem("gate_act")
        val_init = sem("val_init")
        conv_step = sem("conv_step")
        hid_ready = sem("hid_ready")
        acc_ready = sem("acc_ready")
        acc_taken = sem("acc_taken")
        mix_ready = sem("mix_ready")
        act_own, dve_own = sem("act_own"), sem("dve_own")
        hg = {n: sem("hg_" + n) for n in (
            "forget", "logf", "bcum", "decay", "exps", "gated", "vturned", "vtaken", "scores",
            "scopied", "masked", "kturned", "ktaken", "upd", "state", "out", "outtaken", "total",
            "root", "lbdiff", "lbexp")}
        rg = {n: sem("rg_" + n) for n in (
            "softplus", "rate", "conv", "product", "gates", "decay", "square", "root")}
        at = {n: sem("at_" + n) for n in (
            "flog", "fbias", "logsig", "c", "vtile", "vtaken", "scores", "max", "exp", "prob",
            "pturned", "ptaken", "out", "posrow", "poscol", "reduced", "trig", "turned", "roped")}
        s5 = {n: sem("s5_" + n) for n in (
            "dt", "angle", "mag", "trig", "bbar", "bturned", "btaken", "phase", "sincos", "bu",
            "rotated", "state", "y", "ysum", "z")}
        rt = {n: sem("rt_" + n) for n in (
            "logits", "diff", "exp", "comb", "spread", "taken")}
        moe_loaded = [sem(f"moe_loaded{i}") for i in range(HALVES)]
        moe_free = sem("moe_free")
        mo = {n: sem("mo_" + n) for n in (
            "sel", "pos", "posm", "flag", "hturned", "htaken", "pick", "gathered", "xready", "place",
            "ye", "yetaken", "spread", "added")}
        out_turned, out_taken, out_stored = sem("out_turned"), sem("out_taken"), sem("out_stored")

        kh, lf, bc, eb, en, ed = (part(4 * i, 4) for i in range(6))
        qd, kd, ku, oo, rr = lf, en, ed, kh, bc
        st = part(24, 6)
        vt = vtok[0:CHUNK].rearrange("p a (b n) -> p (a b) n", n=P)
        kt = yT[0:CHUNK].rearrange("p a (b n) -> p (a b) n", n=P)
        sc = hT[0:CHUNK, 0:4].rearrange("p a n -> p (a n)")
        xc = part(30, 4).rearrange("p (a n) -> p a n", a=4)
        rm = part(34, 4).rearrange("p (a n) -> p a n", a=4)
        ra, gr_, gi_ = hT[:, 4:8], mixT[:, 4:8], sq[:, 4:8]
        gbuf, vbuf, hid = ([part(4 * k + i) for i in range(4)] for k in range(3))
        cum, negc, fz, fa = (scr[0:HEADS, i * T:(i + 1) * T] for i in range(4))
        mraw = part(0, 6).rearrange("p (a n) -> p a n", a=6)
        mnorm = part(6, 5).rearrange("p (a n) -> p a n", a=5)
        qpe_raw = part(12, 4).rearrange("p (a n) -> p a n", a=4)
        kpe, cos, sin, ang, turns, red, mag_ = (part(16 + i) for i in range(7))
        posf = scr[0:1, 24 * T:25 * T]
        onesrow = scr[0:1, 25 * T:25 * T + P]
        tmp = part(30, 2).rearrange("p (a n) -> p a n", a=2)
        pbuf = [part(26), part(27)]
        pTs = [part(28), part(29)]
        (sv, sk, ss, scs, sA, sB, sC, sD) = (
            part(4 * i, 4).rearrange("p (a n) -> p a n", a=4) for i in range(8))
        xg = part(12, 3).rearrange("p (a n) -> p a n", a=KD)
        ye = part(18, 4)[0:CAP]
        pick = part(22)[:, 0:2 * CAP].rearrange("p (g n) -> p g n", g=2)
        place = part(23)[0:CAP]
        posm = part(24)[:, 0:2 * 16].rearrange("p (g n) -> p g n", g=2)
        sel = part(25)[:, 0:2 * 8].rearrange("p (g n) -> p g n", g=2)
        s5p = part(34, 2).rearrange("p (a n) -> p a n", a=16)
        bexp = mixT[:].rearrange("p a n -> p (a n)").rearrange("p (r t c) -> p r t c", r=2, t=S5_TILES)
        bbar = proj[:, 8:16].rearrange("p a n -> p (a n)").rearrange("p (r t c) -> p r t c", r=2,
                                                                   t=S5_TILES)
        bT = vtok[:].rearrange("p r (q n) -> p r q n", n=P)
        cT = yT[:].rearrange("p a n -> p (a n)").rearrange("p (r q n) -> p r q n", r=2, q=KD)
        DT, LA, ANG, TRN, RED, MAG, SIN, ABS, COS, AR, AI, DEN, GR, GI, PHI, S1 = range(16)
        (LMAX, LD0, LD1, LD2, LSUM, LREC, LB, OML, SPA, SPE, SPL, SPM, SP4, SP8, LG0, LG1, MX0, MX1,
         IX0, IX1, CB0, CB1, GA, GB) = range(24)

        scale_of = {"fox": 1.0, "mla": float(np.float32((HD + ROPE) ** -0.5))}
        at0 = {"fox": 0, "mla": 2 * HEADS}
        mix0 = {"even_out": 0, "odd_out": KD, "mla_o": 2 * KD}

        block = ctx.enter_context(nc.Block())

        @block.sync
        def _(sp):
            sp.dma_start(proj[:, 0:8].rearrange("p a n -> p (a n)").rearrange(
                "p (g d) -> p g d", g=2), a["x"].rearrange("g p d -> p g d")).then_inc(x_loaded, 16)
            for name in STREAM:
                sizes, u0, w = phase_units(name), UNIT0[name], a["w_" + name]

                def load(u, unit, name=name, sizes=sizes, w=w, u0=u0):
                    sp.wait_ge(slot_free, unit + u0 + 1)
                    sp.dma_start(slots[(u0 + u) % SLOTS][:, 0:sizes[u]],
                                 w[bass.ds(unit, 1), :, 0:sizes[u]].rearrange("o p n -> p (o n)")
                                 ).then_inc(slot_loaded[(u0 + u) % SLOTS], 16)

                fours = len(sizes) // SLOTS if name in FFN else 0
                if fours:
                    with sp.Fori(0, fours) as i:
                        for u in range(SLOTS):
                            load(u, i * SLOTS + u)
                for u in range(fours * SLOTS, len(sizes)):
                    load(u, u)
                if name == "ffn2":
                    sp.wait_ge(x_ready, 6 * KD)
                    sp.dma_start(cT, a["s5_cT"]).then_inc(s5_loaded, 16)
                    sp.dma_start(bexp, a["s5_b"]).then_inc(s5_loaded, 16)
            def load_half(h, unit):
                sp.dma_start(slots[h // 2][:, h % 2 * HALF:(h % 2 + 1) * HALF],
                             a["w_moe"][bass.ds(unit, 1)].rearrange("o p n -> p (o n)")
                             ).then_inc(moe_loaded[h], 16)

            for h in range(HALVES):
                sp.wait_ge(slot_free, SLOTS + max(n for n in range(len(LOADED))
                                                  if n % SLOTS == h // 2) + 1)
                load_half(h, h)
            with sp.Fori(1, EXPERTS * FE_TILES // HALVES) as i:
                for h in range(HALVES):
                    sp.wait_ge(moe_free, i * HALVES + h + 1)
                    load_half(h, i * HALVES + h)
            for g in range(2):
                sp.wait_ge(out_taken, 2 * (g + 1))
                sp.dma_start(a["out"][g], proj[:, 0:8].rearrange("p a n -> p (a n)")[
                    :, g * D:(g + 1) * D]).then_inc(out_stored, 16)
            sp.wait_ge(out_stored, 32)

        @block.gpsimd
        def _(pool):
            pool.memset(ones[:, :], 1.0).then_inc(cleared, 1)
            pool.memset(xbp[:, :, 0:3], 0.0).then_inc(cleared, 1)
            pool.wait_ge(hg["scopied"], 2)
            pool.affine_select(out=sc, in_=sc, pattern=[[0, 16], [1, CHUNK]], base=0,
                               channel_multiplier=-1, compare_op=ALU.is_ge, fill=0.0
                               ).then_inc(hg["masked"], 1)

        @block.scalar
        def _(act):
            own = Order(act, act_own)
            for dst, name in ((vec[:, :], "vec"), (cst[:, :], "cst"), (wf[:, :, :], "wf"),
                              (wr[:, :, :], "wr"), (rgw[:, :, :, :], "rgw"),
                              (pos_i[:, :], "positions")):
                act.dma_start(dst, a[name]).then_inc(small_loaded, 16)

            def squares(name, src, ready, first, at_=0):
                for c in range(dict(NORMS)[name]):
                    act.wait_ge(ready, first + c + 1)
                    act.activation(sq[:, at_ + c], src[:, c], ACT.Square).then_inc(sq_ready, 1)

            def root(name):
                n = NORM_NO[name]
                act.wait_ge(sum_ready, n + 1)
                if n:
                    act.wait_ge(rstd_ready, n)
                act.activation(rms[:, :], acc(0), ACT.Sqrt, bias=EPS,
                               scale=1.0 / (P * dict(NORMS)[name])).then_inc(rms_ready, 1)

            def pre_norm(name):
                squares(name, xT, x_ready, (X_VERSION[name] - 1) * KD)
                root(name)

            def take(phase, i, dst, func=ACT.Copy, **kw):
                act.wait_ge(tile_ready, TILE0[phase] + i + 1)
                act.activation(dst, work(TILE0[phase] + i), func, **kw).then_inc(tile_taken, 1)

            def post_linear_norm(phase, name):
                for i in range(KD):
                    take(phase, i, yT[:, i])
                squares(name, yT, tile_taken, TILE0[phase])
                root(name)

            def post_ffn_norm(no, name):
                for i in range(KD):
                    act.wait_ge(acc_ready, no * KD + i // 2 * 2 + 2)
                    act.activation(yT[:, i], acc(i), ACT.Copy).then_inc(acc_taken, 1)
                squares(name, yT, acc_taken, no * KD)
                root(name)

            def hgrn_rglru():
                for i in range(4):
                    take("even_in", i, proj[:, i], ACT.Silu)
                for i in range(4, 8):
                    take("even_in", i, proj[:, i], ACT.Sigmoid)
                for i in range(8, 12):
                    take("even_in", i, proj[:, i])
                for i in range(12, 16):
                    take("even_in", i, proj[:, i], ACT.Sigmoid)
                act.wait_ge(hg["forget"], 4)
                act.activation(lf, proj[:, 4:8].rearrange("p a n -> p (a n)"), ACT.Ln
                               ).then_inc(hg["logf"], 1)
                for i in range(16, 20):
                    take("even_in", i, xbp[:, i - 16, 3:3 + T])
                act.wait_ge(hg["bcum"], 4)
                act.activation(eb, bc, ACT.Exp).then_inc(hg["exps"], 1)
                act.activation(en, bc, ACT.Exp, scale=-1.0).then_inc(hg["exps"], 1)
                act.wait_ge(hg["decay"], 1)
                act.activation(ed, ed, ACT.Exp).then_inc(hg["exps"], 1)
                for i in range(20, 24):
                    take("even_in", i, proj[:, i - 4], ACT.Gelu_apprx_tanh)
                for b in range(2):
                    act.wait_ge(hg["scores"], b + 1)
                    act.activation(sc[:, b * 512:(b + 1) * 512], ps[0:CHUNK, b, :], ACT.Copy
                                   ).then_inc(hg["scopied"], 1)
                for j in range(RG_TILES):
                    for k, (dst, bias) in enumerate(((gr_, "rg_ba"), (gi_, "rg_bx"))):
                        act.wait_ge(rg["product"], 2 * j + k + 1)
                        act.activation(dst[:, j], work(2 * j + k), ACT.Sigmoid, bias=v(bias, j)
                                       ).then_inc(rg["gates"], 1)
                act.wait_ge(rg["rate"], 2)
                act.wait_ge(rg["gates"], 2 * RG_TILES)
                for j in range(RG_TILES):
                    act.activation(rm[:, j], gr_[:, j], ACT.Tanh, scale=tiny[:, SP4, j:j + 1]
                                   ).then_inc(rg["decay"], 1)
                for j in range(RG_TILES):
                    act.activation(ra[:, j], gr_[:, j], ACT.Exp, scale=tiny[:, SP8, j:j + 1]
                                   ).then_inc(rg["decay"], 1)
                act.wait_ge(rg["square"], 1)
                act.activation(rm, rm, ACT.Sqrt).then_inc(rg["root"], 1)
                act.wait_ge(hg["out"], 1)
                for b in range(2):
                    act.activation(oo[:, b * 512:(b + 1) * 512], ps[:, 5 + b, :], ACT.Copy
                                   ).then_inc(hg["outtaken"], 1)
                    act.activation(sq[:, 2 * b:2 * b + 2].rearrange("p a n -> p (a n)"),
                                   ps[:, 5 + b, :], ACT.Square).then_inc(hg["outtaken"], 1)
                for b in range(2):
                    act.wait_ge(hg["total"], b + 1)
                    act.activation(rr[:, b * 512:(b + 1) * 512], ps[:, b, :], ACT.Sqrt, bias=EPS,
                                   scale=1.0 / P).then_inc(hg["root"], 1)

            def attention(kind):
                n0 = at0[kind]

                def taken(i):
                    act.wait_ge(at["pturned"], n0 + i + 1)
                    if i >= 2:
                        act.wait_ge(at["out"], n0 + i - 1)
                    n = P * (i % 2 + 1)
                    act.activation(pTs[i % 2][:, 0:n], ps[:, 6 + i % 2, 0:n], ACT.Copy
                                   ).then_inc(at["ptaken"], 1)

                for i in range(2 * HEADS):
                    n = P * (i % 2 + 1)
                    act.wait_ge(at["max"], n0 + i + 1)
                    if i >= 2:
                        act.wait_ge(at["pturned"], n0 + i - 1)
                    act.activation(pbuf[i % 2][:, 0:n], ps[:, 4 + i % 2, 0:n], ACT.Exp,
                                   bias=stat[:, 1, i:i + 1], scale=scale_of[kind],
                                   accum_out=stat[:, 2, i:i + 1]).then_inc(at["exp"], 1)
                    if i >= 1:
                        taken(i - 1)
                taken(2 * HEADS - 1)
                for j in range(KD):
                    act.wait_ge(at["out"], n0 + j // 2 * 8 + 8)
                    act.activation(mixT[:, j], acc(j), ACT.Copy).then_inc(mix_ready, 1)

            def take_values(n0):
                for i in range(4):
                    act.wait_ge(at["vtile"], n0 + i + 1)
                    half, g = divmod(i, 2)
                    act.activation(vtok[:, g, half * 512:half * 512 + 512], ps[:, 2 * g + half, :],
                                   ACT.Copy).then_inc(at["vtaken"], 1)

            def fox():
                act.wait_ge(at["flog"], 1)
                act.activation(fz, acc(2)[0:HEADS], ACT.Identity,
                               bias=vec[0:HEADS, VEC["fox_bias"]:VEC["fox_bias"] + 1]
                               ).then_inc(at["fbias"], 1)
                act.wait_ge(at["fbias"], 1)
                own.mark(act.activation(fa, fz, ACT.Abs))
                own.wait()
                own.mark(act.activation(fa, fa, ACT.Exp, scale=-1.0))
                own.wait()
                act.activation(fa, fa, ACT.Ln, bias=1.0).then_inc(at["logsig"], 1)
                for i in range(16):
                    take("odd_qk", i, proj[:, i], ACT.Copy, scale=HD ** -0.5 if i < KD else 1.0)
                take_values(0)
                attention("fox")

            def feed_forward(phase, conv):
                layer = {"ffn0": 0, "ffn1": 1}.get(phase, 0)

                def hidden(j, f, i):
                    n, p = f + FT0[phase], pair(j, 0)
                    if not conv:
                        act.wait_ge(up_ready, 2 * n + 1)
                        act.activation(gbuf[j % 4], p, ACT.Silu).then_inc(gate_act, 1)
                        return
                    bias = vec[:, bass.ds(VEC["ffn_conv_b"] + layer * 2 * FF_TILES + f, 1)]
                    tap = vec[:, bass.ds(VEC["ffn_conv_w"] + (layer * 3 + 2) * 2 * FF_TILES + f, 1)]
                    bias_v = vec[:, bass.ds(VEC["ffn_conv_b"] + (layer * 2 + 1) * FF_TILES + f, 1)]
                    tap_v = vec[:, bass.ds(
                        VEC["ffn_conv_w"] + ((layer * 3 + 2) * 2 + 1) * FF_TILES + f, 1)]
                    act.wait_ge(up_ready, 2 * n + 1)
                    act.activation(gbuf[j % 4], p, ACT.Identity, bias=bias, scale=tap
                                   ).then_inc(gate_init, 1)
                    act.wait_ge(gate_conv, n + 1)
                    act.activation(gbuf[j % 4], gbuf[j % 4], ACT.Gelu_apprx_tanh
                                   ).then_inc(gate_act, 1)
                    act.wait_ge(up_ready, 2 * n + 2)
                    act.activation(vbuf[j % 4], pair(j, 1), ACT.Identity, bias=bias_v,
                                   scale=tap_v).then_inc(val_init, 1)

                with act.Fori(0, FFN[phase] // 4) as i:
                    for j in range(4):
                        hidden(j, i * 4 + j, i)
                for f in range(FFN[phase] // 4 * 4, FFN[phase]):
                    hidden(f, f, 0)

            def mla():
                pre_norm("m0")
                for i in range(6):
                    take("mla_in", i, mraw[:, i])
                squares("mq", mraw, tile_taken, TILE0["mla_in"])
                squares("mkv", mraw[:, 3:5], tile_taken, TILE0["mla_in"] + 3, at_=3)
                root("mq")
                act.wait_ge(at["reduced"], 1)
                act.activation(sin, red, ACT.Sin).then_inc(at["trig"], 1)
                own.mark(act.activation(mag_, red, ACT.Abs))
                own.wait()
                act.activation(cos, mag_, ACT.Sin, scale=-1.0, bias=float(np.pi / 2)
                               ).then_inc(at["trig"], 1)
                root("mkv")
                for i in range(8):
                    take("mla_uq", i, proj[:, i])
                for i in range(8, 12):
                    take("mla_uq", i, qpe_raw[:, i - 8])
                for i in range(8):
                    take("mla_uk", i, proj[:, 8 + i])
                take_values(4)
                attention("mla")
                for i in range(KD):
                    take("mla_o", i, yT[:, i])

            def s5_mixer():
                pre_norm("m2")
                act.activation(s5p[:, DT], v("log_dt", 0, 32), ACT.Exp).then_inc(s5["dt"], 1)
                act.wait_ge(s5["angle"], 1)
                act.activation(s5p[:, MAG], s5p[:, LA], ACT.Exp).then_inc(s5["mag"], 1)
                act.activation(s5p[:, SIN], s5p[:, RED], ACT.Sin).then_inc(s5["trig"], 1)
                own.mark(act.activation(s5p[:, ABS], s5p[:, RED], ACT.Abs))
                own.wait()
                act.activation(s5p[:, COS], s5p[:, ABS], ACT.Sin, scale=-1.0,
                               bias=float(np.pi / 2)).then_inc(s5["trig"], 1)
                for i in range(KD):
                    take("s5_in", i, proj[:, i])
                for b in range(4):
                    act.wait_ge(s5["bturned"], b + 1)
                    act.activation(vtok[:, b // 2, (b % 2) * 512:(b % 2) * 512 + 512], ps[:, b, :],
                                   ACT.Copy).then_inc(s5["btaken"], 1)
                for q in range(KD):
                    act.wait_ge(s5["phase"], q + 1)
                    act.activation(ss, sv, ACT.Sin, scale=TWO_PI_SAFE).then_inc(s5["sincos"], 1)
                    own.mark(act.activation(sk, sv, ACT.Abs))
                    own.wait()
                    act.activation(scs, sk, ACT.Sin, scale=-TWO_PI_SAFE, bias=float(np.pi / 2)
                                   ).then_inc(s5["sincos"], 1)
                for q in range(KD):
                    act.wait_ge(s5["ysum"], q + 1)
                    act.activation(hT[:, q], sq[:, q], ACT.Gelu_apprx_tanh).then_inc(s5["z"], 1)
                for j in range(KD):
                    take("s5_glu", 2 * j, mixT[:, j])
                    take("s5_glu", 2 * j + 1, sq[:, j], ACT.Sigmoid)

            def experts_gathered():
                def take_input(n):
                    for b in range(2):
                        act.wait_ge(mo["gathered"], n + b + 1)
                        act.activation(xg[:, 4 * b:4 * b + 4], ps[:, 4 + b, 0:4 * CAP].rearrange(
                            "p (a n) -> p a n", a=4), ACT.Copy).then_inc(mo["xready"], 1)

                take_input(0)
                with act.Fori(0, EXPERTS) as e:
                    with act.Fori(0, FE_TILES // 4) as i:
                        for j in range(4):
                            n = e * FE_TILES + i * 4 + (FT0["moe"] + j)
                            act.wait_ge(up_ready, 2 * n + 1)
                            act.activation(gbuf[j][:, 0:CAP], pair(j, 0)[:, 0:CAP], ACT.Silu
                                           ).then_inc(gate_act, 1)
                    take_input(2 * e + 2)
                    act.wait_ge(mo["ye"], e + 1)
                    for b in range(2):
                        act.activation(ye[:, b * 512:(b + 1) * 512], ps[0:CAP, b, :], ACT.Copy
                                       ).then_inc(mo["yetaken"], 1)

            def experts():
                act.wait_ge(mo["flag"], 1)
                with act.If(act.value_load(crowded[0:1, 0:1], min_val=0, max_val=1) == 1):
                    feed_forward("moe", False)
                with act.Else():
                    experts_gathered()

            def router():
                pre_norm("m3")
                for b in range(4):
                    act.wait_ge(mo["hturned"], b + 1)
                    act.activation(vtok[:, b // 2, (b % 2) * 512:(b % 2) * 512 + 512],
                                   ps[:, 4 + b, :], ACT.Copy).then_inc(mo["htaken"], 1)
                act.wait_ge(rt["diff"], 2)
                act.activation(tiny[:, GA:GA + 1, 0:2], tiny[:, GA:GA + 1, 0:2], ACT.Exp
                               ).then_inc(rt["exp"], 1)
                for b in range(4):
                    act.wait_ge(rt["spread"], b + 1)
                    act.activation(mixT[:, 2 * b:2 * b + 2].rearrange("p a n -> p (a n)"),
                                   ps[:, b, :], ACT.Copy).then_inc(rt["taken"], 1)
                    act.wait_ge(rt["spread"], 4 + b + 1)
                    act.activation(yT[:, 2 * b:2 * b + 2].rearrange("p a n -> p (a n)"),
                                   ps[:, 4 + b, :], ACT.Copy).then_inc(rt["taken"], 1)

            act.wait_ge(small_loaded, 16 * 6)
            act.wait_ge(hg["lbdiff"], 3)
            act.activation(tiny[:, LD0:LD0 + 3, 0:4], tiny[:, LD0:LD0 + 3, 0:4], ACT.Exp
                           ).then_inc(hg["lbexp"], 1)
            own.mark(act.activation(tiny[:, SPA, 0:4], v("rg_lambda", 0, 4), ACT.Abs))
            own.wait()
            own.mark(act.activation(tiny[:, SPE, 0:4], tiny[:, SPA, 0:4], ACT.Exp, scale=-1.0))
            own.wait()
            act.activation(tiny[:, SPL, 0:4], tiny[:, SPE, 0:4], ACT.Ln, bias=1.0
                           ).then_inc(rg["softplus"], 1)
            pre_norm("n0")
            hgrn_rglru()
            post_linear_norm("even_out", "n1")
            pre_norm("n2")
            feed_forward("ffn0", True)
            post_ffn_norm(0, "n3")
            pre_norm("n4")
            fox()
            post_linear_norm("odd_out", "n5")
            pre_norm("n6")
            feed_forward("ffn1", True)
            post_ffn_norm(1, "n7")
            mla()
            pre_norm("m1")
            feed_forward("ffn2", False)
            s5_mixer()
            router()
            experts()
            pre_norm("mf")
            for b in range(4):
                act.wait_ge(out_turned, b + 1)
                act.activation(proj[:, 2 * b:2 * b + 2].rearrange("p a n -> p (a n)"), ps[:, b, :],
                               ACT.Copy).then_inc(out_taken, 1)

        @block.tensor
        def _(pe):
            def need(phase, u):
                n = UNIT0[phase] + u
                pe.wait_ge(slot_loaded[n % SLOTS], LOADED[n])
                return slots[n % SLOTS]

            def total(name, at_=0):
                tiles = dict(NORMS)[name]
                if NORM_NO[name]:
                    pe.wait_ge(rms_ready, NORM_NO[name])
                for c in range(tiles):
                    pe.wait_ge(sq_ready, SQ0[name] + max(c, 1) + 1)
                    m = pe.matmul(acc(0), ones[:, :], sq[:, at_ + c], start=c == 0,
                                  stop=c == tiles - 1, skip_group_check=True)
                m.then_inc(sum_ready, 1)

            def linear(phase, src, ready, first):
                tiles, k = LINEAR[phase]
                per = UNIT_TILES if k == KD else tiles
                for i in range(tiles):
                    n = TILE0[phase] + i
                    if i % per == 0:
                        w = need(phase, i // per)
                    if n >= WORK:
                        pe.wait_ge(tile_taken, n - WORK + 1)
                    for c in range(k):
                        if i == 0:
                            pe.wait_ge(ready, first + c + 1)
                        o = ((i % per) * k + c) * P
                        m = pe.matmul(work(n), w[:, o:o + P], src[:, c], start=c == 0,
                                      stop=c == k - 1, skip_group_check=True)
                    m.then_inc(tile_ready, 1)
                    if i % per == per - 1 or i == tiles - 1:
                        pe.wait_ge(tile_ready, n + 1)
                        pe.sem_inc(slot_free, 1)

            def feed_forward(phase):
                n_ft = FFN[phase]

                def up(f, i):
                    u, half = f // FT_UNIT, f % FT_UNIT
                    n = UNIT0[phase] + u
                    w = slots[n % SLOTS]
                    if half == 0:
                        pe.wait_ge(slot_loaded[n % SLOTS], LOADED[n] + i * 16)
                    for k in range(2):
                        for c in range(KD):
                            o = ((k * FT_UNIT + half) * KD + c) * P
                            m = pe.matmul(pair(f, k), w[:, o:o + P], hT[:, c], start=c == 0,
                                          stop=c == KD - 1, skip_group_check=True)
                        m.then_inc(up_ready, 1)

                def down(f, i, first=False, last=False):
                    u, half = f // FT_UNIT, f % FT_UNIT
                    w = slots[(UNIT0[phase] + u) % SLOTS]
                    pe.wait_ge(hid_ready, i * 8 + (FT0[phase] + f + 1))
                    for d in range(KD):
                        o = (2 * FT_UNIT * KD + half * KD + d) * P
                        m = pe.matmul(acc(d), w[:, o:o + P], hid[f % 4], start=first and d % 2 == 0,
                                      stop=last, skip_group_check=True)
                        if last:
                            m.then_inc(acc_ready, 1)
                    if half == FT_UNIT - 1 and not last:
                        m.then_inc(slot_free, 1)

                for c in range(KD):
                    pe.wait_ge(h_ready, SQ0[{"ffn0": "n2", "ffn1": "n6", "ffn2": "m1",
                                             "moe": "m3"}[phase]] + c + 1)
                up(0, 0)
                up(1, 0)
                down(0, 0, first=True)
                loops = (n_ft - 2) // 8
                with pe.Fori(0, loops) as i:
                    for j in range(8):
                        up(j + 2, i)
                        down(j + 1, i)
                for f in range(8 * loops + 1, n_ft):
                    if f + 1 < n_ft:
                        up(f + 1, 0)
                    down(f, 0, last=f == n_ft - 1)
                pe.wait_ge(acc_ready, KD * (list(FFN).index(phase) + 1))
                pe.sem_inc(slot_free, 1)

            def hgrn_rglru():
                pe.wait_ge(tile_taken, 12)
                for n in range(16):
                    h, c = divmod(n, 4)
                    m = pe.transpose(ps[0:CHUNK, n // 4, (n % 4) * P:(n % 4 + 1) * P],
                                     proj[:, 8 + h, c * CHUNK:(c + 1) * CHUNK], ident)
                    if n % 4 == 3:
                        m.then_inc(hg["vturned"], 1)
                pe.wait_ge(hg["gated"], 2)
                pe.wait_ge(hg["vtaken"], 4)
                for n in range(16):
                    t = slice(n * CHUNK, (n + 1) * CHUNK)
                    m = pe.matmul(ps[0:CHUNK, n // 8, (n % 8) * CHUNK:(n % 8 + 1) * CHUNK],
                                  kd[:, t], qd[:, t], start=True, stop=True, skip_group_check=True)
                    if n % 8 == 7:
                        m.then_inc(hg["scores"], 1)
                pe.wait_ge(tile_taken, 24)
                for j in range(RG_TILES):
                    pe.wait_ge(rg["conv"], j + 1)
                    for k in range(2):
                        if 2 * j + k >= WORK:
                            pe.wait_ge(rg["gates"], 2 * j + k - WORK + 1)
                        pe.matmul(work(2 * j + k), rgw[:, k, j, :], xc[:, j], start=True, stop=True,
                                  skip_group_check=True).then_inc(rg["product"], 1)
                pe.wait_ge(hg["gated"], 3)
                pe.wait_ge(rg["gates"], 2 * RG_TILES)
                for n in range(16):
                    m = pe.transpose(ps[0:CHUNK, 4 + n // 4, (n % 4) * P:(n % 4 + 1) * P],
                                     ku[:, n * CHUNK:(n + 1) * CHUNK], ident)
                    if n % 4 == 3:
                        m.then_inc(hg["kturned"], 1)
                pe.wait_ge(hg["ktaken"], 4)
                for c in range(3):
                    for h in range(A_HEADS):
                        m = pe.matmul(ps[:, 2 + c, h * P:(h + 1) * P], kt[:, 4 * h + c, :],
                                      vt[:, 4 * h + c, :], start=True, stop=True,
                                      skip_group_check=True)
                    m.then_inc(hg["upd"], 1)
                pe.wait_ge(hg["masked"], 1)
                for c in range(NCHUNK):
                    if c:
                        pe.wait_ge(hg["state"], (1, 5, 9)[c - 1])
                    for h in range(A_HEADS):
                        n = 4 * h + c
                        t = slice(n * CHUNK, (n + 1) * CHUNK)
                        o = ps[:, 5 + h // 2, (h % 2) * T + c * CHUNK:(h % 2) * T + (c + 1) * CHUNK]
                        m = pe.matmul(o, vt[:, n, :], sc[:, t], start=True, stop=c == 0,
                                      skip_group_check=True)
                        if c:
                            s = (c - 1) * 512 + h * P
                            m = pe.matmul(o, st[:, s:s + P], qd[:, t], start=False, stop=True,
                                          skip_group_check=True)
                m.then_inc(hg["out"], 1)
                pe.wait_ge(hg["outtaken"], 4)
                for b in range(2):
                    pe.matmul(ps[:, b, :], ones[:, :],
                              sq[:, 2 * b:2 * b + 2].rearrange("p a n -> p (a n)"), start=True,
                              stop=True, skip_group_check=True).then_inc(hg["total"], 1)

            def attention(kind, score):
                n0 = at0[kind]

                def scores(i):
                    if i >= 2:
                        pe.wait_ge(at["exp"], n0 + i - 1)
                    h, qb = divmod(i, 2)
                    score(h, qb, P * (qb + 1), ps[:, 4 + i % 2, :])
                    pe.matmul(ps[:, 4 + i % 2, qb * P:(qb + 1) * P], ident, mask, start=False,
                              stop=True, skip_group_check=True).then_inc(at["scores"], 1)

                def turn(i):
                    pe.wait_ge(at["prob"], n0 + i + 1)
                    if i >= 2:
                        pe.wait_ge(at["ptaken"], n0 + i - 1)
                    for b in range(i % 2 + 1):
                        m = pe.transpose(ps[:, 6 + i % 2, b * P:(b + 1) * P],
                                         pbuf[i % 2][:, b * P:(b + 1) * P], ident)
                    m.then_inc(at["pturned"], 1)

                def output(i):
                    pe.wait_ge(at["ptaken"], n0 + i + 1)
                    h, qb = divmod(i, 2)
                    o = acc(h // 2)[HD * (h % 2):HD * (h % 2) + HD, qb * P:(qb + 1) * P]
                    for b in range(qb + 1):
                        m = pe.matmul(o, vtok[:, b, h * HD:(h + 1) * HD],
                                      pTs[i % 2][:, b * P:(b + 1) * P], start=b == 0, stop=b == qb,
                                      skip_group_check=True)
                    m.then_inc(at["out"], 1)

                pe.wait_ge(at["vtaken"], 4 if kind == "fox" else 8)
                scores(0)
                scores(1)
                for i in range(2 * HEADS):
                    turn(i)
                    if i + 2 < 2 * HEADS:
                        scores(i + 2)
                    output(i)

            def values(phase, src, k, n0):
                units = len(phase_units(phase))
                for half in range(2):
                    if half < units:
                        w = need(phase, half)
                    for g in range(2):
                        for c in range(k):
                            o = c * 512 if units == 2 else c * D + half * 512
                            m = pe.matmul(ps[:, 2 * g + half, :], src[:, c, g * P:(g + 1) * P],
                                          w[:, o:o + 512], start=c == 0, stop=c == k - 1,
                                          skip_group_check=True)
                        m.then_inc(at["vtile"], 1)
                    if units == 2 or half == 1:
                        pe.wait_ge(at["vtile"], n0 + 2 * half + 2)
                        pe.sem_inc(slot_free, 1)

            def fox():
                for c in range(KD):
                    pe.wait_ge(h_ready, SQ0["n4"] + c + 1)
                    m = pe.matmul(acc(2)[0:HEADS], wf[:, c, :], hT[:, c], start=c == 0,
                                  stop=c == KD - 1, skip_group_check=True)
                m.then_inc(at["flog"], 1)
                linear("odd_qk", hT, h_ready, SQ0["n4"])
                pe.wait_ge(at["fbias"], 1)
                values("odd_v", hT, KD, 0)
                pe.wait_ge(tile_taken, TILE0["odd_qk"] + 16)
                pe.wait_ge(at["c"], 2)

                def score(h, qb, n, o):
                    r = HD * (h % 2)
                    pe.matmul(o[:, 0:n], proj[r:r + HD, h // 2, qb * P:(qb + 1) * P],
                              proj[r:r + HD, 8 + h // 2, 0:n], start=True, stop=False,
                              skip_group_check=True)
                    one = cst[0:HEADS, CST["ident"] + h:CST["ident"] + h + 1]
                    pe.matmul(o[:, 0:n], cum[:, qb * P:(qb + 1) * P], one.to_broadcast([HEADS, n]),
                              start=False, stop=False, skip_group_check=True)
                    pe.matmul(o[:, 0:n], one.to_broadcast([HEADS, P]), negc[:, 0:n], start=False,
                              stop=False, skip_group_check=True)

                attention("fox", score)

            def mla():
                total("m0")
                linear("mla_in", hT, h_ready, SQ0["m0"])
                total("mq")
                pe.wait_ge(at["posrow"], 2)
                pe.matmul(acc(2), onesrow, posf, start=True, stop=True, skip_group_check=True
                          ).then_inc(at["poscol"], 1)
                total("mkv", 3)
                linear("mla_uq", mnorm, h_ready, SQ0["mq"])
                linear("mla_uk", mnorm[:, 3:5], h_ready, SQ0["mkv"])
                pe.wait_ge(tile_taken, TILE0["mla_uk"] + 8)
                for i in range(5):
                    if i >= WORK:
                        pe.wait_ge(at["roped"], i - WORK + 1)
                    pe.matmul(work(i), rot, qpe_raw[:, i] if i < 4 else mraw[:, 5], start=True,
                              stop=True, skip_group_check=True).then_inc(at["turned"], 1)
                values("mla_uv", mnorm[:, 3:5], 2, 4)
                pe.wait_ge(at["roped"], 5)

                def score(h, qb, n, o):
                    r = HD * (h % 2)
                    pe.matmul(o[:, 0:n], proj[r:r + HD, h // 2, qb * P:(qb + 1) * P],
                              proj[r:r + HD, 8 + h // 2, 0:n], start=True, stop=False,
                              skip_group_check=True)
                    r = ROPE * (h % 4)
                    pe.matmul(o[:, 0:n], proj[r:r + ROPE, 16 + h // 4, qb * P:(qb + 1) * P],
                              kpe[r:r + ROPE, 0:n], start=False, stop=False, skip_group_check=True)

                attention("mla", score)
                linear("mla_o", mixT, mix_ready, mix0["mla_o"])

            def s5_mixer():
                total("m2")
                linear("s5_in", hT, h_ready, SQ0["m2"])
                pe.wait_ge(s5["bbar"], 2)
                for n in range(16):
                    r, q = divmod(n, 8)
                    m = pe.transpose(ps[:, n // 4, (n % 4) * P:(n % 4 + 1) * P],
                                     bbar[:, r, 4 * q:4 * q + 4, :].rearrange("p t c -> p (t c)"),
                                     ident)
                    if n % 4 == 3:
                        m.then_inc(s5["bturned"], 1)
                pe.wait_ge(s5["btaken"], 4)
                pe.wait_ge(tile_taken, TILE0["s5_in"] + 8)
                pe.wait_ge(s5_loaded, 32)

                def inputs(q):
                    if q:
                        pe.wait_ge(s5["rotated"], q)
                    for r in range(2):
                        for j in range(4):
                            k = 32 * j
                            m = pe.matmul(ps[:, 4 + j, r * T:(r + 1) * T],
                                          bT[k:k + 32, r, q, :], proj[k:k + 32, q, :], start=True,
                                          stop=True, skip_group_check=True)
                    m.then_inc(s5["bu"], 1)

                inputs(0)
                for q in range(KD):
                    if q + 1 < KD:
                        inputs(q + 1)
                    pe.wait_ge(s5["state"], q + 1)
                    if q >= 2:
                        pe.wait_ge(s5["ysum"], q - 1)
                    for j in range(4):
                        k = 32 * j
                        o = ps[k:k + 32, q % 2, 0:T]
                        pe.matmul(o, cT[:, 0, q, k:k + 32], sA[:, j], start=True, stop=False,
                                  skip_group_check=True)
                        m = pe.matmul(o, cT[:, 1, q, k:k + 32], sC[:, j], start=False, stop=True,
                                      skip_group_check=True)
                    m.then_inc(s5["y"], 1)
                linear("s5_glu", hT, s5["z"], 0)

            def router():
                total("m3")
                for g in range(2):
                    for c in range(KD):
                        pe.wait_ge(h_ready, SQ0["m3"] + c + 1)
                        m = pe.matmul(ps[:, 2, g * 8:g * 8 + 8], hT[:, c, g * P:(g + 1) * P],
                                      wr[:, c, :], start=c == 0, stop=c == KD - 1,
                                      skip_group_check=True)
                    m.then_inc(rt["logits"], 1)
                for n in range(16):
                    g, c = divmod(n, 8)
                    m = pe.transpose(ps[:, 4 + n // 4, (n % 4) * P:(n % 4 + 1) * P],
                                     hT[:, c, g * P:(g + 1) * P], ident)
                    if n % 4 == 3:
                        m.then_inc(mo["hturned"], 1)
                pe.wait_ge(mo["sel"], 2)
                for g in range(2):
                    o = ps[:, 3, g * 8:g * 8 + 8]
                    pe.matmul(o, before, sel[:, g], start=True, stop=g == 0, skip_group_check=True)
                    if g:
                        pe.matmul(o, ones[:, :], sel[:, 0], start=False, stop=True,
                                  skip_group_check=True)
                for g in range(2):
                    m = pe.matmul(ps[:, 3, 16:24], ones[:, :], sel[:, g], start=g == 0, stop=g == 1,
                                  skip_group_check=True)
                m.then_inc(mo["pos"], 1)
                pe.wait_ge(rt["comb"], 2)
                pe.wait_ge(mo["posm"], 2)
                pe.wait_ge(mo["flag"], 1)
                pe.wait_ge(mo["htaken"], 4)
                for e in range(EXPERTS):
                    for g in range(2):
                        m = pe.matmul(acc(e)[:, g * P:(g + 1) * P],
                                      tiny[:, CB0 + g, e:e + 1].to_broadcast([P, P]), ident,
                                      start=True, stop=True, skip_group_check=True)
                    if e % 2:
                        m.then_inc(rt["spread"], 1)
                for e in range(EXPERTS):
                    for g in range(2):
                        m = pe.matmul(ps[:, 4 + e // 2, e % 2 * T + g * P:e % 2 * T + (g + 1) * P],
                                      posm[:, g, e:e + 1].to_broadcast([P, P]), ident,
                                      start=True, stop=True, skip_group_check=True)
                    if e % 2:
                        m.then_inc(rt["spread"], 1)
                pe.wait_ge(rt["taken"], 8)

            def half_slot(f, e):
                h = f % HALVES
                pe.wait_ge(moe_loaded[h], e * (16 * FE_TILES // HALVES) + 16 * (f // HALVES + 1))
                return slots[h // 2][:, h % 2 * HALF:(h % 2 + 1) * HALF]

            def experts_dense():
                for b in range(4):
                    pe.matmul(ps[:, b, 0:1], ident, mask[:, 0:1], start=True, stop=False,
                              skip_group_check=True)
                with pe.Fori(0, EXPERTS) as e:
                    def up(f):
                        w = half_slot(f, e)
                        for k in range(2):
                            for c in range(KD):
                                o = (k * KD + c) * P
                                m = pe.matmul(pair(f, k), w[:, o:o + P], hT[:, c], start=c == 0,
                                              stop=c == KD - 1, skip_group_check=True)
                            m.then_inc(up_ready, 1)

                    def down(f):
                        h = f % HALVES
                        pe.wait_ge(hid_ready, e * FE_TILES + (FT0["moe"] + f + 1))
                        for d in range(KD):
                            o = h % 2 * HALF + (2 * KD + d) * P
                            m = pe.matmul(acc(d), slots[h // 2][:, o:o + P], hid[f % 4],
                                          start=False, stop=False, skip_group_check=True)
                        m.then_inc(moe_free, 1)

                    up(0)
                    for f in range(FE_TILES):
                        if f + 1 < FE_TILES:
                            up(f + 1)
                        down(f)
                pe.wait_ge(moe_free, HALVES + EXPERTS * FE_TILES)
                pe.sem_inc(acc_ready, KD)

            def experts_gathered():
                def gather(n, g_no):
                    pe.wait_ge(mo["pick"], g_no)
                    for b in range(2):
                        for k in range(4):
                            c = 4 * b + k
                            for g in range(2):
                                m = pe.matmul(ps[:, 4 + b, k * CAP:(k + 1) * CAP],
                                              vtok[:, g, c * P:(c + 1) * P], pick[:, g],
                                              start=g == 0, stop=g == 1, skip_group_check=True)
                        m.then_inc(mo["gathered"], 1)

                gather(0, 2)
                with pe.Fori(0, EXPERTS) as e:
                    def up(f):
                        w = half_slot(f, e)
                        for k in range(2):
                            for c in range(KD):
                                o = (k * KD + c) * P
                                m = pe.matmul(pair(f, k)[:, 0:CAP], w[:, o:o + P], xg[:, c],
                                              start=c == 0, stop=c == KD - 1, skip_group_check=True)
                            m.then_inc(up_ready, 1)

                    def down(f):
                        h = f % HALVES
                        pe.wait_ge(hid_ready, e * FE_TILES + (FT0["moe"] + f + 1))
                        for b in range(2):
                            o = h % 2 * HALF + 2 * KD * P + b * 512
                            m = pe.matmul(ps[0:CAP, b, :], hid[f % 4][:, 0:CAP],
                                          slots[h // 2][:, o:o + 512], start=f == 0,
                                          stop=f == FE_TILES - 1, skip_group_check=True)
                        m.then_inc(moe_free, 1)

                    pe.wait_ge(mo["xready"], 2 * e + 2)
                    up(0)
                    for f in range(FE_TILES):
                        if f + 1 < FE_TILES:
                            up(f + 1)
                        else:
                            gather(e + 1, 2 * e + 4)
                        down(f)
                    pe.wait_ge(moe_free, e * FE_TILES + (HALVES + FE_TILES))
                    pe.sem_inc(mo["ye"], 1)
                    pe.wait_ge(mo["yetaken"], 2 * e + 2)
                    pe.wait_ge(mo["place"], e + 1)
                    for d in range(KD):
                        pe.wait_ge(mo["added"], e * KD + (d + 1))
                        pe.matmul(ps[:, 2 + d % 2, 0:T], ye[:, d * P:(d + 1) * P], place,
                                  start=True, stop=True, skip_group_check=True
                                  ).then_inc(mo["spread"], 1)

            def experts():
                pe.sem_inc(moe_free, HALVES)
                with pe.If(pe.value_load(crowded[0:1, 0:1], min_val=0, max_val=1) == 1):
                    experts_dense()
                with pe.Else():
                    experts_gathered()

            pe.sem_inc(slot_free, SLOTS)
            pe.wait_ge(small_loaded, 16 * 6)
            pe.wait_ge(x_loaded, 16)
            pe.wait_ge(cleared, 2)
            xin = proj[:, 0:8].rearrange("p a n -> p (a n)")
            for c in range(KD):
                for g in range(2):
                    m = pe.transpose(acc(c)[:, g * P:(g + 1) * P],
                                     xin[:, g * D + c * P:g * D + (c + 1) * P], ident)
                m.then_inc(x_turned, 1)
            pe.wait_ge(x_ready, KD)
            total("n0")
            linear("even_in", hT, h_ready, SQ0["n0"])
            hgrn_rglru()
            linear("even_out", mixT, mix_ready, mix0["even_out"])
            total("n1")
            total("n2")
            feed_forward("ffn0")
            total("n3")
            total("n4")
            fox()
            linear("odd_out", mixT, mix_ready, mix0["odd_out"])
            total("n5")
            total("n6")
            feed_forward("ffn1")
            total("n7")
            mla()
            total("m1")
            feed_forward("ffn2")
            s5_mixer()
            router()
            experts()
            total("mf")
            pe.wait_ge(h_ready, SQ0["mf"] + KD)
            for b in range(4):
                g = b // 2
                for k in range(4):
                    m = pe.transpose(ps[:, b, k * P:(k + 1) * P],
                                     hT[:, 4 * (b % 2) + k, g * P:(g + 1) * P], ident)
                m.then_inc(out_turned, 1)

        @block.vector
        def _(dve):
            own = Order(dve, dve_own)

            def step(instruction):
                own.mark(instruction)
                own.wait()

            def scale_tile(name, c, src, dst, gain):
                dve.scalar_tensor_tensor(out=dst, in0=src, scalar=gain, in1=rstd[:, :],
                                         op0=ALU.mult, op1=ALU.mult).then_inc(h_ready, 1)

            def reciprocal(name):
                n = NORM_NO[name]
                dve.wait_ge(rms_ready, n + 1)
                dve.reciprocal(rstd[:, :], rms[:, :]).then_inc(rstd_ready, 1)
                dve.wait_ge(rstd_ready, n + 1)

            def pre_norm(name, src, dst, gain, i0):
                reciprocal(name)
                for c in range(dict(NORMS)[name]):
                    scale_tile(name, c, src[:, c], dst[:, c], v(gain, i0 + c))

            def post_norm(name, i0):
                reciprocal(name)
                for c in range(KD):
                    scale_tile(name, c, yT[:, c], yT[:, c], v("norm_gains", i0 + c))
                for c in range(KD):
                    dve.wait_ge(h_ready, SQ0[name] + c + 1)
                    dve.tensor_tensor(xT[:, c], xT[:, c], yT[:, c], ALU.add).then_inc(x_ready, 1)

            def hgrn_rglru():
                t0 = TILE0["even_in"]
                for h in range(A_HEADS):
                    dve.wait_ge(tile_taken, t0 + 4 + h + 1)
                    dve.tensor_scalar(proj[:, 4 + h], proj[:, 4 + h], tiny[:, OML, h:h + 1],
                                      tiny[:, LB, h:h + 1], ALU.mult, ALU.add
                                      ).then_inc(hg["forget"], 1)
                dve.wait_ge(hg["forget"], 4)
                own.mark(dve.tensor_scalar(kh, proj[:, 4:8].rearrange("p a n -> p (a n)"), -1.0, 1.0,
                                           ALU.mult, ALU.add))
                dve.wait_ge(hg["logf"], 1)
                for h in range(A_HEADS):
                    dve.tensor_tensor_scan(bc[:, h * T:(h + 1) * T], chunk_mask,
                                           lf[:, h * T:(h + 1) * T], 0.0, ALU.mult, ALU.add
                                           ).then_inc(hg["bcum"], 1)
                dve.wait_ge(hg["bcum"], 4)
                b3 = bc.rearrange("p (n c) -> p n c", c=CHUNK)
                dve.tensor_tensor(ed.rearrange("p (n c) -> p n c", c=CHUNK),
                                  b3[:, :, CHUNK - 1:CHUNK].to_broadcast([P, 16, CHUNK]), b3,
                                  ALU.subtract).then_inc(hg["decay"], 1)
                dve.wait_ge(hg["exps"], 3)
                dve.tensor_tensor(qd, proj[:, 0:4].rearrange("p a n -> p (a n)"), eb, ALU.mult
                                  ).then_inc(hg["gated"], 1)
                own.wait()
                dve.tensor_tensor(kd, kh, en, ALU.mult).then_inc(hg["gated"], 1)
                dve.tensor_tensor(ku, kh, ed, ALU.mult).then_inc(hg["gated"], 1)
                for j in range(RG_TILES):
                    dve.wait_ge(tile_taken, t0 + 16 + j + 1)
                    step(dve.tensor_scalar(xc[:, j], xbp[:, j, 3:3 + T], v("rg_conv_w", 12 + j),
                                           v("rg_conv_b", j), ALU.mult, ALU.add))
                    for k in (2, 1, 0):
                        m = dve.scalar_tensor_tensor(
                            out=xc[:, j], in0=xbp[:, j, k:k + T], scalar=v("rg_conv_w", 4 * k + j),
                            in1=xc[:, j], op0=ALU.mult, op1=ALU.add)
                        if k:
                            step(m)
                    m.then_inc(rg["conv"], 1)
                for b in range(4):
                    dve.wait_ge(hg["vturned"], b + 1)
                    dve.tensor_copy(vt[:, 4 * b:4 * b + 4, :].rearrange("p a n -> p (a n)"),
                                    ps[0:CHUNK, b, :]).then_inc(hg["vtaken"], 1)
                dve.wait_ge(rg["decay"], 2 * RG_TILES)
                step(dve.scalar_tensor_tensor(out=rm, in0=ra, scalar=1.0, in1=rm, op0=ALU.add,
                                              op1=ALU.mult))
                step(dve.tensor_scalar(ra, rm, -1.0, 1.0, ALU.mult, ALU.add))
                dve.scalar_tensor_tensor(out=rm, in0=ra, scalar=1.0, in1=rm, op0=ALU.add,
                                         op1=ALU.mult).then_inc(rg["square"], 1)
                step(dve.tensor_tensor(xc, xc, gi_, ALU.mult))
                for b in range(4):
                    dve.wait_ge(hg["kturned"], b + 1)
                    dve.tensor_copy(kt[:, 4 * b:4 * b + 4, :].rearrange("p a n -> p (a n)"),
                                    ps[0:CHUNK, 4 + b, :]).then_inc(hg["ktaken"], 1)
                dve.wait_ge(hg["upd"], 1)
                dve.tensor_copy(st[:, 0:512], ps[:, 2, :]).then_inc(hg["state"], 1)
                for c in (1, 2):
                    dve.wait_ge(hg["upd"], c + 1)
                    dve.wait_ge(hg["state"], 4 * c - 3)
                    for h in range(A_HEADS):
                        n, last = c * 512 + h * P, h * T + c * CHUNK + CHUNK - 1
                        dve.scalar_tensor_tensor(
                            out=st[:, n:n + P], in0=st[:, n - 512:n - 512 + P],
                            scalar=eb[:, last:last + 1], in1=ps[:, 2 + c, h * P:(h + 1) * P],
                            op0=ALU.mult, op1=ALU.add).then_inc(hg["state"], 1)
                dve.wait_ge(rg["root"], 1)
                own.mark(dve.memset(ra[:, :, 0:1], 0.0))
                step(dve.tensor_tensor(xc, xc, rm, ALU.mult))
                step(dve.tensor_tensor_scan(gi_.rearrange("p a n -> p (a n)"),
                                            ra.rearrange("p a n -> p (a n)"),
                                            xc.rearrange("p a n -> p (a n)"), 0.0, ALU.mult,
                                            ALU.add))
                own.mark(dve.tensor_tensor(mixT[:, 4:8], gi_, proj[:, 16:20], ALU.mult))
                dve.wait_ge(hg["root"], 2)
                step(dve.reciprocal(rr, rr))
                for h in range(A_HEADS):
                    t = slice(h * T, (h + 1) * T)
                    m = dve.scalar_tensor_tensor(out=oo[:, t], in0=oo[:, t], scalar=v("hgrn_norm", h),
                                                 in1=rr[:, t], op0=ALU.mult, op1=ALU.mult)
                    own.mark(m)
                own.wait()
                dve.tensor_tensor(mixT[:, 0:4].rearrange("p a n -> p (a n)"), oo,
                                  proj[:, 12:16].rearrange("p a n -> p (a n)"), ALU.mult
                                  ).then_inc(mix_ready, 8)

            def attention(kind):
                n0 = at0[kind]

                def maximum(i):
                    dve.wait_ge(at["scores"], n0 + i + 1)
                    step(dve.tensor_reduce(stat[:, 0, i:i + 1], ps[:, 4 + i % 2, 0:P * (i % 2 + 1)],
                                           AX.X, ALU.max))
                    dve.tensor_scalar(stat[:, 1, i:i + 1], stat[:, 0, i:i + 1], -scale_of[kind],
                                      None, ALU.mult).then_inc(at["max"], 1)

                maximum(0)
                for i in range(2 * HEADS):
                    if i + 1 < 2 * HEADS:
                        maximum(i + 1)
                    dve.wait_ge(at["exp"], n0 + i + 1)
                    step(dve.reciprocal(stat[:, 3, i:i + 1], stat[:, 2, i:i + 1]))
                    n = P * (i % 2 + 1)
                    dve.tensor_scalar(pbuf[i % 2][:, 0:n], pbuf[i % 2][:, 0:n], stat[:, 3, i:i + 1],
                                      None, ALU.mult).then_inc(at["prob"], 1)

            def fox():
                dve.wait_ge(at["logsig"], 1)
                step(dve.scalar_tensor_tensor(out=fz, in0=fz, scalar=0.0, in1=fa, op0=ALU.min,
                                              op1=ALU.subtract))
                one = cst[0:HEADS, CST["time"] + T // 2 + 1:CST["time"] + T // 2 + 2]
                dve.tensor_tensor_scan(cum, one.to_broadcast([HEADS, T]), fz, 0.0, ALU.mult, ALU.add
                                       ).then_inc(at["c"], 1)
                dve.wait_ge(at["c"], 1)
                dve.tensor_scalar(negc, cum, -1.0, None, ALU.mult).then_inc(at["c"], 1)
                attention("fox")

            def feed_forward(phase, conv):
                layer = {"ffn0": 0, "ffn1": 1}.get(phase, 0)

                def taps(k, f, half):
                    return vec[:, bass.ds(
                        VEC["ffn_conv_w"] + ((layer * 3 + k) * 2 + half) * FF_TILES + f, 1)]

                def convolve(j, f, half, buf, done, count):
                    p = pair(j, half)
                    dve.scalar_tensor_tensor(out=buf[:, 1:T], in0=p[:, 0:T - 1],
                                             scalar=taps(1, f, half), in1=buf[:, 1:T],
                                             op0=ALU.mult, op1=ALU.add).then_inc(conv_step, 1)
                    dve.wait_ge(conv_step, count)
                    dve.scalar_tensor_tensor(out=buf[:, 2:T], in0=p[:, 0:T - 2],
                                             scalar=taps(0, f, half), in1=buf[:, 2:T],
                                             op0=ALU.mult, op1=ALU.add).then_inc(done, 1)

                def hidden(j, f, cb):
                    n, g, u = f + FT0[phase], gbuf[j % 4], vbuf[j % 4]
                    if conv:
                        dve.wait_ge(gate_init, n + 1)
                        convolve(j, f, 0, g, gate_conv, 3 * n + 1)
                        dve.wait_ge(val_init, n + 1)
                        convolve(j, f, 1, u, conv_step, 3 * n + 2)
                        dve.wait_ge(conv_step, 3 * n + 3)
                    elif cb is not None:
                        dve.wait_ge(up_ready, 2 * n + 2)
                        dve.tensor_tensor(u, pair(j, 1), cb, ALU.mult).then_inc(conv_step, 1)
                        dve.wait_ge(conv_step, n - FT0["moe"] + (3 * FT0["ffn2"] + 1))
                    else:
                        dve.wait_ge(up_ready, 2 * n + 2)
                        u = pair(j, 1)
                    dve.wait_ge(gate_act, n + 1)
                    dve.tensor_tensor(hid[j % 4], g, u, ALU.mult).then_inc(hid_ready, 1)

                if phase == "moe":
                    with dve.Fori(0, EXPERTS) as e:
                        with dve.Fori(0, FE_TILES // 4) as i:
                            for j in range(4):
                                hidden(j, e * FE_TILES + i * 4 + j,
                                       mixT[:, bass.ds(e, 1), :].rearrange("p o n -> p (o n)"))
                    return
                with dve.Fori(0, FFN[phase] // 4) as i:
                    for j in range(4):
                        hidden(j, i * 4 + j, None)
                for f in range(FFN[phase] // 4 * 4, FFN[phase]):
                    hidden(f, f, None)

            def reduce_angle(dst, src, turns_):
                step(dve.tensor_scalar(turns_, src, INV_TURN, ROUND, ALU.mult, ALU.add))
                step(dve.tensor_scalar(turns_, turns_, -ROUND, None, ALU.add))
                step(dve.scalar_tensor_tensor(out=dst, in0=turns_, scalar=-TURN_A, in1=src,
                                              op0=ALU.mult, op1=ALU.add))
                for c in (TURN_B, TURN_C):
                    step(dve.scalar_tensor_tensor(out=dst, in0=turns_, scalar=-c, in1=dst,
                                                  op0=ALU.mult, op1=ALU.add))
                return dve.tensor_scalar(dst, dst, PI_SAFE, -PI_SAFE, ALU.min, ALU.max)

            def mla():
                pre_norm("m0", xT, hT, "mix_norm", 0)
                dve.tensor_copy(posf, pos_i[:, :]).then_inc(at["posrow"], 1)
                dve.memset(onesrow, 1.0).then_inc(at["posrow"], 1)
                pre_norm("mq", mraw, mnorm, "q_norm", 0)
                dve.wait_ge(at["poscol"], 1)
                step(dve.tensor_scalar(ang, acc(2), v("inv_freq", 0), None, ALU.mult))
                reduce_angle(red, ang, turns).then_inc(at["reduced"], 1)
                pre_norm("mkv", mraw[:, 3:5], mnorm[:, 3:5], "kv_norm", 0)
                dve.wait_ge(at["trig"], 2)
                for i in range(5):
                    dve.wait_ge(at["turned"], i + 1)
                    if i:
                        dve.wait_ge(at["roped"], i)
                    own.mark(dve.tensor_tensor(tmp[:, 0], qpe_raw[:, i] if i < 4 else mraw[:, 5], cos,
                                               ALU.mult))
                    step(dve.tensor_tensor(tmp[:, 1], work(i), sin, ALU.mult))
                    dve.tensor_tensor(proj[:, 16 + i] if i < 4 else kpe, tmp[:, 0], tmp[:, 1],
                                      ALU.add).then_inc(at["roped"], 1)
                attention("mla")
                for c in range(KD):
                    dve.wait_ge(tile_taken, TILE0["mla_o"] + c + 1)
                    dve.tensor_tensor(xT[:, c], xT[:, c], yT[:, c], ALU.add).then_inc(x_ready, 1)

            def add_accumulated(no):
                for c in range(KD):
                    dve.wait_ge(acc_ready, no * KD + c // 2 * 2 + 2)
                    dve.tensor_tensor(xT[:, c], xT[:, c], acc(c), ALU.add).then_inc(x_ready, 1)

            def s5_mixer():
                pre_norm("m2", xT, hT, "mix_norm", 8)
                lr, li = v("lam_re", 0, 32), v("lam_im", 0, 32)

                def p(n):
                    return s5p[:, n]

                dve.wait_ge(s5["dt"], 1)
                step(dve.tensor_tensor(p(LA), lr, p(DT), ALU.mult))
                step(dve.tensor_tensor(p(ANG), li, p(DT), ALU.mult))
                reduce_angle(p(RED), p(ANG), p(TRN)).then_inc(s5["angle"], 1)
                dve.wait_ge(s5["angle"], 1)
                own.mark(dve.tensor_scalar(p(PHI), p(RED), INV_TURN, None, ALU.mult))
                step(dve.tensor_tensor(p(DEN), lr, lr, ALU.mult))
                step(dve.tensor_tensor(p(S1), li, li, ALU.mult))
                step(dve.tensor_tensor(p(DEN), p(DEN), p(S1), ALU.add))
                step(dve.reciprocal(p(DEN), p(DEN)))
                dve.wait_ge(s5["mag"], 1)
                dve.wait_ge(s5["trig"], 2)
                step(dve.tensor_tensor(p(AR), p(MAG), p(COS), ALU.mult))
                step(dve.tensor_tensor(p(AI), p(MAG), p(SIN), ALU.mult))
                step(dve.tensor_scalar(p(AR), p(AR), -1.0, None, ALU.add))
                step(dve.tensor_tensor(p(GR), p(AR), lr, ALU.mult))
                step(dve.tensor_tensor(p(S1), p(AI), li, ALU.mult))
                step(dve.tensor_tensor(p(GR), p(GR), p(S1), ALU.add))
                step(dve.tensor_tensor(p(GI), p(AI), lr, ALU.mult))
                step(dve.tensor_tensor(p(S1), p(AR), li, ALU.mult))
                step(dve.tensor_tensor(p(GI), p(GI), p(S1), ALU.subtract))
                step(dve.tensor_tensor(p(GR), p(GR), p(DEN), ALU.mult))
                step(dve.tensor_tensor(p(GI), p(GI), p(DEN), ALU.mult))

                def spread(n):
                    return s5p[:, n, :, None].to_broadcast([P, S5_TILES, 32])

                def wide(t):
                    return t.rearrange("p a n -> p (a n)").rearrange("p (t c) -> p t c", c=32)

                dve.wait_ge(s5_loaded, 32)
                br, bi, t1, t2 = bexp[:, 0], bexp[:, 1], wide(sA), wide(sB)
                for r, (x, y, op) in enumerate(((br, bi, ALU.subtract), (bi, br, ALU.add))):
                    own.mark(dve.tensor_tensor(t1, x, spread(GR), ALU.mult))
                    step(dve.tensor_tensor(t2, y, spread(GI), ALU.mult))
                    dve.tensor_tensor(bbar[:, r], t1, t2, op).then_inc(s5["bbar"], 1)
                    dve.wait_ge(s5["bbar"], r + 1)

                for q in range(KD):
                    if q:
                        dve.wait_ge(s5["y"], q)
                    for j in range(4):
                        own.mark(dve.tensor_scalar(sv[:, j], time_row,
                                                   s5p[:, PHI, 4 * q + j:4 * q + j + 1], None,
                                                   ALU.mult))
                    own.wait()
                    step(dve.tensor_scalar(sk, sv, ROUND, -ROUND, ALU.add, ALU.add))
                    dve.tensor_tensor(sv, sv, sk, ALU.subtract).then_inc(s5["phase"], 1)
                    if q:
                        skip(q - 1)
                    dve.wait_ge(s5["sincos"], 2 * (q + 1))
                    dve.wait_ge(s5["bu"], q + 1)
                    ur, ui = ps[:, 4:8, 0:T], ps[:, 4:8, T:2 * T]

                    def flat(t):
                        return t.rearrange("p a n -> p (a n)")

                    own.mark(dve.tensor_tensor(sA, ur, scs, ALU.mult))
                    own.mark(dve.tensor_tensor(sB, ui, ss, ALU.mult))
                    own.mark(dve.tensor_tensor(sC, ui, scs, ALU.mult))
                    dve.tensor_tensor(sD, ur, ss, ALU.mult).then_inc(s5["rotated"], 1)
                    own.wait()
                    own.mark(dve.tensor_tensor(flat(sA), flat(sA), flat(sB), ALU.add))
                    dve.wait_ge(s5["rotated"], q + 1)
                    step(dve.tensor_tensor(flat(sC), flat(sC), flat(sD), ALU.subtract))
                    for src, dst in ((sA, sB), (sC, sD)):
                        for j in range(4):
                            own.mark(dve.tensor_tensor_scan(
                                dst[:, j], s5p[:, MAG, 4 * q + j:4 * q + j + 1].to_broadcast([P, T]),
                                src[:, j], 0.0, ALU.mult, ALU.add))
                    own.wait()
                    own.mark(dve.tensor_tensor(flat(sA), flat(sB), flat(scs), ALU.mult))
                    own.mark(dve.tensor_tensor(flat(sC), flat(sD), flat(ss), ALU.mult))
                    step(dve.tensor_tensor(flat(sv), flat(sB), flat(ss), ALU.mult))
                    own.mark(dve.tensor_tensor(flat(sA), flat(sA), flat(sC), ALU.subtract))
                    own.wait()
                    step(dve.scalar_tensor_tensor(out=flat(sC), in0=flat(sD), scalar=-1.0,
                                                  in1=flat(scs), op0=ALU.mult, op1=ALU.mult))
                    dve.tensor_tensor(flat(sC), flat(sC), flat(sv), ALU.subtract
                                      ).then_inc(s5["state"], 1)
                skip(KD - 1)
                for c in range(KD):
                    dve.wait_ge(tile_taken, TILE0["s5_glu"] + 2 * c + 2)
                    step(dve.tensor_tensor(mixT[:, c], mixT[:, c], sq[:, c], ALU.mult))
                    dve.tensor_tensor(xT[:, c], xT[:, c], mixT[:, c], ALU.add).then_inc(x_ready, 1)

            def skip(q):
                dve.wait_ge(s5["y"], q + 1)
                dve.scalar_tensor_tensor(out=sq[:, q], in0=proj[:, q], scalar=v("s5_d", q),
                                         in1=ps[:, q % 2, 0:T], op0=ALU.mult, op1=ALU.add
                                         ).then_inc(s5["ysum"], 1)

            def router():
                pre_norm("m3", xT, hT, "ffn_norm", 8)
                dve.wait_ge(rt["logits"], 2)
                for g in range(2):
                    step(dve.tensor_copy(tiny[:, LG0 + g, :], ps[:, 2, g * 8:g * 8 + 8]))
                    step(dve.max(tiny[:, MX0 + g, :], tiny[:, LG0 + g, :]))
                    step(dve.max_index(idx[:, g, :], tiny[:, MX0 + g, :], tiny[:, LG0 + g, :]))
                    own.mark(dve.tensor_copy(tiny[:, IX0 + g, :], idx[:, g, :]))
                    dve.tensor_tensor(tiny[:, GA, g:g + 1], tiny[:, MX0 + g, 1:2],
                                      tiny[:, MX0 + g, 0:1], ALU.subtract).then_inc(rt["diff"], 1)
                dve.wait_ge(rt["exp"], 1)
                step(dve.tensor_scalar(tiny[:, GB, 0:2], tiny[:, GA, 0:2], 1.0, None, ALU.add))
                step(dve.reciprocal(tiny[:, GB, 0:2], tiny[:, GB, 0:2]))
                step(dve.tensor_tensor(tiny[:, GA, 0:2], tiny[:, GA, 0:2], tiny[:, GB, 0:2],
                                       ALU.mult))
                for g in range(2):
                    own.mark(dve.tensor_scalar(tiny[:, LG0 + g, :], iota8, tiny[:, IX0 + g, 0:1],
                                               tiny[:, GB, g:g + 1], ALU.is_equal, ALU.mult))
                    step(dve.tensor_scalar(tiny[:, MX0 + g, :], iota8, tiny[:, IX0 + g, 1:2],
                                           tiny[:, GA, g:g + 1], ALU.is_equal, ALU.mult))
                    dve.tensor_tensor(tiny[:, CB0 + g, :], tiny[:, LG0 + g, :], tiny[:, MX0 + g, :],
                                      ALU.add).then_inc(rt["comb"], 1)
                    own.mark(dve.tensor_scalar(sel[:, g], iota8, tiny[:, IX0 + g, 0:1], None,
                                               ALU.is_equal))
                    step(dve.tensor_scalar(tiny[:, LD0 + g, :], iota8, tiny[:, IX0 + g, 1:2], None,
                                           ALU.is_equal))
                    dve.tensor_tensor(sel[:, g], sel[:, g], tiny[:, LD0 + g, :], ALU.add
                                      ).then_inc(mo["sel"], 1)
                step(dve.memset(posm, -1.0))
                dve.wait_ge(mo["sel"], 2)
                dve.wait_ge(mo["pos"], 1)
                for g in range(2):
                    step(dve.scalar_tensor_tensor(out=posm[:, g, 0:8], in0=ps[:, 3, g * 8:g * 8 + 8],
                                                  scalar=1.0, in1=sel[:, g], op0=ALU.add,
                                                  op1=ALU.mult))
                    dve.tensor_scalar(posm[:, g, 0:8], posm[:, g, 0:8], -1.0, None, ALU.add
                                      ).then_inc(mo["posm"], 1)
                step(dve.tensor_reduce(tiny[:, LMAX, 0:1], ps[:, 3, 16:24], AX.X, ALU.max))
                dve.tensor_scalar(crowded[:, :], tiny[:, LMAX, 0:1], float(CAP), None, ALU.is_gt
                                  ).then_inc(mo["flag"], 1)
                dve.wait_ge(mo["posm"], 2)
                dve.wait_ge(rt["taken"], 8)

            def experts_gathered():
                count = cst[:, CST["time"] + T // 2:CST["time"] + T // 2 + CAP]

                def picks(e):
                    for g in range(2):
                        col = posm[:, g, bass.ds(e, 1)]
                        dve.tensor_scalar(pick[:, g], count, col, None, ALU.is_equal
                                          ).then_inc(mo["pick"], 1)

                picks(0)
                with dve.Fori(0, EXPERTS) as e:
                    dve.wait_ge(mo["xready"], 2 * e + 2)
                    picks(e + 1)
                    if_e = yT[0:CAP, bass.ds(e, 1), :].rearrange("p o n -> p (o n)")
                    cb_e = mixT[0:CAP, bass.ds(e, 1), :].rearrange("p o n -> p (o n)")
                    dve.scalar_tensor_tensor(out=place, in0=if_e, scalar=partition[0:CAP], in1=cb_e,
                                             op0=ALU.is_equal, op1=ALU.mult).then_inc(mo["place"], 1)
                    with dve.Fori(0, FE_TILES // 4) as i:
                        for j in range(4):
                            n = e * FE_TILES + i * 4 + (FT0["moe"] + j)
                            dve.wait_ge(up_ready, 2 * n + 2)
                            dve.wait_ge(gate_act, n + 1)
                            dve.tensor_tensor(hid[j][:, 0:CAP], gbuf[j][:, 0:CAP],
                                              pair(j, 1)[:, 0:CAP], ALU.mult).then_inc(hid_ready, 1)
                    for d in range(KD):
                        dve.wait_ge(mo["spread"], e * KD + (d + 1))
                        dve.tensor_tensor(xT[:, d], xT[:, d], ps[:, 2 + d % 2, 0:T], ALU.add
                                          ).then_inc(mo["added"], 1)
                dve.wait_ge(mo["added"], 2 + EXPERTS * KD)
                dve.sem_inc(x_ready, KD)

            def experts():
                dve.sem_inc(mo["added"], 2)
                with dve.If(dve.value_load(crowded[0:1, 0:1], min_val=0, max_val=1) == 1):
                    feed_forward("moe", False)
                    add_accumulated(3)
                with dve.Else():
                    experts_gathered()

            dve.wait_ge(small_loaded, 16 * 6)
            own.mark(dve.tensor_tensor(tiny[:, LMAX, 0:4], v("lb_logits", 0, 4), v("lb_logits", 4, 4),
                                       ALU.max))
            own.wait()
            step(dve.tensor_tensor(tiny[:, LMAX, 0:4], tiny[:, LMAX, 0:4], v("lb_logits", 8, 4),
                                   ALU.max))
            for r in range(3):
                dve.tensor_tensor(tiny[:, LD0 + r, 0:4], v("lb_logits", 4 * r, 4),
                                  tiny[:, LMAX, 0:4], ALU.subtract).then_inc(hg["lbdiff"], 1)
            dve.wait_ge(hg["lbexp"], 1)
            step(dve.tensor_tensor(tiny[:, LSUM, 0:4], tiny[:, LD0, 0:4], tiny[:, LD1, 0:4], ALU.add))
            step(dve.tensor_tensor(tiny[:, LSUM, 0:4], tiny[:, LSUM, 0:4], tiny[:, LD2, 0:4],
                                   ALU.add))
            step(dve.reciprocal(tiny[:, LREC, 0:4], tiny[:, LSUM, 0:4]))
            step(dve.tensor_tensor(tiny[:, LB, 0:4], tiny[:, LD0, 0:4], tiny[:, LREC, 0:4], ALU.mult))
            step(dve.tensor_scalar(tiny[:, OML, 0:4], tiny[:, LB, 0:4], -1.0, 1.0, ALU.mult, ALU.add))
            step(dve.tensor_scalar(tiny[:, SPM, 0:4], v("rg_lambda", 0, 4), -1.0, 0.0, ALU.mult,
                                   ALU.max))
            dve.wait_ge(rg["softplus"], 1)
            step(dve.tensor_tensor(tiny[:, SPM, 0:4], tiny[:, SPM, 0:4], tiny[:, SPL, 0:4], ALU.add))
            dve.tensor_scalar(tiny[:, SP4, 0:4], tiny[:, SPM, 0:4], RG_C / 2, None, ALU.mult
                              ).then_inc(rg["rate"], 1)
            dve.tensor_scalar(tiny[:, SP8, 0:4], tiny[:, SPM, 0:4], -RG_C, None, ALU.mult
                              ).then_inc(rg["rate"], 1)
            for c in range(KD):
                dve.wait_ge(x_turned, c // 2 * 2 + 2)
                dve.tensor_copy(xT[:, c], acc(c)).then_inc(x_ready, 1)
            pre_norm("n0", xT, hT, "norm_gains", 0)
            dve.wait_ge(cleared, 2)
            hgrn_rglru()
            post_norm("n1", 8)
            pre_norm("n2", xT, hT, "norm_gains", 16)
            feed_forward("ffn0", True)
            post_norm("n3", 24)
            pre_norm("n4", xT, hT, "norm_gains", 32)
            fox()
            post_norm("n5", 40)
            pre_norm("n6", xT, hT, "norm_gains", 48)
            feed_forward("ffn1", True)
            post_norm("n7", 56)
            mla()
            pre_norm("m1", xT, hT, "ffn_norm", 0)
            feed_forward("ffn2", False)
            add_accumulated(2)
            s5_mixer()
            router()
            dve.wait_ge(mo["flag"], 1)
            experts()
            pre_norm("mf", xT, hT, "final_norm", 0)


def weight_tiles(w):
    k, n = w.shape
    return w.reshape(k // P, P, n // P, P).transpose(1, 2, 0, 3)


def linear_units(w, sizes):
    flat = weight_tiles(w).reshape(P, -1)
    out, at = np.zeros((len(sizes), P, max(sizes)), w.dtype), 0
    for i, n in enumerate(sizes):
        out[i, :, :n] = flat[:, at:at + n]
        at += n
    return out


def ffn_units(gate, up, down):
    n = gate.shape[1] // (FT_UNIT * P)
    out = np.empty((n, P, 3, FT_UNIT * KD * P), gate.dtype)
    for k, w in enumerate((gate, up)):
        out[:, :, k] = w.reshape(KD, P, n, FT_UNIT, P).transpose(2, 1, 3, 0, 4).reshape(n, P, -1)
    out[:, :, 2] = down.reshape(n, FT_UNIT, P, D).transpose(0, 2, 1, 3).reshape(n, P, -1)
    return out.reshape(n, P, SLOT)


def columns(x):
    return x.reshape(-1, P).T


def layouts(i):
    f = {}
    f["x"] = i["x"].reshape(2, P, D)
    f["w_even_in"] = linear_units(i["even_w_in"][0], phase_units("even_in"))
    f["w_even_out"] = linear_units(i["even_w_out"][0], phase_units("even_out"))
    odd = i["odd_w_in"][0]
    f["w_odd_qk"] = linear_units(odd[:, :2 * D], phase_units("odd_qk"))
    f["w_odd_v"] = odd[:, 2 * D:3 * D].reshape(KD, P, 2, 512).transpose(2, 1, 0, 3).reshape(2, P, -1)
    f["wf"] = odd[:, 3 * D:].reshape(KD, P, HEADS).transpose(1, 0, 2)
    f["w_odd_out"] = linear_units(i["odd_w_out"][0], phase_units("odd_out"))
    for l in range(2):
        up = i["ffn_w_up"][l]
        f[f"w_ffn{l}"] = ffn_units(up[:, :FF], up[:, FF:], i["ffn_w_down"][l])
    f["w_ffn2"] = ffn_units(i["ffn_w_gate_2"][0], i["ffn_w_up_2"][0], i["ffn_w_down_2"][0])
    w = i["mla_w_in_2"][0]
    n = Q_LORA + KV_LORA
    f["w_mla_in"] = linear_units(np.concatenate([w[:, :n]] + [w[:, n:]] * 4, 1),
                                 phase_units("mla_in"))
    w = i["mla_w_uq_2"][0].reshape(Q_LORA, HEADS, HD + ROPE)
    f["w_mla_uq"] = linear_units(np.concatenate(
        [w[:, :, :HD].reshape(Q_LORA, -1), w[:, :, HD:].reshape(Q_LORA, -1)], 1),
        phase_units("mla_uq"))
    w = i["mla_w_ukv_2"][0].reshape(KV_LORA, HEADS, 2 * HD)
    f["w_mla_uk"] = linear_units(w[:, :, :HD].reshape(KV_LORA, D), phase_units("mla_uk"))
    f["w_mla_uv"] = w[:, :, HD:].reshape(2, P, D).transpose(1, 0, 2).reshape(1, P, -1)
    f["w_mla_o"] = linear_units(i["mla_w_o_2"][0], phase_units("mla_o"))
    f["w_s5_in"] = linear_units(i["s5_w_in_2"][0], phase_units("s5_in"))
    w = i["s5_w_glu_2"][0].reshape(D, 2, KD, P).transpose(0, 2, 1, 3).reshape(D, 2 * D)
    f["w_s5_glu"] = linear_units(w, phase_units("s5_glu"))
    w = np.empty((EXPERTS, FE_TILES, P, 3, KD, P), np.float32)
    for k, name in enumerate(("moe_w_gate_2", "moe_w_up_2")):
        w[:, :, :, k] = i[name][0].reshape(EXPERTS, KD, P, FE_TILES, P).transpose(0, 3, 2, 1, 4)
    w[:, :, :, 2] = i["moe_w_down_2"][0].reshape(EXPERTS, FE_TILES, P, KD, P)
    f["w_moe"] = w.reshape(EXPERTS * FE_TILES, P, HALF)
    f["wr"] = i["moe_w_router_2"][0].reshape(KD, P, EXPERTS).transpose(1, 0, 2)
    blocks = np.zeros((2, RG_TILES, 2, 64, 2, 64), np.float32)
    for k, name in enumerate(("rg_wa", "rg_wx")):
        for h in range(2):
            blocks[k, :, h, :, h, :] = i[name][0].reshape(RG_TILES, 2, 64, 64)[:, h]
    f["rgw"] = blocks.reshape(2, RG_TILES, P, P).transpose(2, 0, 1, 3)
    f["positions"] = i["positions_2"].reshape(1, T)
    b = np.zeros((2, 2, 64, S5_TILES, 2, 16), np.float32)
    c = np.zeros((2, 2, 64, KD, 4, 2, 16), np.float32)
    for r, (nb, ncc) in enumerate((("s5_b_re_2", "s5_c_re_2"), ("s5_b_im_2", "s5_c_im_2"))):
        for h in range(2):
            b[r, h, :, :, h, :] = i[nb][0].reshape(S5_TILES, 2, 64, 16)[:, h].transpose(1, 0, 2)
            c[r, h, :, :, :, h, :] = i[ncc][0].reshape(KD, 4, 2, 16, 64)[:, :, h].transpose(3, 0, 1, 2)
    f["s5_b"] = b.reshape(2, P, S5_TILES, 32).transpose(1, 0, 2, 3)
    f["s5_cT"] = c.reshape(2, P, KD, P).transpose(1, 0, 2, 3)
    v = np.zeros((P, N_VEC), np.float32)
    for name, x in (("norm_gains", i["norm_gains"]), ("lb_logits", i["hgrn_lb_logits"]),
                    ("hgrn_norm", i["hgrn_norm"]), ("rg_conv_w", i["rg_conv_w"]),
                    ("rg_conv_b", i["rg_conv_b"]), ("rg_ba", i["rg_ba"]), ("rg_bx", i["rg_bx"]),
                    ("rg_lambda", i["rg_lambda"]), ("ffn_conv_w", i["ffn_conv_w"]),
                    ("ffn_conv_b", i["ffn_conv_b"]), ("mix_norm", i["mix_norm_2"]),
                    ("ffn_norm", i["ffn_norm_2"]), ("final_norm", i["final_norm_2"]),
                    ("q_norm", i["mla_q_norm_2"]), ("kv_norm", i["mla_kv_norm_2"]),
                    ("s5_d", i["s5_d_2"]), ("lam_re", i["s5_lambda_re_2"]),
                    ("lam_im", i["s5_lambda_im_2"]),
                    ("log_dt", np.repeat(i["s5_log_dt_2"].reshape(-1), 64))):
        x = columns(x)
        v[:, VEC[name]:VEC[name] + x.shape[1]] = x
    freq = (10000.0 ** (-np.arange(0, ROPE, 2, dtype=np.float32) / ROPE)).astype(np.float32)
    v[:, VEC["inv_freq"]] = np.tile(freq, P // 16)
    v[:HEADS, VEC["fox_bias"]] = i["fox_f_bias"].reshape(-1)
    f["vec"] = v
    k = np.zeros((P, N_CST), np.float32)
    row = np.arange(P)
    k[:, CST["ident"]:][:, :P] = np.eye(P)
    k[:, CST["mask"]:][:, :P] = np.where(row[None, :] > row[:, None], NEG, 0.0)
    m = row % ROPE < ROPE // 2
    k[(row + 16)[m], CST["rot"] + row[m]] = -1.0
    k[(row - 16)[~m], CST["rot"] + row[~m]] = 1.0
    k[:, CST["chunk"]:][:, :T] = np.arange(T) % CHUNK != 0
    k[:, CST["time"]:][:, :T] = np.arange(T) - T // 2
    k[:, CST["before"]:][:, :P] = row[:, None] < row[None, :]
    k[:, CST["part"]] = row
    k[:, CST["iota8"]:][:, :8] = np.arange(8)
    f["cst"] = k
    return {n: np.ascontiguousarray(x) for n, x in f.items()}


def kernel(**inputs):
    import concourse.bacc as _bacc
    from concourse import mybir as _mybir
    from concourse.bass_utils import run_bass_kernel_spmd as _run

    nc = _bacc.Bacc("TRN2", target_bir_lowering=False, num_devices=1,
                    dynamic_dma_scratch_size=1024)
    arrays = layouts({n: np.asarray(x) for n, x in inputs.items()})
    tensors = {n: nc.dram_tensor("in_" + n, x.shape, _mybir.dt.from_np(x.dtype),
                                 kind="ExternalInput").ap() for n, x in arrays.items()}
    tensors["out"] = nc.dram_tensor("out", (2, P, D), F32, kind="ExternalOutput").ap()
    build_program(nc, tensors)
    r = _run(nc, [{"in_" + n: x for n, x in arrays.items()}], core_ids=[0])
    return r.results[0]["out"].reshape(1, T, D)
```

```python
from contextlib import ExitStack

import numpy as np

import concourse.bass as bass
from concourse import mybir

P = 128
T = 256
D = 1024
KD = D // P
HEADS = 16
HD = D // HEADS
ROPE = 32
EPS = 1e-6
NEG = -1e30

A_HEADS = 4
CHUNK = 64
NCHUNK = T // CHUNK
RG_C = 8.0
RG_TILES = 4
FF = 2816
FF_TILES = FF // P
EXPERTS = 8
FE = 3584
FE_TILES = FE // P
Q_LORA, KV_LORA = 384, 256
S5_TILES = 32

SLOTS = 4
SLOT = 6144
UNIT_TILES = 6
WORK = 4
HALF = SLOT // 2
HALVES = 7
SPREAD_STEPS = 4
CAP = 96
FT_UNIT = 2

F32 = mybir.dt.float32
ALU = mybir.AluOpType
ACT = mybir.ActivationFunctionType
AX = mybir.AxisListType

TURN_A = 6.28125
TURN_B = float(np.float32(np.floor((2 * np.pi - TURN_A) * 2.0**21) / 2.0**21))
TURN_C = float(np.float32(2 * np.pi - TURN_A - TURN_B))
INV_TURN = float(np.float32(1 / (2 * np.pi)))
ROUND = 12582912.0
PI_SAFE = 3.1415925
TWO_PI_SAFE = 6.283185

LINEAR = {
    "even_in": (24, 8), "even_out": (8, 8), "odd_qk": (16, 8), "odd_out": (8, 8),
    "mla_in": (6, 8), "mla_uq": (12, 3), "mla_uk": (8, 2), "mla_o": (8, 8),
    "s5_in": (8, 8), "s5_glu": (16, 8),
}
LINEAR_ORDER = list(LINEAR)


def phase_units(name):
    if name in LINEAR:
        tiles, k = LINEAR[name]
        per = UNIT_TILES if k == KD else tiles
        return [min(per, tiles - t) * k * P for t in range(0, tiles, per)]
    if name == "odd_v":
        return [KD * 512] * 2
    if name == "mla_uv":
        return [2 * D]
    return [SLOT] * (FF_TILES // FT_UNIT)


STREAM = ["even_in", "even_out", "ffn0", "odd_qk", "odd_v", "odd_out", "ffn1", "mla_in", "mla_uq",
          "mla_uk", "mla_uv", "mla_o", "ffn2", "s5_in", "s5_glu"]
UNIT0, LOADED, _n = {}, [], [0] * SLOTS
for _name in STREAM:
    UNIT0[_name] = len(LOADED)
    for _ in phase_units(_name):
        _s = len(LOADED) % SLOTS
        _n[_s] += 16
        LOADED.append(_n[_s])
TILE0, _t = {}, 0
for _name in LINEAR_ORDER:
    TILE0[_name] = _t
    _t += LINEAR[_name][0]
FFN = {"ffn0": FF_TILES, "ffn1": FF_TILES, "ffn2": FF_TILES, "moe": EXPERTS * FE_TILES}
FT0, _t = {}, 0
for _name, _c in FFN.items():
    FT0[_name] = _t
    _t += _c

NORMS = [("n0", 8), ("n1", 8), ("n2", 8), ("n3", 8), ("n4", 8), ("n5", 8), ("n6", 8), ("n7", 8),
         ("m0", 8), ("mq", 3), ("mkv", 2), ("m1", 8), ("m2", 8), ("m3", 8), ("mf", 8)]
NORM_NO = {n: i for i, (n, _) in enumerate(NORMS)}
SQ0, _t = {}, 0
for _name, _c in NORMS:
    SQ0[_name] = _t
    _t += _c
X_VERSION = {"n0": 1, "n2": 2, "n4": 3, "n6": 4, "m0": 5, "m1": 6, "m2": 7, "m3": 8, "mf": 9}

VEC = {}
_t = 0
for _name, _c in [("norm_gains", 64), ("lb_logits", 12), ("hgrn_norm", 4), ("rg_conv_w", 16),
                  ("rg_conv_b", 4), ("rg_ba", 4), ("rg_bx", 4), ("rg_lambda", 4),
                  ("ffn_conv_w", 2 * 3 * 2 * FF_TILES), ("ffn_conv_b", 2 * 2 * FF_TILES),
                  ("mix_norm", 16), ("ffn_norm", 16), ("final_norm", 8), ("q_norm", 3),
                  ("kv_norm", 2), ("s5_d", 8), ("lam_re", 32), ("lam_im", 32), ("log_dt", 32),
                  ("inv_freq", 1), ("fox_bias", 1)]:
    VEC[_name] = _t
    _t += _c
N_VEC = _t

CST = {}
_t = 0
for _name, _c in [("ident", P), ("mask", P), ("rot", P), ("chunk", T), ("time", T), ("iota8", 8), ("before", P)]:
    CST[_name] = _t
    _t += _c
N_CST = _t


class Order:

    def __init__(self, eng, sem):
        self.eng, self.sem, self.n = eng, sem, 0

    def mark(self, instruction):
        instruction.then_inc(self.sem, 1)
        self.n += 1
        return self.n

    def wait(self, n=None):
        self.eng.wait_ge(self.sem, self.n if n is None else n)


def build_program(nc, a):
    ctx = ExitStack()
    with ctx:
        def sb(name, shape, dt=F32):
            return ctx.enter_context(nc.sbuf_tensor(name, shape, dt))

        def sem(name):
            return ctx.enter_context(nc.semaphore(name))

        slots = [sb(f"slot{i}", [P, SLOT]) for i in range(SLOTS)]
        xT = sb("xT", [P, KD, T])
        hT = sb("hT", [P, KD, T])
        sq = sb("sq", [P, KD, T])
        yT = sb("yT", [P, KD, T])
        mixT = sb("mixT", [P, KD, T])
        proj = sb("proj", [P, 20, T])
        vtok = sb("vtok", [P, 2, D])
        scr = sb("scr", [P, 38 * T])
        xbp = sb("xbp", [P, RG_TILES, T + 3])
        rgw = sb("rgw", [P, 2, RG_TILES, P])
        vec = sb("vec", [P, N_VEC])
        cst = sb("cst", [P, N_CST])
        wf = sb("wf", [P, KD, HEADS])
        wr = sb("wr", [P, KD, EXPERTS])
        ones = sb("ones", [P, P])
        rms = sb("rms", [P, T])
        rstd = sb("rstd", [P, T])
        stat = sb("stat", [P, 4, 2 * HEADS])
        tiny = sb("tiny", [P, 24, 8])
        idx = sb("idx", [P, 2, 8], mybir.dt.uint32)
        crowded = sb("crowded", [P, 1], mybir.dt.int32)
        pos_i = sb("pos_i", [1, T], mybir.dt.int32)

        ident = cst[:, CST["ident"]:CST["ident"] + P]
        mask = cst[:, CST["mask"]:CST["mask"] + P]
        rot = cst[:, CST["rot"]:CST["rot"] + P]
        chunk_mask = cst[:, CST["chunk"]:CST["chunk"] + T]
        time_row = cst[:, CST["time"]:CST["time"] + T]
        before = cst[:, CST["before"]:CST["before"] + P]
        iota8 = cst[:, CST["iota8"]:CST["iota8"] + 8]

        def v(name, i, n=1):
            return vec[:, VEC[name] + i:VEC[name] + i + n]

        def part(start, tiles=1):
            return scr[:, start * T:(start + tiles) * T]

        ps = ctx.enter_context(nc.psum_tensor("ps", [P, 8, 512], F32))

        def acc(i):
            return ps[:, i // 2, (i % 2) * T:(i % 2) * T + T]

        def work(i):
            return ps[:, 4 + i % WORK, 0:T]

        def sum_of(name):
            return ps[:, 4, 0:T] if name in ("n3", "n7") else acc(0)

        def pair(f, k):
            return ps[:, 4 + f % 2 * 2 + k, 0:T]

        small_loaded = sem("small_loaded")
        x_loaded = sem("x_loaded")
        s5_loaded = sem("s5_loaded")
        slot_loaded = [sem(f"slot_loaded{i}") for i in range(SLOTS)]
        slot_free = sem("slot_free")
        cleared = sem("cleared")
        x_turned = sem("x_turned")
        x_ready = sem("x_ready")
        h_ready = sem("h_ready")
        sq_ready = sem("sq_ready")
        sum_ready = sem("sum_ready")
        rms_ready = sem("rms_ready")
        rstd_ready = sem("rstd_ready")
        tile_ready = sem("tile_ready")
        tile_taken = sem("tile_taken")
        up_ready = sem("up_ready")
        gate_init = sem("gate_init")
        gate_conv = sem("gate_conv")
        gate_act = sem("gate_act")
        val_init = sem("val_init")
        conv_step = sem("conv_step")
        hid_ready = sem("hid_ready")
        acc_ready = sem("acc_ready")
        mix_ready = sem("mix_ready")
        act_own, dve_own = sem("act_own"), sem("dve_own")
        hg = {n: sem("hg_" + n) for n in (
            "forget", "logf", "bcum", "decay", "exps", "gated", "vturned", "vtaken", "scores",
            "scopied", "masked", "kturned", "ktaken", "upd", "state", "out", "outtaken", "total",
            "root", "lbdiff", "lbexp")}
        rg = {n: sem("rg_" + n) for n in (
            "softplus", "rate", "conv", "product", "gates", "decay", "square", "root")}
        at = {n: sem("at_" + n) for n in (
            "flog", "fbias", "logsig", "c", "vtile", "vtaken", "scores", "max", "exp", "prob",
            "pturned", "ptaken", "out", "posrow", "poscol", "reduced", "trig", "turned", "roped")}
        s5 = {n: sem("s5_" + n) for n in (
            "dt", "angle", "mag", "trig", "bbar", "bturned", "btaken", "steps", "turns", "phase", "sincos",
            "bu", "rotated", "turned", "sums", "state", "y", "ysum", "z")}
        rt = {n: sem("rt_" + n) for n in (
            "logits", "diff", "exp", "comb", "spread", "taken")}
        moe_loaded = [sem(f"moe_loaded{i}") for i in range(HALVES)]
        moe_free = sem("moe_free")
        mo = {n: sem("mo_" + n) for n in (
            "sel", "pos", "posm", "flag", "hturned", "htaken", "pick", "gathered", "xready", "place",
            "ye", "yetaken", "spread", "added", "weighted", "pturned")}
        out_turned, out_taken, out_stored = sem("out_turned"), sem("out_taken"), sem("out_stored")

        kh, lf, bc, eb, en, ed = (part(4 * i, 4) for i in range(6))
        qd, kd, ku, oo, rr = lf, en, ed, kh, bc
        st = part(24, 6)
        vt = vtok[0:CHUNK].rearrange("p a (b n) -> p (a b) n", n=P)
        kt = yT[0:CHUNK].rearrange("p a (b n) -> p (a b) n", n=P)
        sc = hT[0:CHUNK, 0:4].rearrange("p a n -> p (a n)")
        xc = part(30, 4).rearrange("p (a n) -> p a n", a=4)
        rm = part(34, 4).rearrange("p (a n) -> p a n", a=4)
        ra, gr_, gi_ = hT[:, 4:8], mixT[:, 4:8], sq[:, 4:8]
        gbuf, vbuf, hid = ([part(4 * k + i) for i in range(4)] for k in range(3))
        cum, negc, fz, fa = (scr[0:HEADS, i * T:(i + 1) * T] for i in range(4))
        mraw = part(0, 6).rearrange("p (a n) -> p a n", a=6)
        mnorm = part(6, 5).rearrange("p (a n) -> p a n", a=5)
        qpe_raw = part(12, 4).rearrange("p (a n) -> p a n", a=4)
        kpe, cos, sin, ang, turns, red, mag_ = (part(16 + i) for i in range(7))
        posf = scr[0:1, 24 * T:25 * T]
        onesrow = scr[0:1, 25 * T:25 * T + P]
        tmp = part(30, 2).rearrange("p (a n) -> p a n", a=2)
        pbuf = [part(26), part(27)]
        pTs = [part(28), part(29)]
        fours = [part(4 * i, 4).rearrange("p (a n) -> p a n", a=4) for i in range(8)]
        sv = fours[0]
        ss, scs, sA, sB, sC, sD = zip(fours[1:7], (
            fours[7], proj[:, 16:20], mixT[:, 0:4], mixT[:, 4:8], proj[:, 8:12], proj[:, 12:16]))
        xg = part(12, 3).rearrange("p (a n) -> p a n", a=KD)
        ye = part(18, 4)[0:CAP]
        pick = part(22)[:, 0:2 * CAP].rearrange("p (g n) -> p g n", g=2)
        weighted = part(17)[:, 0:2 * CAP].rearrange("p (g n) -> p g n", g=2)
        place = part(23)[0:CAP]
        posm = part(24)[:, 0:2 * 8].rearrange("p (g n) -> p g n", g=2)
        sel = part(25)[:, 0:2 * 8].rearrange("p (g n) -> p g n", g=2)
        s5p = part(34, 2).rearrange("p (a n) -> p a n", a=16)
        bexp = mixT[:].rearrange("p a n -> p (a n)").rearrange("p (r t c) -> p r t c", r=2, t=S5_TILES)
        bbar = proj[:, 8:16].rearrange("p a n -> p (a n)").rearrange("p (r t c) -> p r t c", r=2,
                                                                   t=S5_TILES)
        bT = vtok[:].rearrange("p r (q n) -> p r q n", n=P)
        cT = yT[:].rearrange("p a n -> p (a n)").rearrange("p (r q n) -> p r q n", r=2, q=KD)
        DT, LA, ANG, TRN, RED, MAG, SIN, ABS, COS, AR, AI, DEN, GR, GI, PHI, S1 = range(16)
        (LMAX, LD0, LD1, LD2, LSUM, LREC, LB, OML, SPA, SPE, SPL, SPM, SP4, SP8, LG0, LG1, MX0, MX1,
         IX0, IX1, CB0, CB1, GA, GB) = range(24)

        scale_of = {"fox": 1.0, "mla": float(np.float32((HD + ROPE) ** -0.5))}
        at0 = {"fox": 0, "mla": 2 * HEADS}
        mix0 = {"even_out": 0, "odd_out": KD, "mla_o": 2 * KD}

        block = ctx.enter_context(nc.Block())

        @block.sync
        def _(sp):
            sp.dma_start(proj[:, 0:8].rearrange("p a n -> p (a n)").rearrange(
                "p (g d) -> p g d", g=2), a["x"].rearrange("g p d -> p g d")).then_inc(x_loaded, 16)
            for dst, name in ((cst[:, :], "cst"), (vec[:, :], "vec"), (wf[:, :, :], "wf"),
                              (wr[:, :, :], "wr"), (rgw[:, :, :, :], "rgw"),
                              (pos_i[:, :], "positions")):
                sp.dma_start(dst, a[name]).then_inc(small_loaded, 16)
            for name in STREAM:
                sizes, u0, w = phase_units(name), UNIT0[name], a["w_" + name]

                def load(u, unit, name=name, sizes=sizes, w=w, u0=u0):
                    sp.wait_ge(slot_free, unit + u0 + 1)
                    sp.dma_start(slots[(u0 + u) % SLOTS][:, 0:sizes[u]],
                                 w[bass.ds(unit, 1), :, 0:sizes[u]].rearrange("o p n -> p (o n)")
                                 ).then_inc(slot_loaded[(u0 + u) % SLOTS], 16)

                fours = len(sizes) // SLOTS if name in FFN else 0
                if fours:
                    with sp.Fori(0, fours) as i:
                        for u in range(SLOTS):
                            load(u, i * SLOTS + u)
                for u in range(fours * SLOTS, len(sizes)):
                    load(u, u)
                if name == "ffn2":
                    sp.wait_ge(x_ready, 6 * KD)
                    sp.dma_start(cT, a["s5_cT"]).then_inc(s5_loaded, 16)
                    sp.dma_start(bexp, a["s5_b"]).then_inc(s5_loaded, 16)
            def load_half(h, unit):
                sp.dma_start(slots[h // 2][:, h % 2 * HALF:(h % 2 + 1) * HALF],
                             a["w_moe"][bass.ds(unit, 1)].rearrange("o p n -> p (o n)")
                             ).then_inc(moe_loaded[h], 16)

            for h in range(HALVES):
                sp.wait_ge(slot_free, SLOTS + max(n for n in range(len(LOADED))
                                                  if n % SLOTS == h // 2) + 1)
                load_half(h, h)
            with sp.Fori(1, EXPERTS * FE_TILES // HALVES) as i:
                for h in range(HALVES):
                    sp.wait_ge(moe_free, i * HALVES + h + 1)
                    load_half(h, i * HALVES + h)
            for g in range(2):
                sp.wait_ge(out_taken, 2 * (g + 1))
                sp.dma_start(a["out"][g], proj[:, 0:8].rearrange("p a n -> p (a n)")[
                    :, g * D:(g + 1) * D]).then_inc(out_stored, 16)
            sp.wait_ge(out_stored, 32)

        @block.gpsimd
        def _(pool):
            pool.memset(ones[:, :], 1.0).then_inc(cleared, 1)
            pool.memset(xbp[:, :, 0:3], 0.0).then_inc(cleared, 1)
            pool.wait_ge(hg["scopied"], 2)
            pool.affine_select(out=sc, in_=sc, pattern=[[0, 16], [1, CHUNK]], base=0,
                               channel_multiplier=-1, compare_op=ALU.is_ge, fill=0.0
                               ).then_inc(hg["masked"], 1)

            def phase(q):
                if q >= 2:
                    pool.wait_ge(s5["state"], q - 1)
                pool.wait_ge(s5["steps"], 4 * (q + 1))
                pool.tensor_scalar(ss[q % 2], sv, ROUND, -ROUND, ALU.add, ALU.add
                                   ).then_inc(s5["turns"], 1)
                pool.wait_ge(s5["turns"], q + 1)
                pool.tensor_tensor(sv, sv, ss[q % 2], ALU.subtract).then_inc(s5["phase"], 1)

            def difference(q):
                pool.wait_ge(s5["turned"], q + 1)
                pool.tensor_tensor(sC[q % 2], sC[q % 2], sD[q % 2], ALU.subtract
                                   ).then_inc(s5["sums"], 1)

            phase(0)
            for q in range(KD):
                difference(q)
                if q + 1 < KD:
                    phase(q + 1)

        @block.scalar
        def _(act):
            own = Order(act, act_own)
            def squares(name, src, ready, first, at_=0):
                for c in range(dict(NORMS)[name]):
                    act.wait_ge(ready, first + c + 1)
                    act.activation(sq[:, at_ + c], src[:, c], ACT.Square).then_inc(sq_ready, 1)

            def root(name):
                n = NORM_NO[name]
                act.wait_ge(sum_ready, n + 1)
                if n:
                    act.wait_ge(rstd_ready, n)
                act.activation(rms[:, :], sum_of(name), ACT.Sqrt, bias=EPS,
                               scale=1.0 / (P * dict(NORMS)[name])).then_inc(rms_ready, 1)

            def pre_norm(name):
                squares(name, xT, x_ready, (X_VERSION[name] - 1) * KD)
                root(name)

            def take(phase, i, dst, func=ACT.Copy, **kw):
                n = TILE0[phase] + i
                act.wait_ge(tile_ready, n + 1)
                src = ps[:, 2 + n % 2, 0:T] if phase == "s5_in" else work(n)
                act.activation(dst, src, func, **kw).then_inc(tile_taken, 1)

            def post_linear_norm(phase, name):
                for i in range(KD + 1):
                    if i < KD:
                        take(phase, i, yT[:, i])
                    if i:
                        act.wait_ge(tile_taken, TILE0[phase] + i)
                        act.activation(sq[:, i - 1], yT[:, i - 1], ACT.Square).then_inc(sq_ready, 1)
                root(name)

            def post_ffn_norm(no, name):
                for i in range(KD):
                    act.wait_ge(acc_ready, no * KD + i // 2 * 2 + 2)
                    act.activation(sq[:, i], acc(i), ACT.Square).then_inc(sq_ready, 1)
                root(name)

            def hgrn_rglru():
                for i in range(4):
                    take("even_in", i, proj[:, i], ACT.Silu)
                for i in range(4, 8):
                    take("even_in", i, proj[:, i], ACT.Sigmoid)
                for i in range(8, 12):
                    take("even_in", i, proj[:, i])
                for i in range(12, 16):
                    take("even_in", i, proj[:, i], ACT.Sigmoid)
                act.wait_ge(hg["forget"], 4)
                act.activation(lf, proj[:, 4:8].rearrange("p a n -> p (a n)"), ACT.Ln
                               ).then_inc(hg["logf"], 1)
                for i in range(16, 20):
                    take("even_in", i, xbp[:, i - 16, 3:3 + T])
                act.wait_ge(hg["bcum"], 4)
                act.activation(eb, bc, ACT.Exp).then_inc(hg["exps"], 1)
                act.activation(en, bc, ACT.Exp, scale=-1.0).then_inc(hg["exps"], 1)
                act.wait_ge(hg["decay"], 1)
                act.activation(ed, ed, ACT.Exp).then_inc(hg["exps"], 1)
                for i in range(20, 24):
                    take("even_in", i, proj[:, i - 4], ACT.Gelu_apprx_tanh)
                for b in range(2):
                    act.wait_ge(hg["scores"], b + 1)
                    act.activation(sc[:, b * 512:(b + 1) * 512], ps[0:CHUNK, b, :], ACT.Copy
                                   ).then_inc(hg["scopied"], 1)
                for j in range(RG_TILES):
                    for k, (dst, bias) in enumerate(((gr_, "rg_ba"), (gi_, "rg_bx"))):
                        act.wait_ge(rg["product"], 2 * j + k + 1)
                        act.activation(dst[:, j], work(2 * j + k), ACT.Sigmoid, bias=v(bias, j)
                                       ).then_inc(rg["gates"], 1)
                act.wait_ge(rg["rate"], 2)
                act.wait_ge(rg["gates"], 2 * RG_TILES)
                for j in range(RG_TILES):
                    act.activation(rm[:, j], gr_[:, j], ACT.Tanh, scale=tiny[:, SP4, j:j + 1]
                                   ).then_inc(rg["decay"], 1)
                for j in range(RG_TILES):
                    act.activation(ra[:, j], gr_[:, j], ACT.Exp, scale=tiny[:, SP8, j:j + 1]
                                   ).then_inc(rg["decay"], 1)
                act.wait_ge(rg["square"], 1)
                act.activation(rm, rm, ACT.Sqrt).then_inc(rg["root"], 1)
                for b in range(2):
                    act.wait_ge(hg["out"], b + 1)
                    act.activation(oo[:, b * 512:(b + 1) * 512], ps[:, 5 + b, :], ACT.Copy
                                   ).then_inc(hg["outtaken"], 1)
                    act.activation(sq[:, 2 * b:2 * b + 2].rearrange("p a n -> p (a n)"),
                                   ps[:, 5 + b, :], ACT.Square).then_inc(hg["outtaken"], 1)
                    act.wait_ge(hg["total"], b + 1)
                    act.activation(rr[:, b * 512:(b + 1) * 512], ps[:, b, :], ACT.Sqrt, bias=EPS,
                                   scale=1.0 / P).then_inc(hg["root"], 1)

            def attention(kind):
                n0 = at0[kind]

                def taken(i):
                    act.wait_ge(at["pturned"], n0 + i + 1)
                    if i >= 2:
                        act.wait_ge(at["out"], n0 + i - 1)
                    n = P * (i % 2 + 1)
                    act.activation(pTs[i % 2][:, 0:n], ps[:, 6 + i % 2, 0:n], ACT.Copy
                                   ).then_inc(at["ptaken"], 1)

                for i in range(2 * HEADS):
                    n = P * (i % 2 + 1)
                    act.wait_ge(at["max"], n0 + i + 1)
                    if i >= 2:
                        act.wait_ge(at["pturned"], n0 + i - 1)
                    act.activation(pbuf[i % 2][:, 0:n], ps[:, 4 + i % 2, 0:n], ACT.Exp,
                                   bias=stat[:, 1, i:i + 1], scale=scale_of[kind],
                                   accum_out=stat[:, 2, i:i + 1]).then_inc(at["exp"], 1)
                    if i >= 1:
                        taken(i - 1)
                taken(2 * HEADS - 1)
                for j in range(KD):
                    act.wait_ge(at["out"], n0 + j // 2 * 8 + 8)
                    act.activation(mixT[:, j], acc(j), ACT.Copy).then_inc(mix_ready, 1)

            def take_values(n0):
                for i in range(4):
                    act.wait_ge(at["vtile"], n0 + i + 1)
                    half, g = divmod(i, 2)
                    act.activation(vtok[:, g, half * 512:half * 512 + 512], ps[:, 2 * g + half, :],
                                   ACT.Copy).then_inc(at["vtaken"], 1)

            def fox():
                act.wait_ge(at["flog"], 1)
                act.activation(fz, acc(2)[0:HEADS], ACT.Identity,
                               bias=vec[0:HEADS, VEC["fox_bias"]:VEC["fox_bias"] + 1]
                               ).then_inc(at["fbias"], 1)
                act.wait_ge(at["fbias"], 1)
                own.mark(act.activation(fa, fz, ACT.Abs))
                own.wait()
                own.mark(act.activation(fa, fa, ACT.Exp, scale=-1.0))
                own.wait()
                act.activation(fa, fa, ACT.Ln, bias=1.0).then_inc(at["logsig"], 1)
                for i in range(16):
                    take("odd_qk", i, proj[:, i], ACT.Copy, scale=HD ** -0.5 if i < KD else 1.0)
                take_values(0)
                attention("fox")

            def feed_forward(phase, conv):
                layer = {"ffn0": 0, "ffn1": 1}.get(phase, 0)

                def hidden(j, f, i):
                    n, p = f + FT0[phase], pair(j, 0)
                    if not conv:
                        act.wait_ge(up_ready, 2 * n + 1)
                        act.activation(gbuf[j % 4], p, ACT.Silu).then_inc(gate_act, 1)
                        return
                    bias = vec[:, bass.ds(VEC["ffn_conv_b"] + layer * 2 * FF_TILES + f, 1)]
                    tap = vec[:, bass.ds(VEC["ffn_conv_w"] + (layer * 3 + 2) * 2 * FF_TILES + f, 1)]
                    bias_v = vec[:, bass.ds(VEC["ffn_conv_b"] + (layer * 2 + 1) * FF_TILES + f, 1)]
                    tap_v = vec[:, bass.ds(
                        VEC["ffn_conv_w"] + ((layer * 3 + 2) * 2 + 1) * FF_TILES + f, 1)]
                    act.wait_ge(up_ready, 2 * n + 1)
                    act.activation(gbuf[j % 4], p, ACT.Identity, bias=bias, scale=tap
                                   ).then_inc(gate_init, 1)
                    act.wait_ge(gate_conv, n + 1)
                    act.activation(gbuf[j % 4], gbuf[j % 4], ACT.Gelu_apprx_tanh
                                   ).then_inc(gate_act, 1)
                    act.wait_ge(up_ready, 2 * n + 2)
                    act.activation(vbuf[j % 4], pair(j, 1), ACT.Identity, bias=bias_v,
                                   scale=tap_v).then_inc(val_init, 1)

                loops = (FFN[phase] - (4 if phase == "ffn2" else 0)) // 4
                with act.Fori(0, loops) as i:
                    for j in range(4):
                        hidden(j, i * 4 + j, i)
                for f in range(loops * 4, FFN[phase]):
                    hidden(f, f, 0)
                    if phase == "ffn2" and f in (FFN[phase] - 6, FFN[phase] - 5):
                        s5_parameters(f - (FFN[phase] - 6))

            def s5_parameters(k):
                if k == 0:
                    act.activation(s5p[:, DT], v("log_dt", 0, 32), ACT.Exp).then_inc(s5["dt"], 1)
                    return
                act.wait_ge(s5["angle"], 1)
                act.activation(s5p[:, MAG], s5p[:, LA], ACT.Exp).then_inc(s5["mag"], 1)
                act.activation(s5p[:, SIN], s5p[:, RED], ACT.Sin).then_inc(s5["trig"], 1)
                own.mark(act.activation(s5p[:, ABS], s5p[:, RED], ACT.Abs))
                own.wait()
                act.activation(s5p[:, COS], s5p[:, ABS], ACT.Sin, scale=-1.0,
                               bias=float(np.pi / 2)).then_inc(s5["trig"], 1)

            def mla():
                pre_norm("m0")
                for i in range(6):
                    take("mla_in", i, mraw[:, i])
                squares("mq", mraw, tile_taken, TILE0["mla_in"])
                squares("mkv", mraw[:, 3:5], tile_taken, TILE0["mla_in"] + 3, at_=3)
                root("mq")
                act.wait_ge(at["reduced"], 1)
                act.activation(sin, red, ACT.Sin).then_inc(at["trig"], 1)
                own.mark(act.activation(mag_, red, ACT.Abs))
                own.wait()
                act.activation(cos, mag_, ACT.Sin, scale=-1.0, bias=float(np.pi / 2)
                               ).then_inc(at["trig"], 1)
                root("mkv")
                for i in range(8):
                    take("mla_uq", i, proj[:, i])
                for i in range(8, 12):
                    take("mla_uq", i, qpe_raw[:, i - 8])
                for i in range(8):
                    take("mla_uk", i, proj[:, 8 + i])
                take_values(4)
                attention("mla")
                for i in range(KD):
                    take("mla_o", i, yT[:, i])

            def s5_mixer():
                pre_norm("m2")
                def steps(q):
                    if q:
                        act.wait_ge(s5["phase"], q)
                    for j in range(4):
                        act.activation(sv[:, j], time_row, ACT.Copy,
                                       scale=s5p[:, PHI, 4 * q + j:4 * q + j + 1]
                                       ).then_inc(s5["steps"], 1)

                def sincos(q):
                    act.wait_ge(s5["phase"], q + 1)
                    act.activation(ss[q % 2], sv, ACT.Sin, scale=TWO_PI_SAFE
                                   ).then_inc(s5["sincos"], 1)
                    own.mark(act.activation(scs[q % 2], sv, ACT.Abs))
                    own.wait()
                    act.activation(scs[q % 2], scs[q % 2], ACT.Sin, scale=-TWO_PI_SAFE,
                                   bias=float(np.pi / 2)).then_inc(s5["sincos"], 1)
                    act.wait_ge(s5["sincos"], 2 * q + 2)
                    if q + 1 < KD:
                        steps(q + 1)

                act.wait_ge(s5["angle"], 2)
                steps(0)
                for b in range(4):
                    act.wait_ge(s5["bturned"], b + 1)
                    act.activation(vtok[:, b // 2, (b % 2) * 512:(b % 2) * 512 + 512],
                                   ps[:, 4 + b, :], ACT.Copy).then_inc(s5["btaken"], 1)
                for q in range(KD):
                    take("s5_in", q, proj[:, q])
                    sincos(q)
                for q in range(KD):
                    act.wait_ge(s5["ysum"], q + 1)
                    act.activation(hT[:, q], sq[:, q], ACT.Gelu_apprx_tanh).then_inc(s5["z"], 1)
                for j in range(KD):
                    take("s5_glu", 2 * j, mixT[:, j])
                    take("s5_glu", 2 * j + 1, sq[:, j], ACT.Sigmoid)

            def experts_gathered():
                def take_input(n):
                    for b in range(2):
                        act.wait_ge(mo["gathered"], n + b + 1)
                        act.activation(xg[:, 4 * b:4 * b + 4], ps[:, 4 + b, 0:4 * CAP].rearrange(
                            "p (a n) -> p a n", a=4), ACT.Copy).then_inc(mo["xready"], 1)

                def expert(e, takes_next):
                    with act.Fori(0, FE_TILES // 4) as i:
                        for j in range(4):
                            n = e * FE_TILES + i * 4 + (FT0["moe"] + j)
                            act.wait_ge(up_ready, 2 * n + 1)
                            act.activation(gbuf[j][:, 0:CAP], pair(j, 0)[:, 0:CAP], ACT.Silu
                                           ).then_inc(gate_act, 1)
                    if takes_next:
                        take_input(2 * e + 2)
                    for b in range(2):
                        if b == 0:
                            act.wait_ge(mo["ye"], e + 1)
                        else:
                            act.wait_ge(moe_free, e * FE_TILES + (HALVES + FE_TILES))
                        act.activation(ye[:, b * 512:(b + 1) * 512], ps[0:CAP, b, :], ACT.Copy
                                       ).then_inc(mo["yetaken"], 1)

                take_input(0)
                with act.Fori(0, EXPERTS - 1) as e:
                    expert(e, True)
                expert(EXPERTS - 1, False)

            def experts():
                act.wait_ge(mo["flag"], 1)
                with act.If(act.value_load(crowded[0:1, 0:1], min_val=0, max_val=1) == 1):
                    for b in range(4):
                        act.wait_ge(rt["spread"], b + 1)
                        act.activation(mixT[:, 2 * b:2 * b + 2].rearrange("p a n -> p (a n)"),
                                       ps[:, b, :], ACT.Copy).then_inc(rt["taken"], 1)
                    feed_forward("moe", False)
                with act.Else():
                    experts_gathered()

            def router():
                pre_norm("m3")
                act.wait_ge(rt["diff"], 2)
                act.activation(tiny[:, GA:GA + 1, 0:2], tiny[:, GA:GA + 1, 0:2], ACT.Exp
                               ).then_inc(rt["exp"], 1)
                for b in range(4):
                    act.wait_ge(mo["hturned"], b + 1)
                    act.activation(vtok[:, b // 2, (b % 2) * 512:(b % 2) * 512 + 512],
                                   ps[:, 4 + b, :], ACT.Copy).then_inc(mo["htaken"], 1)

            act.wait_ge(small_loaded, 16 * 6)
            act.wait_ge(hg["lbdiff"], 3)
            act.activation(tiny[:, LD0:LD0 + 3, 0:4], tiny[:, LD0:LD0 + 3, 0:4], ACT.Exp
                           ).then_inc(hg["lbexp"], 1)
            own.mark(act.activation(tiny[:, SPA, 0:4], v("rg_lambda", 0, 4), ACT.Abs))
            own.wait()
            own.mark(act.activation(tiny[:, SPE, 0:4], tiny[:, SPA, 0:4], ACT.Exp, scale=-1.0))
            own.wait()
            act.activation(tiny[:, SPL, 0:4], tiny[:, SPE, 0:4], ACT.Ln, bias=1.0
                           ).then_inc(rg["softplus"], 1)
            pre_norm("n0")
            hgrn_rglru()
            post_linear_norm("even_out", "n1")
            pre_norm("n2")
            feed_forward("ffn0", True)
            post_ffn_norm(0, "n3")
            pre_norm("n4")
            fox()
            post_linear_norm("odd_out", "n5")
            pre_norm("n6")
            feed_forward("ffn1", True)
            post_ffn_norm(1, "n7")
            mla()
            pre_norm("m1")
            feed_forward("ffn2", False)
            s5_mixer()
            router()
            experts()
            pre_norm("mf")
            for b in range(4):
                act.wait_ge(out_turned, b + 1)
                act.activation(proj[:, 2 * b:2 * b + 2].rearrange("p a n -> p (a n)"), ps[:, b, :],
                               ACT.Copy).then_inc(out_taken, 1)

        @block.tensor
        def _(pe):
            def need(phase, u):
                n = UNIT0[phase] + u
                pe.wait_ge(slot_loaded[n % SLOTS], LOADED[n])
                return slots[n % SLOTS]

            def total(name, at_=0):
                tiles = dict(NORMS)[name]
                if NORM_NO[name]:
                    pe.wait_ge(rms_ready, NORM_NO[name])
                for c in range(tiles):
                    pe.wait_ge(sq_ready, SQ0[name] + max(c, 1) + 1)
                    m = pe.matmul(sum_of(name), ones[:, :], sq[:, at_ + c], start=c == 0,
                                  stop=c == tiles - 1, skip_group_check=True)
                m.then_inc(sum_ready, 1)

            def linear(phase, src, ready, first, some=None, ring=WORK, bank0=4):
                tiles, k = LINEAR[phase]
                per = UNIT_TILES if k == KD else tiles
                for i in some or range(tiles):
                    n = TILE0[phase] + i
                    if i % per == 0 or some:
                        w = need(phase, i // per)
                    if n >= ring:
                        pe.wait_ge(tile_taken, n - ring + 1)
                    for c in range(k):
                        if i == 0:
                            pe.wait_ge(ready, first + c + 1)
                        o = ((i % per) * k + c) * P
                        m = pe.matmul(ps[:, bank0 + n % ring, 0:T], w[:, o:o + P], src[:, c],
                                      start=c == 0, stop=c == k - 1, skip_group_check=True)
                    m.then_inc(tile_ready, 1)
                    if i % per == per - 1 or i == tiles - 1:
                        pe.wait_ge(tile_ready, n + 1)
                        pe.sem_inc(slot_free, 1)

            def feed_forward(phase):
                n_ft = FFN[phase]

                def up(f, i):
                    u, half = f // FT_UNIT, f % FT_UNIT
                    n = UNIT0[phase] + u
                    w = slots[n % SLOTS]
                    if half == 0:
                        pe.wait_ge(slot_loaded[n % SLOTS], LOADED[n] + i * 16)
                    for k in range(2):
                        for c in range(KD):
                            o = ((k * FT_UNIT + half) * KD + c) * P
                            m = pe.matmul(pair(f, k), w[:, o:o + P], hT[:, c], start=c == 0,
                                          stop=c == KD - 1, skip_group_check=True)
                        m.then_inc(up_ready, 1)

                def down(f, i, first=False, last=False):
                    u, half = f // FT_UNIT, f % FT_UNIT
                    w = slots[(UNIT0[phase] + u) % SLOTS]
                    pe.wait_ge(hid_ready, i * 8 + (FT0[phase] + f + 1))
                    for d in range(KD):
                        o = (2 * FT_UNIT * KD + half * KD + d) * P
                        m = pe.matmul(acc(d), w[:, o:o + P], hid[f % 4], start=first and d % 2 == 0,
                                      stop=last, skip_group_check=True)
                        if last:
                            m.then_inc(acc_ready, 1)
                    if half == FT_UNIT - 1 and not last:
                        m.then_inc(slot_free, 1)

                for c in range(KD):
                    pe.wait_ge(h_ready, SQ0[{"ffn0": "n2", "ffn1": "n6", "ffn2": "m1",
                                             "moe": "m3"}[phase]] + c + 1)
                up(0, 0)
                up(1, 0)
                down(0, 0, first=True)
                loops = (n_ft - 2) // 8
                with pe.Fori(0, loops) as i:
                    for j in range(8):
                        up(j + 2, i)
                        down(j + 1, i)
                for f in range(8 * loops + 1, n_ft):
                    if f + 1 < n_ft:
                        up(f + 1, 0)
                    down(f, 0, last=f == n_ft - 1)
                pe.wait_ge(acc_ready, KD * (list(FFN).index(phase) + 1))
                pe.sem_inc(slot_free, 1)

            def hgrn_rglru():
                pe.wait_ge(tile_taken, 12)
                for n in range(16):
                    h, c = divmod(n, 4)
                    m = pe.transpose(ps[0:CHUNK, n // 4, (n % 4) * P:(n % 4 + 1) * P],
                                     proj[:, 8 + h, c * CHUNK:(c + 1) * CHUNK], ident)
                    if n % 4 == 3:
                        m.then_inc(hg["vturned"], 1)
                pe.wait_ge(hg["gated"], 2)
                pe.wait_ge(hg["vtaken"], 4)
                for n in range(16):
                    t = slice(n * CHUNK, (n + 1) * CHUNK)
                    m = pe.matmul(ps[0:CHUNK, n // 8, (n % 8) * CHUNK:(n % 8 + 1) * CHUNK],
                                  kd[:, t], qd[:, t], start=True, stop=True, skip_group_check=True)
                    if n % 8 == 7:
                        m.then_inc(hg["scores"], 1)
                pe.wait_ge(tile_taken, 24)
                for j in range(RG_TILES):
                    pe.wait_ge(rg["conv"], j + 1)
                    for k in range(2):
                        if 2 * j + k >= WORK:
                            pe.wait_ge(rg["gates"], 2 * j + k - WORK + 1)
                        pe.matmul(work(2 * j + k), rgw[:, k, j, :], xc[:, j], start=True, stop=True,
                                  skip_group_check=True).then_inc(rg["product"], 1)
                pe.wait_ge(hg["gated"], 3)
                pe.wait_ge(rg["gates"], 2 * RG_TILES)
                for n in range(16):
                    m = pe.transpose(ps[0:CHUNK, 4 + n // 4, (n % 4) * P:(n % 4 + 1) * P],
                                     ku[:, n * CHUNK:(n + 1) * CHUNK], ident)
                    if n % 4 == 3:
                        m.then_inc(hg["kturned"], 1)
                pe.wait_ge(hg["ktaken"], 4)
                for c in range(3):
                    for h in range(A_HEADS):
                        m = pe.matmul(ps[:, 2 + c, h * P:(h + 1) * P], kt[:, 4 * h + c, :],
                                      vt[:, 4 * h + c, :], start=True, stop=True,
                                      skip_group_check=True)
                    m.then_inc(hg["upd"], 1)
                pe.wait_ge(hg["masked"], 1)
                def head_sums(b):
                    pe.wait_ge(hg["outtaken"], 2 * b + 2)
                    pe.matmul(ps[:, b, :], ones[:, :],
                              sq[:, 2 * b:2 * b + 2].rearrange("p a n -> p (a n)"), start=True,
                              stop=True, skip_group_check=True).then_inc(hg["total"], 1)

                for b in range(2):
                    for c in range(NCHUNK):
                        if c:
                            pe.wait_ge(hg["state"], (1, 5, 9)[c - 1])
                        for h in (2 * b, 2 * b + 1):
                            n = 4 * h + c
                            t = slice(n * CHUNK, (n + 1) * CHUNK)
                            o = ps[:, 5 + b, (h % 2) * T + c * CHUNK:(h % 2) * T + (c + 1) * CHUNK]
                            m = pe.matmul(o, vt[:, n, :], sc[:, t], start=True, stop=c == 0,
                                          skip_group_check=True)
                            if c:
                                k = (c - 1) * 512 + h * P
                                m = pe.matmul(o, st[:, k:k + P], qd[:, t], start=False, stop=True,
                                              skip_group_check=True)
                        if b == 1 and c == 1:
                            head_sums(0)
                    m.then_inc(hg["out"], 1)
                head_sums(1)

            def attention(kind, score):
                n0 = at0[kind]

                def scores(i):
                    if i >= 2:
                        pe.wait_ge(at["exp"], n0 + i - 1)
                    h, qb = divmod(i, 2)
                    score(h, qb, P * (qb + 1), ps[:, 4 + i % 2, :])
                    pe.matmul(ps[:, 4 + i % 2, qb * P:(qb + 1) * P], ident, mask, start=False,
                              stop=True, skip_group_check=True).then_inc(at["scores"], 1)

                def turn(i):
                    pe.wait_ge(at["prob"], n0 + i + 1)
                    if i >= 2:
                        pe.wait_ge(at["ptaken"], n0 + i - 1)
                    for b in range(i % 2 + 1):
                        m = pe.transpose(ps[:, 6 + i % 2, b * P:(b + 1) * P],
                                         pbuf[i % 2][:, b * P:(b + 1) * P], ident)
                    m.then_inc(at["pturned"], 1)

                def output(i):
                    pe.wait_ge(at["ptaken"], n0 + i + 1)
                    h, qb = divmod(i, 2)
                    o = acc(h // 2)[HD * (h % 2):HD * (h % 2) + HD, qb * P:(qb + 1) * P]
                    for b in range(qb + 1):
                        m = pe.matmul(o, vtok[:, b, h * HD:(h + 1) * HD],
                                      pTs[i % 2][:, b * P:(b + 1) * P], start=b == 0, stop=b == qb,
                                      skip_group_check=True)
                    m.then_inc(at["out"], 1)

                pe.wait_ge(at["vtaken"], 4 if kind == "fox" else 8)
                scores(0)
                scores(1)
                for i in range(2 * HEADS):
                    turn(i)
                    if i + 2 < 2 * HEADS:
                        scores(i + 2)
                    output(i)

            def values(phase, src, k, n0):
                units = len(phase_units(phase))
                for half in range(2):
                    if half < units:
                        w = need(phase, half)
                    for g in range(2):
                        for c in range(k):
                            o = c * 512 if units == 2 else c * D + half * 512
                            m = pe.matmul(ps[:, 2 * g + half, :], src[:, c, g * P:(g + 1) * P],
                                          w[:, o:o + 512], start=c == 0, stop=c == k - 1,
                                          skip_group_check=True)
                        m.then_inc(at["vtile"], 1)
                    if units == 2 or half == 1:
                        pe.wait_ge(at["vtile"], n0 + 2 * half + 2)
                        pe.sem_inc(slot_free, 1)

            def fox():
                for c in range(KD):
                    pe.wait_ge(h_ready, SQ0["n4"] + c + 1)
                    m = pe.matmul(acc(2)[0:HEADS], wf[:, c, :], hT[:, c], start=c == 0,
                                  stop=c == KD - 1, skip_group_check=True)
                m.then_inc(at["flog"], 1)
                linear("odd_qk", hT, h_ready, SQ0["n4"])
                pe.wait_ge(at["fbias"], 1)
                values("odd_v", hT, KD, 0)
                pe.wait_ge(tile_taken, TILE0["odd_qk"] + 16)
                pe.wait_ge(at["c"], 2)

                def score(h, qb, n, o):
                    r = HD * (h % 2)
                    pe.matmul(o[:, 0:n], proj[r:r + HD, h // 2, qb * P:(qb + 1) * P],
                              proj[r:r + HD, 8 + h // 2, 0:n], start=True, stop=False,
                              skip_group_check=True)
                    one = cst[0:HEADS, CST["ident"] + h:CST["ident"] + h + 1]
                    pe.matmul(o[:, 0:n], cum[:, qb * P:(qb + 1) * P], one.to_broadcast([HEADS, n]),
                              start=False, stop=False, skip_group_check=True)
                    pe.matmul(o[:, 0:n], one.to_broadcast([HEADS, P]), negc[:, 0:n], start=False,
                              stop=False, skip_group_check=True)

                attention("fox", score)

            def mla():
                total("m0")
                linear("mla_in", hT, h_ready, SQ0["m0"])
                total("mq")
                pe.wait_ge(at["posrow"], 2)
                pe.matmul(acc(2), onesrow, posf, start=True, stop=True, skip_group_check=True
                          ).then_inc(at["poscol"], 1)
                total("mkv", 3)
                linear("mla_uq", mnorm, h_ready, SQ0["mq"])
                linear("mla_uk", mnorm[:, 3:5], h_ready, SQ0["mkv"])
                pe.wait_ge(tile_taken, TILE0["mla_uk"] + 8)
                for i in range(5):
                    if i >= WORK:
                        pe.wait_ge(at["roped"], i - WORK + 1)
                    pe.matmul(work(i), rot, qpe_raw[:, i] if i < 4 else mraw[:, 5], start=True,
                              stop=True, skip_group_check=True).then_inc(at["turned"], 1)
                values("mla_uv", mnorm[:, 3:5], 2, 4)
                pe.wait_ge(at["roped"], 5)

                def score(h, qb, n, o):
                    r = HD * (h % 2)
                    pe.matmul(o[:, 0:n], proj[r:r + HD, h // 2, qb * P:(qb + 1) * P],
                              proj[r:r + HD, 8 + h // 2, 0:n], start=True, stop=False,
                              skip_group_check=True)
                    r = ROPE * (h % 4)
                    pe.matmul(o[:, 0:n], proj[r:r + ROPE, 16 + h // 4, qb * P:(qb + 1) * P],
                              kpe[r:r + ROPE, 0:n], start=False, stop=False, skip_group_check=True)

                attention("mla", score)
                linear("mla_o", mixT, mix_ready, mix0["mla_o"])

            def s5_mixer():
                total("m2")

                def projected(some):
                    linear("s5_in", hT, h_ready, SQ0["m2"], some, 2, 2)

                def inputs(q):
                    pe.wait_ge(tile_taken, TILE0["s5_in"] + q + 1)
                    if q:
                        pe.wait_ge(s5["rotated"], q)
                    for r in range(2):
                        for j in range(4):
                            k = 32 * j
                            m = pe.matmul(ps[:, 4 + j, r * T:(r + 1) * T],
                                          bT[k:k + 32, r, q, :], proj[k:k + 32, q, :], start=True,
                                          stop=True, skip_group_check=True)
                    m.then_inc(s5["bu"], 1)

                def outputs(q):
                    pe.wait_ge(s5["state"], q + 1)
                    if q >= 2:
                        pe.wait_ge(s5["ysum"], q - 1)
                    for j in range(4):
                        k = 32 * j
                        terms = [(r, x[q % 2]) for r, x in ((0, sA), (0, sC), (1, sB), (1, sD))]
                        for i, (r, x) in enumerate(terms):
                            m = pe.matmul(ps[k:k + 32, q % 2, 0:T], cT[:, r, q, k:k + 32],
                                          x[:, j], start=i == 0, stop=i == 3,
                                          skip_group_check=True)
                    m.then_inc(s5["y"], 1)

                pe.wait_ge(s5["bbar"], 2)
                for n in range(16):
                    r, q = divmod(n, 8)
                    m = pe.transpose(ps[:, 4 + n // 4, (n % 4) * P:(n % 4 + 1) * P],
                                     bbar[:, r, 4 * q:4 * q + 4, :].rearrange("p t c -> p (t c)"),
                                     ident)
                    if n % 4 == 3:
                        m.then_inc(s5["bturned"], 1)
                projected((0,))
                pe.wait_ge(s5["btaken"], 4)
                pe.wait_ge(s5_loaded, 32)
                inputs(0)
                for q in range(KD):
                    if q + 1 < KD:
                        projected((q + 1,))
                        inputs(q + 1)
                    outputs(q)
                linear("s5_glu", hT, s5["z"], 0)

            def router():
                total("m3")
                for g in range(2):
                    for c in range(KD):
                        pe.wait_ge(h_ready, SQ0["m3"] + c + 1)
                        m = pe.matmul(ps[:, 2, g * 8:g * 8 + 8], hT[:, c, g * P:(g + 1) * P],
                                      wr[:, c, :], start=c == 0, stop=c == KD - 1,
                                      skip_group_check=True)
                    m.then_inc(rt["logits"], 1)
                for n in range(16):
                    g, c = divmod(n, 8)
                    m = pe.transpose(ps[:, 4 + n // 4, (n % 4) * P:(n % 4 + 1) * P],
                                     hT[:, c, g * P:(g + 1) * P], ident)
                    if n % 4 == 3:
                        m.then_inc(mo["hturned"], 1)
                pe.wait_ge(mo["sel"], 2)
                for g in range(2):
                    o = ps[:, 3, g * 8:g * 8 + 8]
                    pe.matmul(o, before, sel[:, g], start=True, stop=g == 0, skip_group_check=True)
                    if g:
                        pe.matmul(o, ones[:, :], sel[:, 0], start=False, stop=True,
                                  skip_group_check=True)
                for g in range(2):
                    m = pe.matmul(ps[:, 3, 16:24], ones[:, :], sel[:, g], start=g == 0, stop=g == 1,
                                  skip_group_check=True)
                m.then_inc(mo["pos"], 1)

            def half_slot(f, e):
                h = f % HALVES
                pe.wait_ge(moe_loaded[h], e * (16 * FE_TILES // HALVES) + 16 * (f // HALVES + 1))
                return slots[h // 2][:, h % 2 * HALF:(h % 2 + 1) * HALF]

            def experts_dense():
                for e in range(EXPERTS):
                    for g in range(2):
                        m = pe.matmul(acc(e)[:, g * P:(g + 1) * P],
                                      tiny[:, CB0 + g, e:e + 1].to_broadcast([P, P]), ident,
                                      start=True, stop=True, skip_group_check=True)
                    if e % 2:
                        m.then_inc(rt["spread"], 1)
                pe.wait_ge(rt["taken"], 4)
                for b in range(4):
                    pe.matmul(ps[:, b, 0:1], ident, mask[:, 0:1], start=True, stop=False,
                              skip_group_check=True)
                with pe.Fori(0, EXPERTS) as e:
                    def up(f):
                        w = half_slot(f, e)
                        for k in range(2):
                            for c in range(KD):
                                o = (k * KD + c) * P
                                m = pe.matmul(pair(f, k), w[:, o:o + P], hT[:, c], start=c == 0,
                                              stop=c == KD - 1, skip_group_check=True)
                            m.then_inc(up_ready, 1)

                    def down(f):
                        h = f % HALVES
                        pe.wait_ge(hid_ready, e * FE_TILES + (FT0["moe"] + f + 1))
                        for d in range(KD):
                            o = h % 2 * HALF + (2 * KD + d) * P
                            m = pe.matmul(acc(d), slots[h // 2][:, o:o + P], hid[f % 4],
                                          start=False, stop=False, skip_group_check=True)
                        m.then_inc(moe_free, 1)

                    up(0)
                    for f in range(FE_TILES):
                        if f + 1 < FE_TILES:
                            up(f + 1)
                        down(f)
                pe.wait_ge(moe_free, HALVES + EXPERTS * FE_TILES)
                pe.sem_inc(acc_ready, KD)

            def experts_gathered():
                def gather(n, g_no):
                    pe.wait_ge(mo["pick"], g_no)
                    for b in range(2):
                        for k in range(4):
                            c = 4 * b + k
                            for g in range(2):
                                m = pe.matmul(ps[:, 4 + b, k * CAP:(k + 1) * CAP],
                                              vtok[:, g, c * P:(c + 1) * P], pick[:, g],
                                              start=g == 0, stop=g == 1, skip_group_check=True)
                        m.then_inc(mo["gathered"], 1)

                def spread(e, d):
                    if d == 0:
                        pe.wait_ge(mo["yetaken"], 2 * e + 2)
                        pe.wait_ge(mo["place"], e + 1)
                    pe.wait_ge(mo["added"], e * KD + (d + 1))
                    pe.matmul(ps[:, 2 + d % 2, 0:T], ye[:, d * P:(d + 1) * P], place,
                              start=True, stop=True, skip_group_check=True
                              ).then_inc(mo["spread"], 1)

                def expert(e, after_one, gathers):
                    def up(f):
                        w = half_slot(f, e)
                        for k in range(2):
                            for c in range(KD):
                                o = (k * KD + c) * P
                                m = pe.matmul(pair(f, k)[:, 0:CAP], w[:, o:o + P], xg[:, c],
                                              start=c == 0, stop=c == KD - 1, skip_group_check=True)
                            m.then_inc(up_ready, 1)

                    def down(f):
                        h = f % HALVES
                        pe.wait_ge(hid_ready, e * FE_TILES + (FT0["moe"] + f + 1))
                        for b in range(2):
                            o = h % 2 * HALF + 2 * KD * P + b * 512
                            m = pe.matmul(ps[0:CAP, b, :], hid[f % 4][:, 0:CAP],
                                          slots[h // 2][:, o:o + 512], start=f == 0,
                                          stop=f == FE_TILES - 1, skip_group_check=True)
                            if f == FE_TILES - 1 and b == 0:
                                m.then_inc(mo["ye"], 1)
                        m.then_inc(moe_free, 1)

                    pe.wait_ge(mo["xready"], 2 * e + 2)
                    up(0)
                    for f in range(FE_TILES):
                        if f == SPREAD_STEPS:
                            pe.wait_ge(mo["weighted"], 2 * e + 2)
                            pe.wait_ge(mo["added"], e * KD + 2)
                            for g in range(2):
                                m = pe.transpose(ps[0:CAP, 2, g * P:(g + 1) * P], weighted[:, g],
                                                 ident)
                            m.then_inc(mo["pturned"], 1)
                        if f + 1 < FE_TILES:
                            up(f + 1)
                        elif gathers:
                            gather(e + 1, 2 * e + 4)
                        if after_one and f < SPREAD_STEPS:
                            for d in range(f * KD // SPREAD_STEPS, (f + 1) * KD // SPREAD_STEPS):
                                spread(e - 1, d)
                        down(f)

                gather(0, 2)
                expert(0, False, True)
                with pe.Fori(1, EXPERTS - 1) as e:
                    expert(e, True, True)
                expert(EXPERTS - 1, True, False)
                for d in range(KD):
                    spread(EXPERTS - 1, d)

            def experts():
                pe.sem_inc(moe_free, HALVES)
                pe.wait_ge(rt["comb"], 2)
                pe.wait_ge(mo["flag"], 1)
                pe.wait_ge(mo["posm"], 2)
                pe.wait_ge(mo["htaken"], 4)
                with pe.If(pe.value_load(crowded[0:1, 0:1], min_val=0, max_val=1) == 1):
                    experts_dense()
                with pe.Else():
                    experts_gathered()

            pe.sem_inc(slot_free, SLOTS)
            pe.wait_ge(small_loaded, 16 * 6)
            pe.wait_ge(x_loaded, 16)
            pe.wait_ge(cleared, 2)
            xin = proj[:, 0:8].rearrange("p a n -> p (a n)")
            for c in range(KD):
                for g in range(2):
                    m = pe.transpose(acc(c)[:, g * P:(g + 1) * P],
                                     xin[:, g * D + c * P:g * D + (c + 1) * P], ident)
                m.then_inc(x_turned, 1)
            pe.wait_ge(x_ready, KD)
            total("n0")
            linear("even_in", hT, h_ready, SQ0["n0"])
            hgrn_rglru()
            linear("even_out", mixT, mix_ready, mix0["even_out"])
            total("n1")
            total("n2")
            feed_forward("ffn0")
            total("n3")
            total("n4")
            fox()
            linear("odd_out", mixT, mix_ready, mix0["odd_out"])
            total("n5")
            total("n6")
            feed_forward("ffn1")
            total("n7")
            mla()
            total("m1")
            feed_forward("ffn2")
            s5_mixer()
            router()
            experts()
            total("mf")
            pe.wait_ge(h_ready, SQ0["mf"] + KD)
            for b in range(4):
                g = b // 2
                for k in range(4):
                    m = pe.transpose(ps[:, b, k * P:(k + 1) * P],
                                     hT[:, 4 * (b % 2) + k, g * P:(g + 1) * P], ident)
                m.then_inc(out_turned, 1)

        @block.vector
        def _(dve):
            own = Order(dve, dve_own)

            def step(instruction):
                own.mark(instruction)
                own.wait()

            def scale_tile(name, c, src, dst, gain):
                dve.scalar_tensor_tensor(out=dst, in0=src, scalar=gain, in1=rstd[:, :],
                                         op0=ALU.mult, op1=ALU.mult).then_inc(h_ready, 1)

            def reciprocal(name):
                n = NORM_NO[name]
                dve.wait_ge(rms_ready, n + 1)
                dve.reciprocal(rstd[:, :], rms[:, :]).then_inc(rstd_ready, 1)
                dve.wait_ge(rstd_ready, n + 1)

            def pre_norm(name, src, dst, gain, i0):
                reciprocal(name)
                for c in range(dict(NORMS)[name]):
                    scale_tile(name, c, src[:, c], dst[:, c], v(gain, i0 + c))

            def post_norm(name, i0, src=None):
                reciprocal(name)
                for c in range(KD + 1):
                    if c < KD:
                        scale_tile(name, c, yT[:, c] if src is None else src(c), yT[:, c],
                                   v("norm_gains", i0 + c))
                    if c:
                        dve.wait_ge(h_ready, SQ0[name] + c)
                        dve.tensor_tensor(xT[:, c - 1], xT[:, c - 1], yT[:, c - 1], ALU.add
                                          ).then_inc(x_ready, 1)

            def hgrn_rglru():
                t0 = TILE0["even_in"]
                for h in range(A_HEADS):
                    dve.wait_ge(tile_taken, t0 + 4 + h + 1)
                    dve.tensor_scalar(proj[:, 4 + h], proj[:, 4 + h], tiny[:, OML, h:h + 1],
                                      tiny[:, LB, h:h + 1], ALU.mult, ALU.add
                                      ).then_inc(hg["forget"], 1)
                dve.wait_ge(hg["forget"], 4)
                own.mark(dve.tensor_scalar(kh, proj[:, 4:8].rearrange("p a n -> p (a n)"), -1.0, 1.0,
                                           ALU.mult, ALU.add))
                dve.wait_ge(hg["logf"], 1)
                for h in range(A_HEADS):
                    dve.tensor_tensor_scan(bc[:, h * T:(h + 1) * T], chunk_mask,
                                           lf[:, h * T:(h + 1) * T], 0.0, ALU.mult, ALU.add
                                           ).then_inc(hg["bcum"], 1)
                dve.wait_ge(hg["bcum"], 4)
                b3 = bc.rearrange("p (n c) -> p n c", c=CHUNK)
                dve.tensor_tensor(ed.rearrange("p (n c) -> p n c", c=CHUNK),
                                  b3[:, :, CHUNK - 1:CHUNK].to_broadcast([P, 16, CHUNK]), b3,
                                  ALU.subtract).then_inc(hg["decay"], 1)
                dve.wait_ge(hg["exps"], 3)
                dve.tensor_tensor(qd, proj[:, 0:4].rearrange("p a n -> p (a n)"), eb, ALU.mult
                                  ).then_inc(hg["gated"], 1)
                own.wait()
                dve.tensor_tensor(kd, kh, en, ALU.mult).then_inc(hg["gated"], 1)
                dve.tensor_tensor(ku, kh, ed, ALU.mult).then_inc(hg["gated"], 1)
                for j in range(RG_TILES):
                    dve.wait_ge(tile_taken, t0 + 16 + j + 1)
                    step(dve.tensor_scalar(xc[:, j], xbp[:, j, 3:3 + T], v("rg_conv_w", 12 + j),
                                           v("rg_conv_b", j), ALU.mult, ALU.add))
                    for k in (2, 1, 0):
                        m = dve.scalar_tensor_tensor(
                            out=xc[:, j], in0=xbp[:, j, k:k + T], scalar=v("rg_conv_w", 4 * k + j),
                            in1=xc[:, j], op0=ALU.mult, op1=ALU.add)
                        if k:
                            step(m)
                    m.then_inc(rg["conv"], 1)
                for b in range(4):
                    dve.wait_ge(hg["vturned"], b + 1)
                    dve.tensor_copy(vt[:, 4 * b:4 * b + 4, :].rearrange("p a n -> p (a n)"),
                                    ps[0:CHUNK, b, :]).then_inc(hg["vtaken"], 1)
                for b in range(4):
                    dve.wait_ge(hg["kturned"], b + 1)
                    dve.tensor_copy(kt[:, 4 * b:4 * b + 4, :].rearrange("p a n -> p (a n)"),
                                    ps[0:CHUNK, 4 + b, :]).then_inc(hg["ktaken"], 1)
                dve.wait_ge(rg["decay"], 2 * RG_TILES)
                step(dve.scalar_tensor_tensor(out=rm, in0=ra, scalar=1.0, in1=rm, op0=ALU.add,
                                              op1=ALU.mult))
                step(dve.tensor_scalar(ra, rm, -1.0, 1.0, ALU.mult, ALU.add))
                dve.scalar_tensor_tensor(out=rm, in0=ra, scalar=1.0, in1=rm, op0=ALU.add,
                                         op1=ALU.mult).then_inc(rg["square"], 1)
                step(dve.tensor_tensor(xc, xc, gi_, ALU.mult))
                dve.wait_ge(hg["upd"], 1)
                dve.tensor_copy(st[:, 0:512], ps[:, 2, :]).then_inc(hg["state"], 1)
                for c in (1, 2):
                    dve.wait_ge(hg["upd"], c + 1)
                    dve.wait_ge(hg["state"], 4 * c - 3)
                    for h in range(A_HEADS):
                        n, last = c * 512 + h * P, h * T + c * CHUNK + CHUNK - 1
                        dve.scalar_tensor_tensor(
                            out=st[:, n:n + P], in0=st[:, n - 512:n - 512 + P],
                            scalar=eb[:, last:last + 1], in1=ps[:, 2 + c, h * P:(h + 1) * P],
                            op0=ALU.mult, op1=ALU.add).then_inc(hg["state"], 1)
                dve.wait_ge(rg["root"], 1)
                own.mark(dve.memset(ra[:, :, 0:1], 0.0))
                step(dve.tensor_tensor(xc, xc, rm, ALU.mult))
                step(dve.tensor_tensor_scan(gi_.rearrange("p a n -> p (a n)"),
                                            ra.rearrange("p a n -> p (a n)"),
                                            xc.rearrange("p a n -> p (a n)"), 0.0, ALU.mult,
                                            ALU.add))
                own.mark(dve.tensor_tensor(mixT[:, 4:8], gi_, proj[:, 16:20], ALU.mult))
                for h in range(A_HEADS):
                    t = slice(h * T, (h + 1) * T)
                    dve.wait_ge(hg["root"], h // 2 + 1)
                    step(dve.reciprocal(rr[:, t], rr[:, t]))
                    step(dve.scalar_tensor_tensor(out=oo[:, t], in0=oo[:, t], scalar=v("hgrn_norm", h),
                                                  in1=rr[:, t], op0=ALU.mult, op1=ALU.mult))
                    dve.tensor_tensor(mixT[:, h], oo[:, t], proj[:, 12 + h], ALU.mult
                                      ).then_inc(mix_ready, 5 if h == A_HEADS - 1 else 1)

            def attention(kind):
                n0 = at0[kind]

                def maximum(i):
                    dve.wait_ge(at["scores"], n0 + i + 1)
                    step(dve.tensor_reduce(stat[:, 0, i:i + 1], ps[:, 4 + i % 2, 0:P * (i % 2 + 1)],
                                           AX.X, ALU.max))
                    dve.tensor_scalar(stat[:, 1, i:i + 1], stat[:, 0, i:i + 1], -scale_of[kind],
                                      None, ALU.mult).then_inc(at["max"], 1)

                for i in range(2 * HEADS):
                    maximum(i)
                    dve.wait_ge(at["exp"], n0 + i + 1)
                    step(dve.reciprocal(stat[:, 3, i:i + 1], stat[:, 2, i:i + 1]))
                    n = P * (i % 2 + 1)
                    dve.tensor_scalar(pbuf[i % 2][:, 0:n], pbuf[i % 2][:, 0:n], stat[:, 3, i:i + 1],
                                      None, ALU.mult).then_inc(at["prob"], 1)

            def fox():
                dve.wait_ge(at["logsig"], 1)
                step(dve.scalar_tensor_tensor(out=fz, in0=fz, scalar=0.0, in1=fa, op0=ALU.min,
                                              op1=ALU.subtract))
                one = cst[0:HEADS, CST["time"] + T // 2 + 1:CST["time"] + T // 2 + 2]
                dve.tensor_tensor_scan(cum, one.to_broadcast([HEADS, T]), fz, 0.0, ALU.mult, ALU.add
                                       ).then_inc(at["c"], 1)
                dve.wait_ge(at["c"], 1)
                dve.tensor_scalar(negc, cum, -1.0, None, ALU.mult).then_inc(at["c"], 1)
                attention("fox")

            def feed_forward(phase, conv):
                layer = {"ffn0": 0, "ffn1": 1}.get(phase, 0)

                def taps(k, f, half):
                    return vec[:, bass.ds(
                        VEC["ffn_conv_w"] + ((layer * 3 + k) * 2 + half) * FF_TILES + f, 1)]

                def convolve(j, f, half, buf, done, count):
                    p = pair(j, half)
                    dve.scalar_tensor_tensor(out=buf[:, 1:T], in0=p[:, 0:T - 1],
                                             scalar=taps(1, f, half), in1=buf[:, 1:T],
                                             op0=ALU.mult, op1=ALU.add).then_inc(conv_step, 1)
                    dve.wait_ge(conv_step, count)
                    dve.scalar_tensor_tensor(out=buf[:, 2:T], in0=p[:, 0:T - 2],
                                             scalar=taps(0, f, half), in1=buf[:, 2:T],
                                             op0=ALU.mult, op1=ALU.add).then_inc(done, 1)

                def hidden(j, f, cb):
                    n, g, u = f + FT0[phase], gbuf[j % 4], vbuf[j % 4]
                    if conv:
                        dve.wait_ge(gate_init, n + 1)
                        convolve(j, f, 0, g, gate_conv, 3 * n + 1)
                        dve.wait_ge(val_init, n + 1)
                        convolve(j, f, 1, u, conv_step, 3 * n + 2)
                        dve.wait_ge(conv_step, 3 * n + 3)
                    elif cb is not None:
                        dve.wait_ge(up_ready, 2 * n + 2)
                        dve.tensor_tensor(u, pair(j, 1), cb, ALU.mult).then_inc(conv_step, 1)
                        dve.wait_ge(conv_step, n - FT0["moe"] + (3 * FT0["ffn2"] + 1))
                    else:
                        dve.wait_ge(up_ready, 2 * n + 2)
                        u = pair(j, 1)
                    dve.wait_ge(gate_act, n + 1)
                    dve.tensor_tensor(hid[j % 4], g, u, ALU.mult).then_inc(hid_ready, 1)

                if phase == "moe":
                    with dve.Fori(0, EXPERTS) as e:
                        with dve.Fori(0, FE_TILES // 4) as i:
                            for j in range(4):
                                hidden(j, e * FE_TILES + i * 4 + j,
                                       mixT[:, bass.ds(e, 1), :].rearrange("p o n -> p (o n)"))
                    return
                meanwhile = {} if phase != "ffn2" else {
                    FFN[phase] - 5: s5_angle, FFN[phase] - 4: s5_gain,
                    FFN[phase] - 3: lambda: s5_input_matrix(0),
                    FFN[phase] - 2: lambda: s5_input_matrix(1)}
                loops = (FFN[phase] - len(meanwhile)) // 4
                with dve.Fori(0, loops) as i:
                    for j in range(4):
                        hidden(j, i * 4 + j, None)
                for f in range(loops * 4, FFN[phase]):
                    hidden(f, f, None)
                    if f in meanwhile:
                        meanwhile[f]()

            def reduce_angle(dst, src, turns_):
                step(dve.tensor_scalar(turns_, src, INV_TURN, ROUND, ALU.mult, ALU.add))
                step(dve.tensor_scalar(turns_, turns_, -ROUND, None, ALU.add))
                step(dve.scalar_tensor_tensor(out=dst, in0=turns_, scalar=-TURN_A, in1=src,
                                              op0=ALU.mult, op1=ALU.add))
                for c in (TURN_B, TURN_C):
                    step(dve.scalar_tensor_tensor(out=dst, in0=turns_, scalar=-c, in1=dst,
                                                  op0=ALU.mult, op1=ALU.add))
                return dve.tensor_scalar(dst, dst, PI_SAFE, -PI_SAFE, ALU.min, ALU.max)

            lr, li = v("lam_re", 0, 32), v("lam_im", 0, 32)

            def p(n):
                return s5p[:, n]

            def s5_angle():
                dve.wait_ge(s5["dt"], 1)
                step(dve.tensor_tensor(p(LA), lr, p(DT), ALU.mult))
                step(dve.tensor_tensor(p(ANG), li, p(DT), ALU.mult))
                reduce_angle(p(RED), p(ANG), p(TRN)).then_inc(s5["angle"], 1)
                dve.wait_ge(s5["angle"], 1)
                dve.tensor_scalar(p(PHI), p(RED), INV_TURN, None, ALU.mult).then_inc(s5["angle"], 1)

            def s5_gain():
                step(dve.tensor_tensor(p(DEN), lr, lr, ALU.mult))
                step(dve.tensor_tensor(p(S1), li, li, ALU.mult))
                step(dve.tensor_tensor(p(DEN), p(DEN), p(S1), ALU.add))
                step(dve.reciprocal(p(DEN), p(DEN)))
                dve.wait_ge(s5["mag"], 1)
                dve.wait_ge(s5["trig"], 2)
                step(dve.tensor_tensor(p(AR), p(MAG), p(COS), ALU.mult))
                step(dve.tensor_tensor(p(AI), p(MAG), p(SIN), ALU.mult))
                step(dve.tensor_scalar(p(AR), p(AR), -1.0, None, ALU.add))
                step(dve.tensor_tensor(p(GR), p(AR), lr, ALU.mult))
                step(dve.tensor_tensor(p(S1), p(AI), li, ALU.mult))
                step(dve.tensor_tensor(p(GR), p(GR), p(S1), ALU.add))
                step(dve.tensor_tensor(p(GI), p(AI), lr, ALU.mult))
                step(dve.tensor_tensor(p(S1), p(AR), li, ALU.mult))
                step(dve.tensor_tensor(p(GI), p(GI), p(S1), ALU.subtract))
                step(dve.tensor_tensor(p(GR), p(GR), p(DEN), ALU.mult))
                step(dve.tensor_tensor(p(GI), p(GI), p(DEN), ALU.mult))

            def s5_input_matrix(r):
                def spread(n):
                    return s5p[:, n, :, None].to_broadcast([P, S5_TILES, 32])

                def wide(t):
                    return t.rearrange("p a n -> p (a n)").rearrange("p (t c) -> p t c", c=32)

                dve.wait_ge(s5_loaded, 32)
                t1, t2 = wide(sA[0]), wide(sB[0])
                x, y, op = ((bexp[:, 0], bexp[:, 1], ALU.subtract),
                            (bexp[:, 1], bexp[:, 0], ALU.add))[r]
                own.mark(dve.tensor_tensor(t1, x, spread(GR), ALU.mult))
                step(dve.tensor_tensor(t2, y, spread(GI), ALU.mult))
                dve.tensor_tensor(bbar[:, r], t1, t2, op).then_inc(s5["bbar"], 1)
                dve.wait_ge(s5["bbar"], r + 1)

            def mla():
                pre_norm("m0", xT, hT, "mix_norm", 0)
                dve.tensor_copy(posf, pos_i[:, :]).then_inc(at["posrow"], 1)
                dve.memset(onesrow, 1.0).then_inc(at["posrow"], 1)
                pre_norm("mq", mraw, mnorm, "q_norm", 0)
                dve.wait_ge(at["poscol"], 1)
                step(dve.tensor_scalar(ang, acc(2), v("inv_freq", 0), None, ALU.mult))
                reduce_angle(red, ang, turns).then_inc(at["reduced"], 1)
                pre_norm("mkv", mraw[:, 3:5], mnorm[:, 3:5], "kv_norm", 0)
                dve.wait_ge(at["trig"], 2)
                for i in range(5):
                    dve.wait_ge(at["turned"], i + 1)
                    if i:
                        dve.wait_ge(at["roped"], i)
                    own.mark(dve.tensor_tensor(tmp[:, 0], qpe_raw[:, i] if i < 4 else mraw[:, 5], cos,
                                               ALU.mult))
                    step(dve.tensor_tensor(tmp[:, 1], work(i), sin, ALU.mult))
                    dve.tensor_tensor(proj[:, 16 + i] if i < 4 else kpe, tmp[:, 0], tmp[:, 1],
                                      ALU.add).then_inc(at["roped"], 1)
                attention("mla")
                for c in range(KD):
                    dve.wait_ge(tile_taken, TILE0["mla_o"] + c + 1)
                    dve.tensor_tensor(xT[:, c], xT[:, c], yT[:, c], ALU.add).then_inc(x_ready, 1)

            def add_accumulated(no):
                for c in range(KD):
                    dve.wait_ge(acc_ready, no * KD + c // 2 * 2 + 2)
                    dve.tensor_tensor(xT[:, c], xT[:, c], acc(c), ALU.add).then_inc(x_ready, 1)

            def s5_mixer():
                pre_norm("m2", xT, hT, "mix_norm", 8)
                def flat(t):
                    return t.rearrange("p a n -> p (a n)")

                dve.wait_ge(s5["bturned"], 4)
                ur, ui = ps[:, 4:8, 0:T], ps[:, 4:8, T:2 * T]
                for q in range(KD):
                    A, B, C, E, sin_, cos_ = (x[q % 2] for x in (sA, sB, sC, sD, ss, scs))
                    if q >= 2:
                        dve.wait_ge(s5["y"], q - 1)
                    dve.wait_ge(s5["sincos"], 2 * q + 1)
                    dve.wait_ge(s5["bu"], q + 1)
                    dve.tensor_tensor(E, ur, sin_, ALU.mult)
                    own.mark(dve.tensor_tensor(B, ui, sin_, ALU.mult))
                    dve.wait_ge(s5["sincos"], 2 * q + 2)
                    dve.tensor_tensor(C, ui, cos_, ALU.mult).then_inc(s5["turned"], 1)
                    dve.tensor_tensor(A, ur, cos_, ALU.mult).then_inc(s5["rotated"], 1)
                    own.wait()
                    dve.wait_ge(s5["rotated"], q + 1)
                    step(dve.tensor_tensor(flat(A), flat(A), flat(B), ALU.add))
                    for k, (src, dst) in enumerate(((A, B), (C, E))):
                        if k:
                            dve.wait_ge(s5["sums"], q + 1)
                        for j in range(4):
                            own.mark(dve.tensor_tensor_scan(
                                dst[:, j], s5p[:, MAG, 4 * q + j:4 * q + j + 1].to_broadcast([P, T]),
                                src[:, j], 0.0, ALU.mult, ALU.add))
                    if q:
                        skip(q - 1)
                    own.wait()
                    dve.tensor_tensor(flat(A), flat(B), flat(cos_), ALU.mult)
                    own.mark(dve.scalar_tensor_tensor(out=flat(C), in0=flat(E), scalar=-1.0,
                                                      in1=flat(sin_), op0=ALU.mult, op1=ALU.mult))
                    own.wait()
                    dve.scalar_tensor_tensor(out=flat(B), in0=flat(B), scalar=-1.0,
                                             in1=flat(sin_), op0=ALU.mult, op1=ALU.mult)
                    dve.scalar_tensor_tensor(out=flat(E), in0=flat(E), scalar=-1.0,
                                             in1=flat(cos_), op0=ALU.mult, op1=ALU.mult
                                             ).then_inc(s5["state"], 1)
                skip(KD - 1)
                for c in range(KD):
                    dve.wait_ge(tile_taken, TILE0["s5_glu"] + 2 * c + 2)
                    step(dve.tensor_tensor(mixT[:, c], mixT[:, c], sq[:, c], ALU.mult))
                    dve.tensor_tensor(xT[:, c], xT[:, c], mixT[:, c], ALU.add).then_inc(x_ready, 1)

            def skip(q):
                dve.wait_ge(s5["y"], q + 1)
                dve.scalar_tensor_tensor(out=sq[:, q], in0=proj[:, q], scalar=v("s5_d", q),
                                         in1=ps[:, q % 2, 0:T], op0=ALU.mult, op1=ALU.add
                                         ).then_inc(s5["ysum"], 1)

            def router():
                pre_norm("m3", xT, hT, "ffn_norm", 8)
                dve.wait_ge(rt["logits"], 2)
                for g in range(2):
                    step(dve.tensor_copy(tiny[:, LG0 + g, :], ps[:, 2, g * 8:g * 8 + 8]))
                    step(dve.max(tiny[:, MX0 + g, :], tiny[:, LG0 + g, :]))
                    step(dve.max_index(idx[:, g, :], tiny[:, MX0 + g, :], tiny[:, LG0 + g, :]))
                    own.mark(dve.tensor_copy(tiny[:, IX0 + g, :], idx[:, g, :]))
                    dve.tensor_tensor(tiny[:, GA, g:g + 1], tiny[:, MX0 + g, 1:2],
                                      tiny[:, MX0 + g, 0:1], ALU.subtract).then_inc(rt["diff"], 1)
                for g in range(2):
                    own.mark(dve.tensor_scalar(sel[:, g], iota8, tiny[:, IX0 + g, 0:1], None,
                                               ALU.is_equal))
                    step(dve.tensor_scalar(tiny[:, LD0 + g, :], iota8, tiny[:, IX0 + g, 1:2], None,
                                           ALU.is_equal))
                    dve.tensor_tensor(sel[:, g], sel[:, g], tiny[:, LD0 + g, :], ALU.add
                                      ).then_inc(mo["sel"], 1)
                dve.wait_ge(rt["exp"], 1)
                step(dve.tensor_scalar(tiny[:, GB, 0:2], tiny[:, GA, 0:2], 1.0, None, ALU.add))
                step(dve.reciprocal(tiny[:, GB, 0:2], tiny[:, GB, 0:2]))
                step(dve.tensor_tensor(tiny[:, GA, 0:2], tiny[:, GA, 0:2], tiny[:, GB, 0:2],
                                       ALU.mult))
                for g in range(2):
                    own.mark(dve.tensor_scalar(tiny[:, LG0 + g, :], iota8, tiny[:, IX0 + g, 0:1],
                                               tiny[:, GB, g:g + 1], ALU.is_equal, ALU.mult))
                    step(dve.tensor_scalar(tiny[:, MX0 + g, :], iota8, tiny[:, IX0 + g, 1:2],
                                           tiny[:, GA, g:g + 1], ALU.is_equal, ALU.mult))
                    dve.tensor_tensor(tiny[:, CB0 + g, :], tiny[:, LG0 + g, :], tiny[:, MX0 + g, :],
                                      ALU.add).then_inc(rt["comb"], 1)
                dve.wait_ge(mo["sel"], 2)
                dve.wait_ge(mo["pos"], 1)
                step(dve.tensor_reduce(tiny[:, LMAX, 0:1], ps[:, 3, 16:24], AX.X, ALU.max))
                dve.tensor_scalar(crowded[:, :], tiny[:, LMAX, 0:1], float(CAP), None, ALU.is_gt
                                  ).then_inc(mo["flag"], 1)
                for g in range(2):
                    step(dve.scalar_tensor_tensor(out=posm[:, g], in0=ps[:, 3, g * 8:g * 8 + 8],
                                                  scalar=1.0, in1=sel[:, g], op0=ALU.add,
                                                  op1=ALU.mult))
                    dve.tensor_scalar(posm[:, g], posm[:, g], -1.0, None, ALU.add
                                      ).then_inc(mo["posm"], 1)
                dve.wait_ge(mo["posm"], 2)
                dve.wait_ge(rt["comb"], 2)

            def experts_gathered():
                count = cst[:, CST["time"] + T // 2:CST["time"] + T // 2 + CAP]

                def picks(e):
                    for g in range(2):
                        col = posm[:, g, bass.ds(e, 1)]
                        dve.tensor_scalar(pick[:, g], count, col, None, ALU.is_equal
                                          ).then_inc(mo["pick"], 1)

                def hidden(e, i, j):
                    n = e * FE_TILES + i * 4 + (FT0["moe"] + j)
                    dve.wait_ge(up_ready, 2 * n + 2)
                    dve.wait_ge(gate_act, n + 1)
                    dve.tensor_tensor(hid[j][:, 0:CAP], gbuf[j][:, 0:CAP], pair(j, 1)[:, 0:CAP],
                                      ALU.mult).then_inc(hid_ready, 1)

                def add(e, d):
                    dve.wait_ge(mo["spread"], e * KD + (d + 1))
                    dve.tensor_tensor(xT[:, d], xT[:, d], ps[:, 2 + d % 2, 0:T], ALU.add
                                      ).then_inc(mo["added"], 1)

                def expert(e, after_one, picks_next):
                    if picks_next:
                        dve.wait_ge(mo["xready"], 2 * e + 2)
                        picks(e + 1)
                    for g in range(2):
                        dve.tensor_scalar(weighted[:, g], count, posm[:, g, bass.ds(e, 1)],
                                          tiny[:, CB0 + g, bass.ds(e, 1)], ALU.is_equal, ALU.mult
                                          ).then_inc(mo["weighted"], 1)
                    for j in range(4):
                        hidden(e, 0, j)
                        if after_one:
                            for d in range(j * KD // SPREAD_STEPS, (j + 1) * KD // SPREAD_STEPS):
                                add(e - 1, d)
                    dve.wait_ge(mo["pturned"], e + 1)
                    dve.tensor_copy(place, ps[0:CAP, 2, 0:T]).then_inc(mo["place"], 1)
                    with dve.Fori(1, FE_TILES // 4) as i:
                        for j in range(4):
                            hidden(e, i, j)

                picks(0)
                expert(0, False, True)
                with dve.Fori(1, EXPERTS - 1) as e:
                    expert(e, True, True)
                expert(EXPERTS - 1, True, False)
                for d in range(KD):
                    add(EXPERTS - 1, d)
                dve.wait_ge(mo["added"], 2 + EXPERTS * KD)
                dve.sem_inc(x_ready, KD)

            def experts():
                dve.sem_inc(mo["added"], 2)
                with dve.If(dve.value_load(crowded[0:1, 0:1], min_val=0, max_val=1) == 1):
                    dve.wait_ge(rt["taken"], 4)
                    feed_forward("moe", False)
                    add_accumulated(3)
                with dve.Else():
                    experts_gathered()

            dve.wait_ge(small_loaded, 16 * 6)
            own.mark(dve.tensor_tensor(tiny[:, LMAX, 0:4], v("lb_logits", 0, 4), v("lb_logits", 4, 4),
                                       ALU.max))
            own.wait()
            step(dve.tensor_tensor(tiny[:, LMAX, 0:4], tiny[:, LMAX, 0:4], v("lb_logits", 8, 4),
                                   ALU.max))
            for r in range(3):
                dve.tensor_tensor(tiny[:, LD0 + r, 0:4], v("lb_logits", 4 * r, 4),
                                  tiny[:, LMAX, 0:4], ALU.subtract).then_inc(hg["lbdiff"], 1)
            dve.wait_ge(hg["lbexp"], 1)
            step(dve.tensor_tensor(tiny[:, LSUM, 0:4], tiny[:, LD0, 0:4], tiny[:, LD1, 0:4], ALU.add))
            step(dve.tensor_tensor(tiny[:, LSUM, 0:4], tiny[:, LSUM, 0:4], tiny[:, LD2, 0:4],
                                   ALU.add))
            step(dve.reciprocal(tiny[:, LREC, 0:4], tiny[:, LSUM, 0:4]))
            step(dve.tensor_tensor(tiny[:, LB, 0:4], tiny[:, LD0, 0:4], tiny[:, LREC, 0:4], ALU.mult))
            step(dve.tensor_scalar(tiny[:, OML, 0:4], tiny[:, LB, 0:4], -1.0, 1.0, ALU.mult, ALU.add))
            step(dve.tensor_scalar(tiny[:, SPM, 0:4], v("rg_lambda", 0, 4), -1.0, 0.0, ALU.mult,
                                   ALU.max))
            dve.wait_ge(rg["softplus"], 1)
            step(dve.tensor_tensor(tiny[:, SPM, 0:4], tiny[:, SPM, 0:4], tiny[:, SPL, 0:4], ALU.add))
            dve.tensor_scalar(tiny[:, SP4, 0:4], tiny[:, SPM, 0:4], RG_C / 2, None, ALU.mult
                              ).then_inc(rg["rate"], 1)
            dve.tensor_scalar(tiny[:, SP8, 0:4], tiny[:, SPM, 0:4], -RG_C, None, ALU.mult
                              ).then_inc(rg["rate"], 1)
            for c in range(KD):
                dve.wait_ge(x_turned, c // 2 * 2 + 2)
                dve.tensor_copy(xT[:, c], acc(c)).then_inc(x_ready, 1)
            pre_norm("n0", xT, hT, "norm_gains", 0)
            dve.wait_ge(cleared, 2)
            hgrn_rglru()
            post_norm("n1", 8)
            pre_norm("n2", xT, hT, "norm_gains", 16)
            feed_forward("ffn0", True)
            post_norm("n3", 24, acc)
            pre_norm("n4", xT, hT, "norm_gains", 32)
            fox()
            post_norm("n5", 40)
            pre_norm("n6", xT, hT, "norm_gains", 48)
            feed_forward("ffn1", True)
            post_norm("n7", 56, acc)
            mla()
            pre_norm("m1", xT, hT, "ffn_norm", 0)
            feed_forward("ffn2", False)
            add_accumulated(2)
            s5_mixer()
            router()
            dve.wait_ge(mo["flag"], 1)
            experts()
            pre_norm("mf", xT, hT, "final_norm", 0)


def weight_tiles(w):
    k, n = w.shape
    return w.reshape(k // P, P, n // P, P).transpose(1, 2, 0, 3)


def linear_units(w, sizes):
    flat = weight_tiles(w).reshape(P, -1)
    out, at = np.zeros((len(sizes), P, max(sizes)), w.dtype), 0
    for i, n in enumerate(sizes):
        out[i, :, :n] = flat[:, at:at + n]
        at += n
    return out


def ffn_units(gate, up, down):
    n = gate.shape[1] // (FT_UNIT * P)
    out = np.empty((n, P, 3, FT_UNIT * KD * P), gate.dtype)
    for k, w in enumerate((gate, up)):
        out[:, :, k] = w.reshape(KD, P, n, FT_UNIT, P).transpose(2, 1, 3, 0, 4).reshape(n, P, -1)
    out[:, :, 2] = down.reshape(n, FT_UNIT, P, D).transpose(0, 2, 1, 3).reshape(n, P, -1)
    return out.reshape(n, P, SLOT)


def columns(x):
    return x.reshape(-1, P).T


def layouts(i):
    f = {}
    f["x"] = i["x"].reshape(2, P, D)
    f["w_even_in"] = linear_units(i["even_w_in"][0], phase_units("even_in"))
    f["w_even_out"] = linear_units(i["even_w_out"][0], phase_units("even_out"))
    odd = i["odd_w_in"][0]
    f["w_odd_qk"] = linear_units(odd[:, :2 * D], phase_units("odd_qk"))
    f["w_odd_v"] = odd[:, 2 * D:3 * D].reshape(KD, P, 2, 512).transpose(2, 1, 0, 3).reshape(2, P, -1)
    f["wf"] = odd[:, 3 * D:].reshape(KD, P, HEADS).transpose(1, 0, 2)
    f["w_odd_out"] = linear_units(i["odd_w_out"][0], phase_units("odd_out"))
    for l in range(2):
        up = i["ffn_w_up"][l]
        f[f"w_ffn{l}"] = ffn_units(up[:, :FF], up[:, FF:], i["ffn_w_down"][l])
    f["w_ffn2"] = ffn_units(i["ffn_w_gate_2"][0], i["ffn_w_up_2"][0], i["ffn_w_down_2"][0])
    w = i["mla_w_in_2"][0]
    n = Q_LORA + KV_LORA
    f["w_mla_in"] = linear_units(np.concatenate([w[:, :n]] + [w[:, n:]] * 4, 1),
                                 phase_units("mla_in"))
    w = i["mla_w_uq_2"][0].reshape(Q_LORA, HEADS, HD + ROPE)
    f["w_mla_uq"] = linear_units(np.concatenate(
        [w[:, :, :HD].reshape(Q_LORA, -1), w[:, :, HD:].reshape(Q_LORA, -1)], 1),
        phase_units("mla_uq"))
    w = i["mla_w_ukv_2"][0].reshape(KV_LORA, HEADS, 2 * HD)
    f["w_mla_uk"] = linear_units(w[:, :, :HD].reshape(KV_LORA, D), phase_units("mla_uk"))
    f["w_mla_uv"] = w[:, :, HD:].reshape(2, P, D).transpose(1, 0, 2).reshape(1, P, -1)
    f["w_mla_o"] = linear_units(i["mla_w_o_2"][0], phase_units("mla_o"))
    f["w_s5_in"] = linear_units(i["s5_w_in_2"][0], phase_units("s5_in"))
    w = i["s5_w_glu_2"][0].reshape(D, 2, KD, P).transpose(0, 2, 1, 3).reshape(D, 2 * D)
    f["w_s5_glu"] = linear_units(w, phase_units("s5_glu"))
    w = np.empty((EXPERTS, FE_TILES, P, 3, KD, P), np.float32)
    for k, name in enumerate(("moe_w_gate_2", "moe_w_up_2")):
        w[:, :, :, k] = i[name][0].reshape(EXPERTS, KD, P, FE_TILES, P).transpose(0, 3, 2, 1, 4)
    w[:, :, :, 2] = i["moe_w_down_2"][0].reshape(EXPERTS, FE_TILES, P, KD, P)
    f["w_moe"] = w.reshape(EXPERTS * FE_TILES, P, HALF)
    f["wr"] = i["moe_w_router_2"][0].reshape(KD, P, EXPERTS).transpose(1, 0, 2)
    blocks = np.zeros((2, RG_TILES, 2, 64, 2, 64), np.float32)
    for k, name in enumerate(("rg_wa", "rg_wx")):
        for h in range(2):
            blocks[k, :, h, :, h, :] = i[name][0].reshape(RG_TILES, 2, 64, 64)[:, h]
    f["rgw"] = blocks.reshape(2, RG_TILES, P, P).transpose(2, 0, 1, 3)
    f["positions"] = i["positions_2"].reshape(1, T)
    b = np.zeros((2, 2, 64, S5_TILES, 2, 16), np.float32)
    c = np.zeros((2, 2, 64, KD, 4, 2, 16), np.float32)
    for r, (nb, ncc) in enumerate((("s5_b_re_2", "s5_c_re_2"), ("s5_b_im_2", "s5_c_im_2"))):
        for h in range(2):
            b[r, h, :, :, h, :] = i[nb][0].reshape(S5_TILES, 2, 64, 16)[:, h].transpose(1, 0, 2)
            c[r, h, :, :, :, h, :] = i[ncc][0].reshape(KD, 4, 2, 16, 64)[:, :, h].transpose(3, 0, 1, 2)
    f["s5_b"] = b.reshape(2, P, S5_TILES, 32).transpose(1, 0, 2, 3)
    f["s5_cT"] = c.reshape(2, P, KD, P).transpose(1, 0, 2, 3)
    v = np.zeros((P, N_VEC), np.float32)
    for name, x in (("norm_gains", i["norm_gains"]), ("lb_logits", i["hgrn_lb_logits"]),
                    ("hgrn_norm", i["hgrn_norm"]), ("rg_conv_w", i["rg_conv_w"]),
                    ("rg_conv_b", i["rg_conv_b"]), ("rg_ba", i["rg_ba"]), ("rg_bx", i["rg_bx"]),
                    ("rg_lambda", i["rg_lambda"]), ("ffn_conv_w", i["ffn_conv_w"]),
                    ("ffn_conv_b", i["ffn_conv_b"]), ("mix_norm", i["mix_norm_2"]),
                    ("ffn_norm", i["ffn_norm_2"]), ("final_norm", i["final_norm_2"]),
                    ("q_norm", i["mla_q_norm_2"]), ("kv_norm", i["mla_kv_norm_2"]),
                    ("s5_d", i["s5_d_2"]), ("lam_re", i["s5_lambda_re_2"]),
                    ("lam_im", i["s5_lambda_im_2"]),
                    ("log_dt", np.repeat(i["s5_log_dt_2"].reshape(-1), 64))):
        x = columns(x)
        v[:, VEC[name]:VEC[name] + x.shape[1]] = x
    freq = (10000.0 ** (-np.arange(0, ROPE, 2, dtype=np.float32) / ROPE)).astype(np.float32)
    v[:, VEC["inv_freq"]] = np.tile(freq, P // 16)
    v[:HEADS, VEC["fox_bias"]] = i["fox_f_bias"].reshape(-1)
    f["vec"] = v
    k = np.zeros((P, N_CST), np.float32)
    row = np.arange(P)
    k[:, CST["ident"]:][:, :P] = np.eye(P)
    k[:, CST["mask"]:][:, :P] = np.where(row[None, :] > row[:, None], NEG, 0.0)
    m = row % ROPE < ROPE // 2
    k[(row + 16)[m], CST["rot"] + row[m]] = -1.0
    k[(row - 16)[~m], CST["rot"] + row[~m]] = 1.0
    k[:, CST["chunk"]:][:, :T] = np.arange(T) % CHUNK != 0
    k[:, CST["time"]:][:, :T] = np.arange(T) - T // 2
    k[:, CST["before"]:][:, :P] = row[:, None] < row[None, :]
    k[:, CST["iota8"]:][:, :8] = np.arange(8)
    f["cst"] = k
    return {n: np.ascontiguousarray(x) for n, x in f.items()}


def kernel(**inputs):
    import concourse.bacc as _bacc
    from concourse import mybir as _mybir
    from concourse.bass_utils import run_bass_kernel_spmd as _run

    nc = _bacc.Bacc("TRN2", target_bir_lowering=False, num_devices=1,
                    dynamic_dma_scratch_size=1024)
    arrays = layouts({n: np.asarray(x) for n, x in inputs.items()})
    tensors = {n: nc.dram_tensor("in_" + n, x.shape, _mybir.dt.from_np(x.dtype),
                                 kind="ExternalInput").ap() for n, x in arrays.items()}
    tensors["out"] = nc.dram_tensor("out", (2, P, D), F32, kind="ExternalOutput").ap()
    build_program(nc, tensors)
    r = _run(nc, [{"in_" + n: x for n, x in arrays.items()}], core_ids=[0])
    return r.results[0]["out"].reshape(1, T, D)
```
